# Optimizing a Trainium2 kernel written in Bass

```python
import jax, jax.numpy as jnp
from jax import lax
import numpy as np
import math

D_MODEL = 1024
BATCH = 1
SEQ = 1024
DEPTH = 1

RET_HEADS = 4
RET_HEAD_DIM = 128
RET_WIDTH = RET_HEADS * RET_HEAD_DIM
RET_CHUNK = 128
ROPE_BASE = 10000.0
SGU_GROUPS = 4
SGU_GROUP_DIM = 128
SGU_WIDTH = SGU_GROUPS * SGU_GROUP_DIM
SGU_CHUNK = 128
MIX_WIDTH = RET_WIDTH + SGU_WIDTH
PROJ_WIDTH = 4 * RET_WIDTH + 2 * SGU_WIDTH
D_FF = 2816
CONV_WIDTH = 3
EPS = 1e-6


def rmsnorm(x, g):
    xf = x.astype(jnp.float32)
    y = xf * lax.rsqrt(jnp.mean(xf * xf, axis=-1, keepdims=True) + EPS)
    return (y * g.astype(jnp.float32)).astype(x.dtype)

def layernorm(x, g, b):
    xf = x.astype(jnp.float32)
    mu = jnp.mean(xf, axis=-1, keepdims=True)
    xc = xf - mu
    y = xc * lax.rsqrt(jnp.mean(xc * xc, axis=-1, keepdims=True) + EPS)
    return (y * g.astype(jnp.float32) + b.astype(jnp.float32)).astype(x.dtype)

def rotary(x, cos, sin):
    half = x.shape[-1] // 2
    x1, x2 = x[..., :half], x[..., half:]
    c = cos[None, :, None, :]
    s = sin[None, :, None, :]
    return jnp.concatenate([x1 * c - x2 * s, x2 * c + x1 * s], axis=-1)

def retention_chunkwise(q, k, v):
    B, S, H, D = q.shape
    C = RET_CHUNK
    N = S // C
    dt = q.dtype
    log_gamma = jnp.log(1.0 - jnp.power(2.0, -5.0 - jnp.arange(H, dtype=jnp.float32)))
    pos = jnp.arange(C, dtype=jnp.float32)
    diff = pos[:, None] - pos[None, :]
    decay_mask = jnp.where(diff >= 0.0,
                           jnp.exp(log_gamma[:, None, None] * jnp.maximum(diff, 0.0)[None]),
                           0.0).astype(dt)
    k_decay = jnp.exp(log_gamma[:, None] * (C - 1.0 - pos)[None]).astype(dt)
    q_decay = jnp.exp(log_gamma[:, None] * (pos + 1.0)[None]).astype(dt)
    chunk_decay = jnp.exp(log_gamma * C).astype(dt)

    def to_chunks(t):
        return t.reshape(B, N, C, H, D).transpose(0, 3, 1, 2, 4)

    qc, kc, vc = to_chunks(q), to_chunks(k), to_chunks(v)
    scores = jnp.einsum('bhnqd,bhnkd->bhnqk', qc, kc) * decay_mask[None, :, None]
    intra = jnp.einsum('bhnqk,bhnkd->bhnqd', scores, vc)
    kv = jnp.einsum('bhnkd,bhnke->bhnde', kc * k_decay[None, :, None, :, None], vc)

    def step(state, kv_n):
        return state * chunk_decay[None, :, None, None] + kv_n, state

    init = jnp.zeros((B, H, D, D), dtype=kv.dtype)
    _, s_prev = lax.scan(step, init, jnp.moveaxis(kv, 2, 0))
    s_prev = jnp.moveaxis(s_prev, 0, 2)
    cross = jnp.einsum('bhnqd,bhnde->bhnqe', qc * q_decay[None, :, None, :, None], s_prev)
    out = intra + cross
    return out.transpose(0, 2, 3, 1, 4).reshape(B, S, H, D)

def spatial_gating_chunked(u, v, ln_g, ln_b, w_s, b_s):
    B, S, _ = u.shape
    C = SGU_CHUNK
    N = S // C
    G, dg = SGU_GROUPS, SGU_GROUP_DIM
    vn = layernorm(v.reshape(B, N, C, G, dg), ln_g, ln_b)
    causal = jnp.tril(jnp.ones((C, C), dtype=w_s.dtype))
    w = w_s * causal[None]
    mixed = jnp.einsum('gts,bnsgd->bntgd', w, vn) + b_s.T[None, None, :, :, None]
    return u * mixed.reshape(B, S, G * dg)

def causal_depthwise_conv(h, w, b):
    S = h.shape[1]
    hp = jnp.pad(h, ((0, 0), (CONV_WIDTH - 1, 0), (0, 0)))
    y = hp[:, 0:S] * w[0]
    for j in range(1, CONV_WIDTH):
        y = y + hp[:, j:j + S] * w[j]
    return y + b

def first_inputs(seed: int = 0) -> dict:
    key = jax.random.key(seed)
    ks = jax.random.split(key, 16)
    f32 = jnp.float32
    nrm = lambda k, shape, scale: jax.random.normal(k, shape, f32) * scale
    return {
        "x": nrm(ks[0], (BATCH, SEQ, D_MODEL), 1.0),
        "mix_norm_g": 1.0 + nrm(ks[1], (DEPTH, D_MODEL), 0.01),
        "w_in": nrm(ks[2], (DEPTH, D_MODEL, PROJ_WIDTH), D_MODEL ** -0.5),
        "ret_norm_g": 1.0 + nrm(ks[3], (DEPTH, RET_WIDTH), 0.01),
        "sgu_ln_g": 1.0 + nrm(ks[4], (DEPTH, SGU_GROUPS, SGU_GROUP_DIM), 0.01),
        "sgu_ln_b": nrm(ks[5], (DEPTH, SGU_GROUPS, SGU_GROUP_DIM), 0.01),
        "sgu_w_s": nrm(ks[6], (DEPTH, SGU_GROUPS, SGU_CHUNK, SGU_CHUNK), SGU_CHUNK ** -0.5),
        "sgu_b_s": 1.0 + nrm(ks[7], (DEPTH, SGU_GROUPS, SGU_CHUNK), 0.01),
        "w_out": nrm(ks[8], (DEPTH, MIX_WIDTH, D_MODEL), MIX_WIDTH ** -0.5),
        "ffn_norm_g": 1.0 + nrm(ks[9], (DEPTH, D_MODEL), 0.01),
        "w_up": nrm(ks[10], (DEPTH, D_MODEL, 2 * D_FF), D_MODEL ** -0.5),
        "conv_w": nrm(ks[11], (DEPTH, CONV_WIDTH, 2 * D_FF), CONV_WIDTH ** -0.5),
        "conv_b": nrm(ks[12], (DEPTH, 2 * D_FF), 0.01),
        "w_down": nrm(ks[13], (DEPTH, D_FF, D_MODEL), D_FF ** -0.5),
        "final_norm_g": 1.0 + nrm(ks[14], (D_MODEL,), 0.01),
    }

def first_block(x, mix_norm_g, w_in, ret_norm_g, sgu_ln_g, sgu_ln_b, sgu_w_s, sgu_b_s,
              w_out, ffn_norm_g, w_up, conv_w, conv_b, w_down, final_norm_g):
    B, S, _ = x.shape
    half = RET_HEAD_DIM // 2
    inv_freq = jnp.power(ROPE_BASE, -jnp.arange(half, dtype=jnp.float32) / half)
    ang = jnp.arange(S, dtype=jnp.float32)[:, None] * inv_freq[None, :]
    cos, sin = jnp.cos(ang).astype(x.dtype), jnp.sin(ang).astype(x.dtype)
    splits = [RET_WIDTH, 2 * RET_WIDTH, 3 * RET_WIDTH, 4 * RET_WIDTH, 4 * RET_WIDTH + SGU_WIDTH]

    for l in range(DEPTH):
        h = rmsnorm(x, mix_norm_g[l])
        proj = h @ w_in[l]
        q, k, v, g, u, sv = jnp.split(proj, splits, axis=-1)
        q = rotary(q.reshape(B, S, RET_HEADS, RET_HEAD_DIM), cos, sin)
        k = rotary(k.reshape(B, S, RET_HEADS, RET_HEAD_DIM), cos, sin) * (RET_HEAD_DIM ** -0.5)
        v = v.reshape(B, S, RET_HEADS, RET_HEAD_DIM)
        ret = retention_chunkwise(q, k, v)
        ret = rmsnorm(ret, ret_norm_g[l].reshape(RET_HEADS, RET_HEAD_DIM)).reshape(B, S, RET_WIDTH)
        ret = jax.nn.silu(g) * ret
        sgu = spatial_gating_chunked(jax.nn.gelu(u, approximate=False),
                                     jax.nn.gelu(sv, approximate=False),
                                     sgu_ln_g[l], sgu_ln_b[l], sgu_w_s[l], sgu_b_s[l])
        mixed = jnp.concatenate([ret, sgu], axis=-1) @ w_out[l]
        x = x + mixed
        h = rmsnorm(x, ffn_norm_g[l])
        up = causal_depthwise_conv(h @ w_up[l], conv_w[l], conv_b[l])
        a, bgate = jnp.split(up, [D_FF], axis=-1)
        x = x + (jax.nn.silu(a) * bgate) @ w_down[l]

    return rmsnorm(x, final_norm_g)


_first_inputs = first_inputs


def first_inputs(seed=0):
    import zlib

    import numpy as np

    out = dict(_first_inputs(seed))
    spreads = {}
    factors = {'mix_norm_g': 5.241,
     'ret_norm_g': 8.0,
     'sgu_ln_g': 8.0,
     'sgu_ln_b': 8.0,
     'sgu_b_s': 8.0,
     'ffn_norm_g': 8.0,
     'conv_b': 8.0,
     'final_norm_g': 5.738}
    for name, (base, spread) in spreads.items():
        noise = np.random.default_rng([zlib.crc32(name.encode()), seed]).standard_normal(out[name].shape)
        drawn = base * np.exp(spread * noise) if base else spread * noise
        out[name] = __import__('jax').numpy.asarray(drawn.astype(out[name].dtype))
    for name, factor in factors.items():
        out[name] = (out[name] * factor).astype(out[name].dtype)
    return out


_narrow_inputs = first_inputs


def first_inputs(seed=0):

    out = dict(_narrow_inputs(seed))
    wider = {'ret_norm_g': 8.2,
     'sgu_ln_g': 11.4,
     'sgu_ln_b': 10.43,
     'sgu_b_s': 8.06,
     'ffn_norm_g': 5.55,
     'conv_b': 5.52,
     'final_norm_g': 6.42}
    for name, times in wider.items():
        mean = out[name].mean()
        out[name] = (mean + times * (out[name] - mean)).astype(out[name].dtype)
    return out


D_MIX = D_MODEL
CONV_CH = D_MIX // 2
CONV_GROUPS = 8
N_HEADS = 8
HEAD_DIM = 64
ATT_CH = N_HEADS * HEAD_DIM
CONV_WIDTH_2 = 31
GRID_W = 64
MAX_KH = 8
KW = 16
PROJ_OUT = 3 * CONV_CH + 4 * ATT_CH


def rms_norm(x, g):
    x32 = x.astype(jnp.float32)
    y = x32 * lax.rsqrt(jnp.mean(x32 * x32, axis=-1, keepdims=True) + EPS)
    return (y * g.astype(jnp.float32)).astype(x.dtype)

def layer_norm(x, g, b):
    x32 = x.astype(jnp.float32)
    mu = jnp.mean(x32, axis=-1, keepdims=True)
    var = jnp.mean(jnp.square(x32 - mu), axis=-1, keepdims=True)
    y = (x32 - mu) * lax.rsqrt(var + EPS)
    return (y * g.astype(jnp.float32) + b.astype(jnp.float32)).astype(x.dtype)

def grouped_rms_norm(y, g, n_groups):
    B, T, C = y.shape
    y32 = y.astype(jnp.float32).reshape(B, T, n_groups, C // n_groups)
    y32 = y32 * lax.rsqrt(jnp.mean(y32 * y32, axis=-1, keepdims=True) + EPS)
    return (y32.reshape(B, T, C) * g.astype(jnp.float32)).astype(y.dtype)

def conformer_conv(glu_a, glu_b, dw_w, dw_b, cln_g, cln_b, pw_w, pw_b):
    u = glu_a * jax.nn.sigmoid(glu_b)
    pad = CONV_WIDTH_2 // 2
    u = lax.conv_general_dilated(
        u, dw_w[:, None, :].astype(u.dtype), window_strides=(1,),
        padding=[(pad, pad)], dimension_numbers=("NWC", "WIO", "NWC"),
        feature_group_count=u.shape[-1]) + dw_b
    u = layer_norm(u, cln_g, cln_b)
    u = jax.nn.silu(u)
    return u @ pw_w + pw_b

def neighbourhood_attention(q, k, v, rpb):
    B, T, _ = q.shape
    rows = T // GRID_W
    kh = min(MAX_KH, rows)

    def to_grid(t):
        return t.reshape(B, rows, GRID_W, N_HEADS, HEAD_DIM).transpose(0, 3, 1, 2, 4)

    qg, kg, vg = to_grid(q), to_grid(k), to_grid(v)
    scale = HEAD_DIM ** -0.5

    row_ids = jnp.arange(rows)
    row_start = jnp.clip(row_ids - kh // 2, 0, rows - kh)
    col_ids = jnp.arange(GRID_W)
    col_start = jnp.clip(col_ids - KW // 2, 0, GRID_W - KW)
    col_idx = col_start[:, None] + jnp.arange(KW)[None, :]
    col_rel = col_idx - col_ids[:, None] + (KW - 1)

    def one_row(args):
        r, rs = args
        q_row = lax.dynamic_index_in_dim(qg, r, axis=2, keepdims=False)
        k_rows = lax.dynamic_slice_in_dim(kg, rs, kh, axis=2)
        v_rows = lax.dynamic_slice_in_dim(vg, rs, kh, axis=2)
        k_win = k_rows[:, :, :, col_idx, :]
        v_win = v_rows[:, :, :, col_idx, :]
        s = jnp.einsum("bhwd,bhiwjd->bhwij", q_row, k_win).astype(jnp.float32) * scale
        row_rel = rs + jnp.arange(kh) - r + (MAX_KH - 1)
        bias = rpb[:, row_rel[:, None, None], col_rel[None, :, :]]
        s = s + bias.transpose(0, 2, 1, 3).astype(jnp.float32)[None]
        p = jax.nn.softmax(s.reshape(B, N_HEADS, GRID_W, kh * KW), axis=-1)
        p = p.reshape(B, N_HEADS, GRID_W, kh, KW).astype(v.dtype)
        return jnp.einsum("bhwij,bhiwjd->bhwd", p, v_win)

    out = lax.map(one_row, (row_ids, row_start))
    return out.transpose(1, 0, 3, 2, 4).reshape(B, T, ATT_CH)

def second_inputs(seed: int = 0) -> dict:
    key = jax.random.key(seed)
    ks = jax.random.split(key, 16)
    f32 = jnp.float32
    nrm = lambda k, s: jax.random.normal(k, s, f32)
    return {
        "x": nrm(ks[0], (BATCH, SEQ, D_MODEL)),
        "ln_g": 1.0 + 0.01 * nrm(ks[1], (DEPTH, D_MODEL)),
        "w_in": nrm(ks[2], (DEPTH, D_MODEL, PROJ_OUT)) * D_MODEL ** -0.5,
        "b_in": 0.01 * nrm(ks[3], (DEPTH, PROJ_OUT)),
        "dw_w": nrm(ks[4], (DEPTH, CONV_WIDTH_2, CONV_CH)) * CONV_WIDTH_2 ** -0.5,
        "dw_b": 0.01 * nrm(ks[5], (DEPTH, CONV_CH)),
        "cln_g": 1.0 + 0.01 * nrm(ks[6], (DEPTH, CONV_CH)),
        "cln_b": 0.01 * nrm(ks[7], (DEPTH, CONV_CH)),
        "pw_w": nrm(ks[8], (DEPTH, CONV_CH, CONV_CH)) * CONV_CH ** -0.5,
        "pw_b": 0.01 * nrm(ks[9], (DEPTH, CONV_CH)),
        "rpb": 0.02 * nrm(ks[10], (DEPTH, N_HEADS, 2 * MAX_KH - 1, 2 * KW - 1)),
        "gn_conv_g": 1.0 + 0.01 * nrm(ks[11], (DEPTH, CONV_CH)),
        "gn_att_g": 1.0 + 0.01 * nrm(ks[12], (DEPTH, ATT_CH)),
        "w_out": nrm(ks[13], (DEPTH, D_MIX, D_MODEL)) * D_MIX ** -0.5,
        "final_g": 1.0 + 0.01 * nrm(ks[14], (D_MODEL,)),
    }

def second_block(x, ln_g, w_in, b_in, dw_w, dw_b, cln_g, cln_b, pw_w, pw_b, rpb,
              gn_conv_g, gn_att_g, w_out, final_g):
    h = x
    cuts = [CONV_CH, 2 * CONV_CH, 3 * CONV_CH, 3 * CONV_CH + ATT_CH,
            3 * CONV_CH + 2 * ATT_CH, 3 * CONV_CH + 3 * ATT_CH]
    for l in range(DEPTH):
        hn = rms_norm(h, ln_g[l])
        proj = hn @ w_in[l] + b_in[l]
        glu_a, glu_b, z_conv, q, k, v, z_att = jnp.split(proj, cuts, axis=-1)
        y_conv = conformer_conv(glu_a, glu_b, dw_w[l], dw_b[l], cln_g[l], cln_b[l],
                                pw_w[l], pw_b[l])
        y_att = neighbourhood_attention(q, k, v, rpb[l])
        y_conv = grouped_rms_norm(y_conv, gn_conv_g[l], CONV_GROUPS) * jax.nn.silu(z_conv)
        y_att = grouped_rms_norm(y_att, gn_att_g[l], N_HEADS) * jax.nn.silu(z_att)
        y = jnp.concatenate([y_conv, y_att], axis=-1)
        h = h + y @ w_out[l]
    return rms_norm(h, final_g)


_first_inputs_2 = second_inputs


def second_inputs(seed=0):
    import zlib

    import numpy as np

    out = dict(_first_inputs_2(seed))
    spreads = {}
    factors = {'ln_g': 5.827,
     'dw_b': 29.293,
     'cln_g': 62.635,
     'cln_b': 64.0,
     'pw_b': 45.797,
     'rpb': 8.0,
     'gn_conv_g': 62.548,
     'gn_att_g': 64.0,
     'final_g': 33.043,
     'b_in': 6.355}
    for name, (base, spread) in spreads.items():
        noise = np.random.default_rng([zlib.crc32(name.encode()), seed]).standard_normal(out[name].shape)
        drawn = base * np.exp(spread * noise) if base else spread * noise
        out[name] = __import__('jax').numpy.asarray(drawn.astype(out[name].dtype))
    for name, factor in factors.items():
        out[name] = (out[name] * factor).astype(out[name].dtype)
    return out


_narrow_inputs_2 = second_inputs


def second_inputs(seed=0):

    out = dict(_narrow_inputs_2(seed))
    wider = {'cln_g': 8.97,
     'cln_b': 9.09,
     'pw_b': 8.93,
     'gn_conv_g': 8.89,
     'gn_att_g': 9.11,
     'final_g': 6.47}
    for name, times in wider.items():
        mean = out[name].mean()
        out[name] = (mean + times * (out[name] - mean)).astype(out[name].dtype)
    return out


SB_HEADS = D_MODEL // (2 * HEAD_DIM)
SWA_HEADS = D_MODEL // (2 * HEAD_DIM)
SWA_KV_HEADS = max(1, SWA_HEADS // 4)
SB_WIDTH = SB_HEADS * HEAD_DIM
SWA_WIDTH = SWA_HEADS * HEAD_DIM
SWA_KV_WIDTH = SWA_KV_HEADS * HEAD_DIM
MIX_WIDTH_3 = SB_WIDTH + SWA_WIDTH
IN_COLS = 3 * SB_WIDTH + SWA_WIDTH + 2 * SWA_KV_WIDTH
BLOCK = 128
WINDOW = 128
REL_BUCKETS = 32
REL_MAX_DIST = 128
D_FF_3 = -((-8 * D_MODEL) // (3 * 256)) * 256
ALPHA = (2 * DEPTH) ** 0.25
BETA_INIT = (8 * DEPTH) ** -0.25
LN_EPS = 1e-5
RMS_EPS = 1e-6


def layer_norm_3(x, g, b):
    xf = x.astype(jnp.float32)
    mu = jnp.mean(xf, axis=-1, keepdims=True)
    var = jnp.mean(jnp.square(xf - mu), axis=-1, keepdims=True)
    return ((xf - mu) * lax.rsqrt(var + LN_EPS)).astype(x.dtype) * g + b

def rms_norm_3(x, g):
    xf = x.astype(jnp.float32)
    y = xf * lax.rsqrt(jnp.mean(jnp.square(xf), axis=-1, keepdims=True) + RMS_EPS)
    return y.astype(x.dtype) * g

def t5_causal_bucket(distance):
    exact = REL_BUCKETS // 2
    d = jnp.maximum(distance, 0)
    d_f = jnp.maximum(d, 1).astype(jnp.float32)
    large = exact + (jnp.log(d_f / exact) / math.log(REL_MAX_DIST / exact)
                     * (REL_BUCKETS - exact)).astype(jnp.int32)
    large = jnp.minimum(large, REL_BUCKETS - 1)
    return jnp.where(d < exact, d, large)

def stick_breaking_attention(q, k, v):
    B, S, H, Dh = q.shape
    nb = S // BLOCK
    scale = Dh ** -0.5
    qb = q.reshape(B, nb, BLOCK, H, Dh).transpose(1, 0, 3, 2, 4)
    key_pos = jnp.arange(S)

    def one_block(args):
        q_blk, i = args
        z = jnp.einsum('bhqd,bkhd->bhqk', q_blk, k).astype(jnp.float32) * scale
        q_pos = i * BLOCK + jnp.arange(BLOCK)
        causal = key_pos[None, :] < q_pos[:, None]
        log_beta = jax.nn.log_sigmoid(z)
        log_1m_beta = jnp.where(causal, jax.nn.log_sigmoid(-z), 0.0)
        suffix = lax.cumsum(log_1m_beta, axis=3, reverse=True) - log_1m_beta
        attn = jnp.where(causal, jnp.exp(log_beta + suffix), 0.0)
        return jnp.einsum('bhqk,bkhd->bqhd', attn.astype(v.dtype), v)

    out = lax.map(one_block, (qb, jnp.arange(nb)))
    return out.transpose(1, 0, 2, 3, 4).reshape(B, S, H * Dh).astype(v.dtype)

def sliding_window_attention(q, k, v, sinks, rel_bias):
    B, S, H, Dh = q.shape
    KVH = k.shape[2]
    G = H // KVH
    nb = S // BLOCK
    scale = Dh ** -0.5
    qb = q.reshape(B, nb, BLOCK, KVH, G, Dh)

    def band(t):
        tb = t.reshape(B, nb, BLOCK, KVH, Dh)
        prev = jnp.pad(tb[:, :-1], ((0, 0), (1, 0), (0, 0), (0, 0), (0, 0)))
        return jnp.concatenate([prev, tb], axis=2)

    kb, vb = band(k), band(v)
    logits = jnp.einsum('bnqhgd,bnchd->bnhgqc', qb, kb).astype(jnp.float32) * scale

    qi = jnp.arange(BLOCK)[:, None]
    cj = jnp.arange(2 * BLOCK)[None, :]
    dist = qi + BLOCK - cj
    key_abs = jnp.arange(nb)[:, None, None] * BLOCK - BLOCK + cj[None]
    valid = (dist >= 0)[None] & (dist < WINDOW)[None] & (key_abs >= 0)
    bias = rel_bias.astype(jnp.float32)[t5_causal_bucket(dist)]
    bias = bias.transpose(2, 0, 1).reshape(KVH, G, BLOCK, 2 * BLOCK)
    logits = jnp.where(valid[None, :, None, None], logits + bias, -jnp.inf)

    sink = sinks.astype(jnp.float32).reshape(1, 1, KVH, G, 1, 1)
    m = jnp.maximum(jnp.max(logits, axis=-1, keepdims=True), sink)
    p = jnp.exp(logits - m)
    denom = jnp.sum(p, axis=-1, keepdims=True) + jnp.exp(sink - m)
    o = jnp.einsum('bnhgqc,bnchd->bnqhgd', (p / denom).astype(v.dtype), vb)
    return o.reshape(B, S, H * Dh).astype(v.dtype)

def hybrid_mixer(h, w_in, sb_norm_g, swa_norm_g, sinks, rel_bias, w_out):
    B, S, _ = h.shape
    proj = h @ w_in
    o1 = SB_WIDTH
    o2 = o1 + SB_WIDTH
    o3 = o2 + SB_WIDTH
    o4 = o3 + SWA_WIDTH
    o5 = o4 + SWA_KV_WIDTH
    q_sb, k_sb, v_sb, q_sw, k_sw, v_sw = jnp.split(proj, [o1, o2, o3, o4, o5], axis=-1)
    sb_out = stick_breaking_attention(
        q_sb.reshape(B, S, SB_HEADS, HEAD_DIM),
        k_sb.reshape(B, S, SB_HEADS, HEAD_DIM),
        v_sb.reshape(B, S, SB_HEADS, HEAD_DIM))
    swa_out = sliding_window_attention(
        q_sw.reshape(B, S, SWA_HEADS, HEAD_DIM),
        k_sw.reshape(B, S, SWA_KV_HEADS, HEAD_DIM),
        v_sw.reshape(B, S, SWA_KV_HEADS, HEAD_DIM),
        sinks, rel_bias)
    merged = jnp.concatenate([rms_norm_3(sb_out, sb_norm_g),
                              rms_norm_3(swa_out, swa_norm_g)], axis=-1)
    return merged @ w_out

def swiglu_ffn(h, w_gate_up, w_down):
    gate, up = jnp.split(h @ w_gate_up, 2, axis=-1)
    return (jax.nn.silu(gate) * up) @ w_down

def third_inputs(seed: int = 0) -> dict:
    key = jax.random.key(seed)
    ks = jax.random.split(key, 16)
    f32 = jnp.float32
    n = lambda k, shape, s: jax.random.normal(k, shape, f32) * s
    return {
        "x": n(ks[0], (BATCH, SEQ, D_MODEL), 1.0),
        "ln_in_g": 1.0 + n(ks[1], (D_MODEL,), 0.02),
        "ln_in_b": n(ks[2], (D_MODEL,), 0.02),
        "w_in": n(ks[3], (DEPTH, D_MODEL, IN_COLS), D_MODEL ** -0.5),
        "sb_norm_g": 1.0 + n(ks[4], (DEPTH, SB_WIDTH), 0.02),
        "swa_norm_g": 1.0 + n(ks[5], (DEPTH, SWA_WIDTH), 0.02),
        "sinks": n(ks[6], (DEPTH, SWA_HEADS), 0.5),
        "rel_bias": n(ks[7], (REL_BUCKETS, SWA_HEADS), 0.5),
        "w_out": n(ks[8], (DEPTH, MIX_WIDTH_3, D_MODEL), MIX_WIDTH_3 ** -0.5 * BETA_INIT),
        "ln1_g": 1.0 + n(ks[9], (DEPTH, D_MODEL), 0.02),
        "ln1_b": n(ks[10], (DEPTH, D_MODEL), 0.02),
        "w_gate_up": n(ks[11], (DEPTH, D_MODEL, 2 * D_FF_3), D_MODEL ** -0.5),
        "w_down": n(ks[12], (DEPTH, D_FF_3, D_MODEL), D_FF_3 ** -0.5 * BETA_INIT),
        "ln2_g": 1.0 + n(ks[13], (DEPTH, D_MODEL), 0.02),
        "ln2_b": n(ks[14], (DEPTH, D_MODEL), 0.02),
    }

def third_block(x, ln_in_g, ln_in_b, w_in, sb_norm_g, swa_norm_g, sinks, rel_bias,
              w_out, ln1_g, ln1_b, w_gate_up, w_down, ln2_g, ln2_b):
    h = layer_norm_3(x, ln_in_g, ln_in_b)
    for l in range(DEPTH):
        mix = hybrid_mixer(h, w_in[l], sb_norm_g[l], swa_norm_g[l], sinks[l], rel_bias, w_out[l])
        h = layer_norm_3(ALPHA * h + mix, ln1_g[l], ln1_b[l])
        ffn = swiglu_ffn(h, w_gate_up[l], w_down[l])
        h = layer_norm_3(ALPHA * h + ffn, ln2_g[l], ln2_b[l])
    return h


_first_inputs_3 = third_inputs


def third_inputs(seed=0):
    import zlib

    import numpy as np

    out = dict(_first_inputs_3(seed))
    spreads = {}
    factors = {'sb_norm_g': 8.0,
     'swa_norm_g': 8.0,
     'sinks': 8.0,
     'ln1_g': 2.74,
     'ln1_b': 2.806,
     'ln2_g': 2.749,
     'ln2_b': 2.873}
    for name, (base, spread) in spreads.items():
        noise = np.random.default_rng([zlib.crc32(name.encode()), seed]).standard_normal(out[name].shape)
        drawn = base * np.exp(spread * noise) if base else spread * noise
        out[name] = __import__('jax').numpy.asarray(drawn.astype(out[name].dtype))
    for name, factor in factors.items():
        out[name] = (out[name] * factor).astype(out[name].dtype)
    return out


_narrow_inputs_3 = third_inputs


def third_inputs(seed=0):

    out = dict(_narrow_inputs_3(seed))
    wider = {'sb_norm_g': 3.88, 'swa_norm_g': 3.75, 'ln2_g': 3.09, 'ln2_b': 3.09}
    for name, times in wider.items():
        mean = out[name].mean()
        out[name] = (mean + times * (out[name] - mean)).astype(out[name].dtype)
    return out


def setup_inputs(seed=0):
    out = dict(first_inputs(seed))
    for name, value in second_inputs(seed + 1).items():
        if name != "x":
            out[name + "_2"] = value
    for name, value in third_inputs(seed + 2).items():
        if name != "x":
            out[name + "_3"] = value
    return out


def reference(
    x, mix_norm_g, w_in, ret_norm_g, sgu_ln_g, sgu_ln_b, sgu_w_s, sgu_b_s, w_out, ffn_norm_g,
    w_up, conv_w, conv_b, w_down, final_norm_g, ln_g_2, w_in_2, b_in_2, dw_w_2, dw_b_2, cln_g_2,
    cln_b_2, pw_w_2, pw_b_2, rpb_2, gn_conv_g_2, gn_att_g_2, w_out_2, final_g_2, ln_in_g_3,
    ln_in_b_3, w_in_3, sb_norm_g_3, swa_norm_g_3, sinks_3, rel_bias_3, w_out_3, ln1_g_3,
    ln1_b_3, w_gate_up_3, w_down_3, ln2_g_3, ln2_b_3,
):
    x = first_block(
        x, mix_norm_g, w_in, ret_norm_g, sgu_ln_g, sgu_ln_b, sgu_w_s, sgu_b_s, w_out,
        ffn_norm_g, w_up, conv_w, conv_b, w_down, final_norm_g,
    )
    x = second_block(
        x, ln_g_2, w_in_2, b_in_2, dw_w_2, dw_b_2, cln_g_2, cln_b_2, pw_w_2, pw_b_2, rpb_2,
        gn_conv_g_2, gn_att_g_2, w_out_2, final_g_2,
    )
    return third_block(
        x, ln_in_g_3, ln_in_b_3, w_in_3, sb_norm_g_3, swa_norm_g_3, sinks_3, rel_bias_3,
        w_out_3, ln1_g_3, ln1_b_3, w_gate_up_3, w_down_3, ln2_g_3, ln2_b_3,
    )


_drawn_inputs = setup_inputs


def setup_inputs(seed=0):
    import zlib

    import numpy as np

    out = dict(_drawn_inputs(seed))
    spreads = {}
    factors = {}
    for name, (base, spread) in spreads.items():
        noise = np.random.default_rng([zlib.crc32(name.encode()), seed]).standard_normal(out[name].shape)
        drawn = base * np.exp(spread * noise) if base else spread * noise
        out[name] = __import__('jax').numpy.asarray(drawn.astype(out[name].dtype))
    for name, factor in factors.items():
        out[name] = (out[name] * factor).astype(out[name].dtype)
    return out
```

```python
from contextlib import ExitStack, contextmanager

import concourse.bass as bass
from concourse import mybir
import numpy as np

ALU = mybir.AluOpType
ACT = mybir.ActivationFunctionType
F32 = mybir.dt.float32
F32R = mybir.dt.float32r
AX_X = mybir.AxisListType.X

P = 128
S = 1024
D = 1024
KD = D // P
HALF = 512
CH = 128
NCH = S // CH
DFF = 2816
NGROUP = DFF // (2 * P)
MASKED = -1e30
SCALE = 64 ** -0.5
EPS = 1e-6
LN_EPS = 1e-5
ALPHA = 2.0 ** 0.25

RET_HEADS = 4
SGU_GROUPS = 4
CONV_TILES = 4
TAPS = 31
PAD = TAPS // 2
GRID_W = 64
ROWS = S // GRID_W
KH = 8
KW = 16
NA_HEADS = 8
REL_H = 2 * KH - 1
REL_W = 2 * KW - 1
REL_PAD = 2 * GRID_W
SWA_HEADS = 8
BUCKETS = 32
LN_TOP = 40.0
BAND = 2 * CH
REL_BAND = 384

VEC = {}


def _lay_vectors():
    at = 0
    for name, n in (("mix_norm_g", 8), ("ret_norm_g", 4), ("sgu_ln_g", 4), ("sgu_ln_b", 4),
                    ("ffn_norm_g", 8), ("conv_w0", 44), ("conv_w1", 44), ("conv_w2", 44), ("conv_b", 44),
                    ("final_norm_g", 8), ("ln_g_2", 8), ("b_in_2", 28), ("dw_w_2", 4 * TAPS), ("dw_b_2", 4),
                    ("cln_g_2", 4), ("cln_b_2", 4), ("pw_b_2", 4), ("gn_conv_g_2", 4), ("gn_att_g_2", 4),
                    ("final_g_2", 8), ("ln_in_g_3", 8), ("ln_in_b_3", 8), ("sb_norm_g_3", 4),
                    ("swa_norm_g_3", 4), ("ln1_g_3", 8), ("ln1_b_3", 8), ("ln2_g_3", 8), ("ln2_b_3", 8)):
        VEC[name] = at
        at += n
    return at


NVEC = _lay_vectors()

CONST_COLS = {}


def shape_constants():
    f = np.float32
    i = np.arange(P)
    parts = [
        ("ident", np.eye(P)),
        ("mean1024", np.full((P, P), 1 / 1024)),
        ("mean512", np.full((P, P), 1 / 512)),
        ("mean128", np.full((P, P), 1 / 128)),
        ("mean64", (i[:, None] // 64 == i[None, :] // 64) / 64),
        ("neg_tri", -(i[:, None] >= i[None, :]).astype(f)),
        ("neg_ones", np.full((P, P), -1.0)),
        ("after", (i[:, None] < i[None, :])),
        ("bar_after", np.where(i[:, None] < i[None, :], 0, MASKED)),
        ("tril_t", (i[:, None] <= i[None, :])),
        (f"eps{EPS}", np.full((P, 1), EPS)),
        (f"eps{LN_EPS}", np.full((P, 1), LN_EPS)),
    ]
    at = 0
    for name, a in parts:
        CONST_COLS[name] = at
        at += a.shape[1]
    common = np.concatenate([np.asarray(a, f) for _, a in parts], axis=1)

    half = P // 2
    inv = np.power(f(10000.0), -np.arange(half, dtype=f) / f(half)).astype(f)
    ang = (np.arange(S, dtype=f)[None, :] * inv[:, None]).astype(f)
    rotary = np.stack([np.concatenate([np.cos(ang)] * 2), np.concatenate([np.sin(ang), -np.sin(ang)])], 1)

    pos = np.arange(CH, dtype=np.float64)
    ret = []
    for h in range(RET_HEADS):
        lg = np.log(1.0 - 2.0 ** (-5.0 - h))
        diff = pos[None, :] - pos[:, None]
        scale = P ** -0.5
        mask = np.where(diff >= 0, np.exp(lg * np.maximum(diff, 0)), 0) * scale
        qd = np.broadcast_to(np.exp(lg * (pos + 1))[None, :], (P, CH))
        kd = (np.exp(lg * (CH - 1 - pos)) * scale)[:, None]
        ret.append(np.concatenate([mask, qd, kd, np.full((P, 1), np.exp(lg * CH))], 1))

    w = np.arange(GRID_W)
    start = np.clip(w - KW // 2, 0, GRID_W - KW)
    seen = (w[None, :] >= start[:, None]) & (w[None, :] < start[:, None] + KW)
    cols = np.tile(np.where(seen, 0, MASKED), (2, 1))

    j = np.arange(REL_BAND)
    dist = 255 - j
    exact = BUCKETS // 2
    d = np.maximum(dist, 0)
    large = exact + (np.log(np.maximum(d, 1).astype(f) / exact) / f(np.log(128 / exact)) * exact).astype(np.int32)
    bucket = np.where(d < exact, d, np.minimum(large, BUCKETS - 1))
    inside = (dist >= 0) & (dist < CH)
    onehot = ((np.arange(BUCKETS)[:, None] == bucket[None, :]) & inside[None, :])
    outside = np.broadcast_to(np.where(inside, 0, MASKED)[None, :], (SWA_HEADS, REL_BAND))
    tables = {"rotary": rotary, "retention": np.stack(ret), "seen": cols, "onehot": onehot, "outside": outside}
    return common, {k: np.ascontiguousarray(v, dtype=f) for k, v in tables.items()}


COMMON, TABLES = shape_constants()


class Token:
    def __init__(self, line, count, loop, shift=0):
        self.line, self.count, self.loop, self.shift = line, count, loop, shift


class Line:

    def __init__(self, prog, sem, step=1):
        self.prog, self.sem, self.step, self.count = prog, sem, step, 0
        prog.lines.append(self)
        prog.line_of[sem.name] = self

    def sig(self, ins):
        ins.then_inc(self.sem, self.step)
        self.count += self.step
        return Token(self, self.count, self.prog.loop)


class Loop:
    def __init__(self, name, n, index, starts, per):
        self.name, self.n, self.index, self.starts, self.per, self.open = name, n, index, starts, per, True


class Held:

    def __init__(self, prog, name):
        self.prog, self.name, self.tokens, self.loop = prog, name, [], None
        prog.held.append(self)

    def set(self, *tokens):
        self.tokens, self.loop = list(tokens), self.prog.loop

    def follow(self, *engines):
        loop = self.prog.loop
        for eng in engines:
            eng.wait(*self.tokens)
            if loop is not None and self.loop is not loop:
                for sem, back in self.prog.last_turn.get((loop.name, self.name), []):
                    line = self.prog.line_of[sem]
                    eng.wait(Token(line, loop.starts[line] + back, loop, shift=-1))


class Slot(Held):

    def __init__(self, prog, name, ap):
        super().__init__(prog, name)
        self.ap = ap

    def claim(self, eng):
        self.follow(eng)
        self.set()
        return self.ap

    def free(self, *tokens):
        self.set(*self.tokens, *tokens)


class Engine:

    def __init__(self, prog, eng, sem):
        self.prog, self.e, self.line, self.seen = prog, eng, Line(prog, sem), {}

    def sig(self, ins):
        return self.line.sig(ins)

    def wait(self, *tokens):
        for t in tokens:
            loop = t.loop
            if loop is not None and loop.open:
                per = loop.per.get(t.line.sem.name, 0)
                base = t.count + t.shift * per
                key = (t.line, loop, t.shift)
                if self.seen.get(key, -1) >= t.count:
                    continue
                self.seen[key] = t.count
                if per == 0:
                    self.e.wait_ge(t.line.sem, max(base, 1))
                else:
                    assert base >= 1, (loop.name, t.line.sem.name, base)
                    self.e.wait_ge(t.line.sem, loop.index * per + base)
            else:
                value = t.count
                if loop is not None:
                    value += (loop.n - 1) * loop.per.get(t.line.sem.name, 0)
                if self.seen.get(t.line, 0) >= value:
                    continue
                self.seen[t.line] = value
                self.e.wait_ge(t.line.sem, value)

    def turn_before(self):
        loop = self.prog.loop
        return Token(self.line, loop.starts[self.line], loop)


class Program:
    BUMP = 1024

    def __init__(self, nc, ctx, counts, last_turn):
        self.nc, self.ctx, self.counts, self.last_turn = nc, ctx, counts, last_turn
        self.lines, self.line_of, self.held, self.loop = [], {}, [], None
        self.found_counts, self.found_last = {}, {}
        self.pe, self.act, self.dve, self.pool, self.sp = (
            Engine(self, e, self.sem(n)) for e, n in (
                (nc.tensor, "pe_done"), (nc.scalar, "act_done"), (nc.vector, "dve_done"),
                (nc.gpsimd, "pool_done"), (nc.sync, "sp_done")))
        for eng in (self.pe, self.act, self.dve, self.pool):
            eng.e.sem_inc(eng.line.sem, self.BUMP)
            eng.line.count = self.BUMP

    def sem(self, name):
        return self.ctx.enter_context(self.nc.semaphore(name))

    def dma_line(self, name):
        line = Line(self, self.sem(name), 16)
        self.nc.sync.sem_inc(line.sem, self.BUMP)
        line.count = self.BUMP
        return line

    def slot(self, name, ap):
        return Slot(self, name, ap)

    @contextmanager
    def repeat(self, name, n):
        starts = {x: x.count for x in self.lines}
        with self.nc.Fori(0, n) as index:
            self.loop = Loop(name, n, index, starts, self.counts.get(name, {}))
            loop = self.loop
            yield index
            self.loop = None
        per = {x.sem.name: x.count - starts[x] for x in self.lines}
        assert not self.counts or per == self.counts[name], name
        self.found_counts[name] = per
        loop.per, loop.open = per, False
        for s in self.held:
            mine = [t for t in s.tokens if t.loop is loop]
            if mine:
                self.found_last[(name, s.name)] = [(t.line.sem.name, t.count - starts[t.line]) for t in mine]
        for x in self.lines:
            x.count = starts[x] + n * per[x.sem.name]
        for eng in (self.pe, self.act, self.dve, self.pool, self.sp):
            eng.seen = {}

    def meet(self):
        self.nc.all_engine_barrier()


class Blocks(Program):
    def setup(self, t, blocks):
        nc, ctx = self.nc, self.ctx
        self.t = t
        self.blocks = blocks

        def sb(name, shape, dt=F32):
            return ctx.enter_context(nc.sbuf_tensor(name, shape, dt))

        self.x = sb("residual", [P, KD, S])
        self.h_hi = sb("h_hi", [P, KD, S], F32R)
        self.h_lo = sb("h_lo", [P, KD, S], F32R)
        self.vec = sb("vectors", [P, NVEC])
        self.common = sb("common", [P, COMMON.shape[1]])
        raw = sb("w_raw", [P, 2, KD * P])
        whi = sb("w_hi", [P, 2, KD * P], F32R)
        wlo = sb("w_lo", [P, 2, KD * P], F32R)
        self.w_raw = [self.slot(f"w_raw{i}", raw[:, i, :]) for i in range(2)]
        self.w_split = [self.slot(f"w_split{i}", (whi[:, i, :], wlo[:, i, :])) for i in range(2)]
        self.w_line = [self.dma_line(f"w_loaded{i}") for i in range(2)]
        self.aux = {}
        self.out_line = self.dma_line("stored")
        psum = ctx.enter_context(nc.psum_tensor("psum", [P, 8, HALF], F32))
        self.psum = psum
        two = lambda b: psum[:, b:b + 2, :].rearrange("p b n -> p (b n)")
        self.acc = [self.slot(f"acc{i}", two(2 * i)) for i in range(2)]
        self.wide = [self.slot(f"wide{i}", two(4 + 2 * i)) for i in range(2)]
        self.bank = [self.slot(f"bank{i}", psum[:, i, :]) for i in range(8)]
        self.n_acc = self.n_wide = 0
        self.w_loaded = [Held(self, f"w_loaded{i}") for i in range(2)]
        self.w_ready = [Held(self, f"w_ready{i}") for i in range(2)]
        self.tile_no, self.tile_base = 0, 0
        sp = self.sp
        self.fetch("start", self.vec[:], t["vectors"])
        self.fetch("start", self.common[:], t["common"])
        self.load_token = self.fetch("start", self.x[:], t["x_t"].rearrange("(c p) s -> p c s", p=P))
        for eng in (self.pe, self.act, self.dve, self.pool):
            eng.wait(self.load_token)
        self.w_load(0)
        self.w_load(1)
        self.w_split_tile(0)
        if blocks != (1,):
            self.bias_copies()

    def fetch(self, name, dst, src):
        return self.line_for(name).sig(self.sp.e.dma_start(dst, src))

    def line_for(self, name):
        if name not in self.aux:
            self.aux[name] = self.dma_line(f"{name}_loaded")
        return self.aux[name]

    def c(self, name, n=P):
        at = CONST_COLS[name]
        return self.common[:, at:at + n]

    def v(self, name, i=0):
        at = VEC[name] + i
        return self.vec[:, bass.ds(at, 1)]

    def bias_copies(self):
        sp, pe, dve, t = self.sp, self.pe, self.dve, self.t
        with self.scope("bias") as sb:
            padded = sb("padded", [NA_HEADS * REL_H, REL_PAD])
            sp.wait(dve.sig(dve.e.memset(padded[:], 0.0)))
            off = GRID_W - KW
            sp.wait(self.fetch("rpb", padded[:, off:off + REL_W], t["rpb"]))
            put_rel = self.fetch("rel_rows", t["rel_rows"], padded[:])
            rel = sb("rel", [BUCKETS, SWA_HEADS])
            onehot = sb("onehot", [BUCKETS, REL_BAND])
            band = sb("band", [SWA_HEADS, REL_BAND])
            self.fetch("swa", rel[:], t["rel_bias"])
            self.fetch("swa", onehot[:], t["onehot"])
            got = self.fetch("swa", band[:], t["outside"])
            pe.wait(got)
            b = self.bank[7]
            done = pe.sig(pe.e.matmul(b.claim(pe)[0:SWA_HEADS, 0:REL_BAND], rel[:], onehot[:], start=True, stop=True))
            dve.wait(done, got)
            line = dve.sig(dve.e.tensor_tensor(band[:], band[:], b.ap[0:SWA_HEADS, 0:REL_BAND], ALU.add))
            b.free(line)
            sp.wait(line)
            put_band = self.fetch("band_rows", t["band_rows"], band[:])
            sp.wait(put_rel, put_band)
            for h in range(NA_HEADS):
                rows = t["rel_rows"][h * REL_H:(h + 1) * REL_H, :].rearrange("(o r) w -> o (r w)", o=1)
                self.fetch("rel_copies", t["rel_copies"][h, :].rearrange("(q n) -> q n", q=GRID_W),
                           rows.broadcast_to([GRID_W, REL_H * REL_PAD]))
                self.fetch("band_copies", t["band_copies"][h, :].rearrange("(q n) -> q n", q=CH),
                           t["band_rows"][h:h + 1, :].broadcast_to([CH, REL_BAND]))

    def copies_done(self, name):
        line = self.aux[name]
        self.sp.wait(Token(line, line.count, None))

    def w_load(self, ahead_no):
        slot = self.w_raw[ahead_no % 2]
        slot.claim(self.sp)
        no = ahead_no
        if self.loop is not None:
            no = ahead_no + self.loop.index * self.w_turn
        src = self.t["weights"][bass.ds(no, 1), :, :].rearrange("a p n -> (a p) n") if self.loop is not None \
            else self.t["weights"][no, :, :]
        self.w_loaded[ahead_no % 2].set(self.w_line[ahead_no % 2].sig(self.sp.e.dma_start(slot.ap, src)))

    def w_split_tile(self, no):
        raw, out = self.w_raw[no % 2], self.w_split[no % 2]
        hi, lo = out.claim(self.act)
        self.w_loaded[no % 2].follow(self.act)
        a = self.act.sig(self.act.e.activation(hi, raw.ap, ACT.Copy))
        self.dve.wait(a)
        b = self.dve.sig(self.dve.e.tensor_tensor(lo, raw.ap, hi.bitcast(F32), ALU.subtract))
        raw.free(b)
        self.w_ready[no % 2].set(a, b)

    @contextmanager
    def w_turns(self, name, n, tiles):
        assert tiles % 2 == 0
        self.w_turn = tiles
        before = self.tile_no
        with self.repeat(name, n) as i:
            yield i
            assert self.tile_no == before + tiles, (name, self.tile_no - before)
        self.tile_no = before + n * tiles

    def next_tile(self):
        t = self.tile_no
        self.w_split_tile(t + 1)
        slot = self.w_split[t % 2]
        self.w_ready[t % 2].follow(self.pe)
        self.w_load(t + 2)
        self.tile_no = t + 1
        return slot

    def gemm(self, slot_out, tile, n_k, cols, lo_col, src, ready=None):
        pe = self.pe
        out = slot_out.claim(pe)
        hi, lo = (a.rearrange("p (k n) -> p k n", n=cols) for a in tile.ap)
        for k in range(n_k):
            if ready is not None:
                pe.wait(*ready[k])
            for part, (w, x) in enumerate(((hi, src(k, 0)), (hi, src(k, 1)), (lo, src(k, 0)))):
                for half in range(2):
                    s = slice(half * HALF, (half + 1) * HALF)
                    ins = pe.e.matmul(out[:, s], w[:, k, lo_col:lo_col + P], x[:, s],
                                      start=(k == 0 and part == 0), stop=(k == n_k - 1 and part == 2))
        return pe.sig(ins)

    def next_acc(self):
        self.n_acc += 1
        return self.acc[(self.n_acc - 1) % 2]

    def next_wide(self):
        self.n_wide += 1
        return self.wide[(self.n_wide - 1) % 2]

    def project(self, ready=None):
        tile = self.next_tile()
        acc = self.next_acc()
        done = self.gemm(acc, tile, KD, P, 0, lambda k, part: (self.h_lo if part else self.h_hi)[:, k, :], ready)
        tile.free(done)
        return acc, done

    def column_mean(self, ones, src, token, w=None):
        w = w or self.next_wide()
        out = w.claim(self.pe)
        self.pe.wait(token)
        for half in range(2):
            s = slice(half * HALF, (half + 1) * HALF)
            ins = self.pe.e.matmul(out[:, s], ones, src[:, s], start=True, stop=True)
        return w, self.pe.sig(ins)

    def rsqrt_of(self, w, token, out, eps):
        act = self.act
        act.wait(token)
        ln = act.sig(act.e.activation(out, w.ap, ACT.Ln, bias=self.c(f"eps{eps}", 1)))
        w.free(ln)
        act.wait(ln)
        return act.sig(act.e.activation(out, out, ACT.Exp, scale=-0.5))

    def split(self, src, hi, lo, token):
        self.act.wait(token)
        a = self.act.sig(self.act.e.activation(hi, src, ACT.Copy))
        self.dve.wait(a)
        b = self.dve.sig(self.dve.e.tensor_tensor(lo, src, hi.bitcast(F32), ALU.subtract))
        return (a, b)

    def sum_of_squares(self, tiles, acc, sq, tokens):
        act, dve = self.act, self.dve
        last = None
        for k, tile in enumerate(tiles):
            act.wait(*tokens[k])
            if k == 0:
                last = act.sig(act.e.activation(acc, tile, ACT.Square))
            else:
                buf = sq[k % 2]
                q = act.sig(act.e.activation(buf.claim(act), tile, ACT.Square))
                dve.wait(q, last)
                last = dve.sig(dve.e.tensor_tensor(acc, acc, buf.ap, ALU.add))
                buf.free(last)
        return last

    def rms(self, tiles, ones, gain, eps, out, name, tokens=None):
        tokens = tokens or [()] * len(tiles)
        with self.scope(name) as sb:
            acc = sb("acc", [P, S])
            sq = [self.slot(f"{name}_sq{i}", sb(f"sq{i}", [P, S])[:]) for i in range(2)]
            rstd = sb("rstd", [P, S])
            total = self.sum_of_squares(tiles, acc[:], sq, tokens)
            w, m = self.column_mean(ones, acc[:], total)
            r = self.rsqrt_of(w, m, rstd[:], eps)
            self.dve.wait(r)
            res = []
            for k, tile in enumerate(tiles):
                if out is None:
                    res.append(self.dve.sig(self.dve.e.scalar_tensor_tensor(
                        tile, tile, self.v(gain, k), rstd[:], ALU.mult, ALU.mult)))
                else:
                    buf = sq[k % 2]
                    n = self.dve.sig(self.dve.e.scalar_tensor_tensor(
                        buf.claim(self.dve), tile, self.v(gain, k), rstd[:], ALU.mult, ALU.mult))
                    pair = self.split(buf.ap, *out(k), n)
                    buf.free(*pair)
                    res.append(pair)
            if out is None:
                self.dve.wait(res[-1])
        return res

    def layer_norm(self, tiles, ones, gain, bias, eps, name, split_to=None, func=None):
        act, dve = self.act, self.dve
        res = []
        with self.scope(name) as sb:
            acc = sb("acc", [P, S])
            sq = [self.slot(f"{name}_sq{i}", sb(f"sq{i}", [P, S])[:]) for i in range(2)]
            rstd = sb("rstd", [P, S])
            last = dve.sig(dve.e.tensor_tensor(acc[:], tiles[0], tiles[1], ALU.add))
            for tile in tiles[2:]:
                dve.wait(last)
                last = dve.sig(dve.e.tensor_tensor(acc[:], acc[:], tile, ALU.add))
            w, m = self.column_mean(ones, acc[:], last)
            dve.wait(m)
            centred = [dve.sig(dve.e.tensor_tensor(t, t, w.ap, ALU.subtract)) for t in tiles]
            w.free(centred[-1])
            total = self.sum_of_squares(tiles, acc[:], sq, [(t,) for t in centred])
            w, m = self.column_mean(ones, acc[:], total)
            r = self.rsqrt_of(w, m, rstd[:], eps)
            dve.wait(r)
            for k, tile in enumerate(tiles):
                n = dve.sig(dve.e.scalar_tensor_tensor(tile, tile, self.v(gain, k), rstd[:], ALU.mult, ALU.mult))
                act.wait(n)
                n = act.sig(act.e.activation(tile, tile, func or ACT.Identity, bias=self.v(bias, k)))
                if split_to is not None:
                    act.wait(n)
                    dve.wait(n)
                    res.append(self.split(tile, *split_to(k), n))
            dve.wait(n)
        return res

    @contextmanager
    def scope(self, name):
        with ExitStack() as ctx:
            yield lambda n, shape, dt=F32: ctx.enter_context(self.nc.sbuf_tensor(f"{name}_{n}", shape, dt))
            self.meet()

    def h(self, k):
        return self.h_hi[:, k, :], self.h_lo[:, k, :]

    def mix_out(self, name, alpha, ready):
        with self.w_turns(f"{name}_out", KD // 2, 2) as i:
            for j in range(2):
                acc, done = self.project(ready)
                self.dve.wait(done)
                x = self.x[:, i * 2 + j, :]
                acc.free(self.dve.sig(self.dve.e.scalar_tensor_tensor(x, x, alpha, acc.ap, ALU.mult, ALU.add)))

    def mlp(self, name, conv):
        act, dve, pe = self.act, self.dve, self.pe
        with self.scope(name) as sb:
            act_hi = sb("act_hi", [P, 2, S], F32R)
            act_lo = sb("act_lo", [P, 2, S], F32R)
            hid = [self.slot(f"{name}_hid{j}", (act_hi[:, j, :], act_lo[:, j, :])) for j in range(2)]
            ta = self.slot(f"{name}_ta", sb("ta", [P, S])[:])
            tb = self.slot(f"{name}_tb", sb("tb", [P, S])[:])
            tp = self.slot(f"{name}_tp", sb("tp", [P, S])[:])
            state = {}
            hid_ready = [Held(self, f"{name}_hid_ready{j}") for j in range(2)]

            def taps(dst, acc, done, channel):
                act.wait(done)
                y = dst.claim(act)
                t0 = act.sig(act.e.activation(y, acc.ap, ACT.Identity, bias=self.v("conv_b", channel),
                                              scale=self.v("conv_w2", channel)))
                dve.wait(t0)
                t1 = dve.sig(dve.e.scalar_tensor_tensor(y[:, 1:S], acc.ap[:, 0:S - 1], self.v("conv_w1", channel),
                                                        y[:, 1:S], ALU.mult, ALU.add))
                dve.wait(t1)
                t2 = dve.sig(dve.e.scalar_tensor_tensor(y[:, 2:S], acc.ap[:, 0:S - 2], self.v("conv_w0", channel),
                                                        y[:, 2:S], ALU.mult, ALU.add))
                acc.free(t2)
                return t2

            def gate(channel, ready=None):
                acc, done = self.project(ready)
                if conv:
                    t = taps(ta, acc, done, channel)
                    act.wait(t)
                    state["a"] = act.sig(act.e.activation(ta.ap, ta.ap, ACT.Silu))
                else:
                    act.wait(done)
                    state["a"] = act.sig(act.e.activation(ta.claim(act), acc.ap, ACT.Silu))
                    acc.free(state["a"])

            def up(channel, j):
                acc, done = self.project()
                if conv:
                    t = taps(tb, acc, done, channel + DFF // P)
                    src = tb.ap
                else:
                    t, src = done, acc.ap
                dve.wait(t, state["a"])
                out = tp.claim(dve)
                m = dve.sig(dve.e.tensor_tensor(out, ta.ap, src, ALU.mult))
                ta.free(m)
                (tb if conv else acc).free(m)
                hi, lo = hid[j].claim(act)
                pair = self.split(out, hi, lo, m)
                tp.free(*pair)
                hid_ready[j].set(*pair)

            def down():
                hid_ready[0].follow(pe)
                hid_ready[1].follow(pe)
                for half in range(2):
                    tile = self.next_tile()
                    for n in range(4):
                        w = self.next_wide()
                        done = self.gemm(w, tile, 2, 4 * P, n * P,
                                         lambda k, part: (act_lo if part else act_hi)[:, k, :])
                        x = self.x[:, half * 4 + n, :]
                        dve.wait(done)
                        w.free(dve.sig(dve.e.tensor_tensor(x, x, w.ap, ALU.add)))
                    tile.free(done)
                hid[0].free(done)
                hid[1].free(done)

            gate(0, self.h_ready)
            up(0, 0)
            gate(1)
            up(1, 1)
            with self.w_turns(name, NGROUP - 1, 6) as i:
                gate(i * 2 + 2)
                down()
                up(i * 2 + 2, 0)
                gate(i * 2 + 3)
                up(i * 2 + 3, 1)
            down()

    def first(self):
        self.h_ready = self.rms([self.x[:, k, :] for k in range(KD)], self.c("mean1024"), "mix_norm_g", EPS,
                                self.h, "norm1")
        y = self.ctx_y("y1")
        self.retention(y)
        self.sgu(y)
        ready = [self.split(y[:, k, :], *self.h(k), self.dve_now()) for k in range(KD)]
        self.meet()
        self.close_y()
        self.mix_out("mix1", 1.0, ready)
        self.meet()
        self.h_ready = self.rms([self.x[:, k, :] for k in range(KD)], self.c("mean1024"), "ffn_norm_g", EPS,
                                self.h, "norm2")
        self.mlp("mlp1", True)
        self.rms([self.x[:, k, :] for k in range(KD)], self.c("mean1024"), "final_norm_g", EPS, None, "norm3")

    def dve_now(self):
        return Token(self.dve.line, self.dve.line.count, None)

    def ctx_y(self, name):
        self.y_ctx = ExitStack()
        return self.y_ctx.enter_context(self.nc.sbuf_tensor(name, [P, KD, S], F32))

    def close_y(self):
        self.y_ctx.close()

    def transposes(self, w, src, token, n=NCH, step=CH, first=0):
        pe = self.pe
        out = w.claim(pe)
        pe.wait(token)
        for b in range(n):
            at = (first + b) * step
            ins = pe.e.transpose(out[:, b * P:(b + 1) * P], src[:, at:at + P], self.c("ident"))
        return pe.sig(ins)

    def retention(self, y):
        act, dve, pe, sp = self.act, self.dve, self.pe, self.sp
        with self.scope("ret") as sb:
            rot = sb("rotary", [P, 2, S])
            table = sb("table", [P, 2 * P + 2])
            buf = {n: sb(n, [P, S]) for n in ("q", "k", "t", "gate", "state", "vtok", "ktok", "sT")}
            q, k, t, gate, st, vtok, ktok, sT = (buf[n][:] for n in ("q", "k", "t", "gate", "state", "vtok", "ktok", "sT"))
            mask, qdec = table[:, 0:P], table[:, P:2 * P]
            kdec, cdec = table[:, 2 * P:2 * P + 1], table[:, 2 * P + 1:2 * P + 2]
            rot_loaded = self.fetch("rotary", rot[:], self.t["rotary"])
            dve.wait(rot_loaded)
            table_slot = self.slot("ret_table", table[:])
            self.line_for("ret_table")
            chunks = lambda a: a.rearrange("p (n c) -> p n c", c=CH)

            def rotary(dst, acc, done, prior):
                dve.wait(done, *prior)
                a = dve.sig(dve.e.tensor_tensor(t[0:64, :], acc.ap[64:P, :], rot[64:P, 1, :], ALU.mult))
                b = dve.sig(dve.e.tensor_tensor(t[64:P, :], acc.ap[0:64, :], rot[0:64, 1, :], ALU.mult))
                c = dve.sig(dve.e.tensor_tensor(dst, acc.ap, rot[:, 0, :], ALU.mult))
                acc.free(c)
                dve.wait(c)
                d = dve.sig(dve.e.tensor_tensor(dst, dst, t, ALU.add))
                dve.wait(d)
                return d

            first = [self.h_ready]
            with self.w_turns("ret", RET_HEADS, 4) as head:
                table_slot.claim(sp)
                got_table = self.fetch(
                    "ret_table", table[:], self.t["retention"][bass.ds(head, 1), :, :].rearrange("a p n -> (a p) n"))
                before = [pe.turn_before(), act.turn_before()]
                acc, done = self.project(first[0])
                q_rot = rotary(q, acc, done, before)
                acc, done = self.project()
                k_rot = rotary(k, acc, done, [])
                acc, done = self.project()
                act.wait(done, k_rot)
                v_raw = act.sig(act.e.activation(t, acc.ap, ACT.Copy))
                acc.free(v_raw)
                acc, done = self.project()
                act.wait(done, dve.turn_before())
                g_silu = act.sig(act.e.activation(gate, acc.ap, ACT.Silu))
                acc.free(g_silu)
                w = self.next_wide()
                tr = self.transposes(w, t, v_raw)
                act.wait(tr)
                v_tok = act.sig(act.e.activation(vtok, w.ap, ACT.Copy))
                w.free(v_tok)
                w = self.next_wide()
                tr = self.transposes(w, k, k_rot)
                act.wait(tr, got_table)
                k_tok = act.sig(act.e.activation(ktok, w.ap, ACT.Copy, scale=kdec))
                w.free(k_tok)
                w = self.next_wide()
                out = w.claim(pe)
                for n in range(NCH):
                    c = slice(n * CH, (n + 1) * CH)
                    ins = pe.e.matmul(out[:, c], k[:, c], q[:, c], start=True, stop=True)
                s_done = pe.sig(ins)
                dve.wait(s_done, got_table)
                s_mask = dve.sig(dve.e.tensor_tensor(
                    chunks(sT), chunks(w.ap), mask.unsqueeze(1).broadcast_to([P, NCH, CH]), ALU.mult))
                w.free(s_mask)
                q_dec = dve.sig(dve.e.tensor_tensor(
                    chunks(q), chunks(q), qdec.unsqueeze(1).broadcast_to([P, NCH, CH]), ALU.mult))
                w = self.next_wide()
                out = w.claim(pe)
                pe.wait(v_tok, k_tok)
                for n in range(NCH - 1):
                    c = slice(n * CH, (n + 1) * CH)
                    ins = pe.e.matmul(out[:, c], ktok[:, c], vtok[:, c], start=True, stop=True)
                kv = pe.sig(ins)
                dve.wait(kv)
                last = dve.sig(dve.e.tensor_copy(st[:, CH:2 * CH], w.ap[:, 0:CH]))
                for n in range(2, NCH):
                    dve.wait(last)
                    last = dve.sig(dve.e.scalar_tensor_tensor(
                        st[:, n * CH:(n + 1) * CH], st[:, (n - 1) * CH:n * CH], cdec,
                        w.ap[:, (n - 1) * CH:n * CH], ALU.mult, ALU.add))
                w.free(last)
                table_slot.free(last, k_tok)
                w = self.next_wide()
                out = w.claim(pe)
                pe.wait(s_mask, q_dec, last)
                for n in range(NCH):
                    c = slice(n * CH, (n + 1) * CH)
                    ins = pe.e.matmul(out[:, c], vtok[:, c], sT[:, c], start=True, stop=(n == 0))
                    if n:
                        ins = pe.e.matmul(out[:, c], st[:, c], q[:, c], start=False, stop=True)
                o_done = pe.sig(ins)
                act.wait(o_done)
                sq = act.sig(act.e.activation(sT, w.ap, ACT.Square))
                dve.wait(sq)
                o = dve.sig(dve.e.tensor_scalar(k, w.ap, self.v("ret_norm_g", head), None, ALU.mult))
                w.free(sq, o)
                w, m = self.column_mean(self.c("mean128"), sT, sq)
                r = self.rsqrt_of(w, m, st, EPS)
                dve.wait(r, o)
                n1 = dve.sig(dve.e.tensor_tensor(k, k, st, ALU.mult))
                dve.wait(n1, g_silu)
                dve.sig(dve.e.tensor_tensor(y[:, head, :], k, gate, ALU.mult))

    def sgu(self, y):
        act, dve, pe, sp = self.act, self.dve, self.pe, self.sp
        with self.scope("sgu") as sb:
            names = ("u", "v", "t", "rstd", "vtok")
            u, v, t, rstd, vtok = (sb(n, [P, S])[:] for n in names)
            w_t = sb("w_t", [P, CH])
            b_s = sb("b_s", [P, CH])
            load = self.slot("sgu_load", None)
            self.line_for("sgu")
            with self.w_turns("sgu", SGU_GROUPS, 2) as g:
                load.claim(sp)
                self.fetch("sgu", w_t[:], self.t["sgu_w_t"][bass.ds(g, 1), :, :].rearrange("a s t -> (a s) t"))
                loaded = self.fetch("sgu", b_s[:], self.t["sgu_b_s"][bass.ds(g, 1), :].broadcast_to([P, CH]))
                acc, done = self.project()
                act.wait(done, dve.turn_before())
                a = act.sig(act.e.activation(u, acc.ap, ACT.Gelu))
                acc.free(a)
                acc, done = self.project()
                act.wait(done)
                gv = act.sig(act.e.activation(v, acc.ap, ACT.Gelu))
                acc.free(gv)
                w, m = self.column_mean(self.c("mean128"), v, gv)
                dve.wait(m)
                cent = dve.sig(dve.e.tensor_tensor(v, v, w.ap, ALU.subtract))
                w.free(cent)
                act.wait(cent)
                sq = act.sig(act.e.activation(t, v, ACT.Square))
                w, m = self.column_mean(self.c("mean128"), t, sq)
                r = self.rsqrt_of(w, m, rstd, EPS)
                dve.wait(r)
                n1 = dve.sig(dve.e.scalar_tensor_tensor(v, v, self.v("sgu_ln_g", g), rstd, ALU.mult, ALU.mult))
                act.wait(n1)
                vn = act.sig(act.e.activation(v, v, ACT.Identity, bias=self.v("sgu_ln_b", g)))
                w = self.next_wide()
                tr = self.transposes(w, v, vn)
                act.wait(tr)
                vt = act.sig(act.e.activation(vtok, w.ap, ACT.Copy))
                w.free(vt)
                dve.wait(loaded)
                wm = dve.sig(dve.e.tensor_tensor(w_t[:], w_t[:], self.c("tril_t"), ALU.mult))
                w = self.next_wide()
                out = w.claim(pe)
                pe.wait(vt, wm)
                for n in range(NCH):
                    c = slice(n * CH, (n + 1) * CH)
                    ins = pe.e.matmul(out[:, c], vtok[:, c], w_t[:], start=True, stop=True)
                mixed = pe.sig(ins)
                dve.wait(mixed)
                b = dve.sig(dve.e.tensor_tensor(
                    t.rearrange("p (n c) -> p n c", c=CH), w.ap.rearrange("p (n c) -> p n c", c=CH),
                    b_s[:].unsqueeze(1).broadcast_to([P, NCH, CH]), ALU.add))
                w.free(b)
                load.free(b)
                dve.wait(b, a)
                dve.sig(dve.e.tensor_tensor(y[:, g + RET_HEADS, :], t, u, ALU.mult))

    def second(self):
        self.h_ready = self.rms([self.x[:, k, :] for k in range(KD)], self.c("mean1024"), "ln_g_2", EPS,
                                self.h, "norm4")
        y = self.ctx_y("y2")
        self.conformer(y)
        self.neighbourhood(y)
        ready = [self.split(y[:, k, :], *self.h(k), self.dve_now()) for k in range(KD)]
        self.meet()
        self.close_y()
        self.mix_out("mix2", 1.0, ready)
        self.meet()
        self.rms([self.x[:, k, :] for k in range(KD)], self.c("mean1024"), "final_g_2", EPS, None, "norm5")

    def conformer(self, y):
        act, dve, pe, sp = self.act, self.dve, self.pe, self.sp
        with self.scope("conv") as sb:
            u = sb("u", [P, S + 2 * PAD])
            ga = self.slot("conv_ga", sb("ga", [P, S])[:])
            gb = self.slot("conv_gb", sb("gb", [P, S])[:])
            z1 = dve.sig(dve.e.memset(u[:, 0:PAD], 0.0))
            z2 = dve.sig(dve.e.memset(u[:, PAD + S:], 0.0))
            dve.wait(z1, z2)
            first = [self.h_ready]
            with self.w_turns("conv", CONV_TILES, 2) as i:
                acc, done = self.project(first[0])
                act.wait(done)
                a = act.sig(act.e.activation(ga.claim(act), acc.ap, ACT.Identity, bias=self.v("b_in_2", i)))
                acc.free(a)
                acc, done = self.project()
                act.wait(done)
                b = act.sig(act.e.activation(gb.claim(act), acc.ap, ACT.Sigmoid, bias=self.v("b_in_2", i + 4)))
                acc.free(b)
                dve.wait(a, b, dve.turn_before())
                last = dve.sig(dve.e.tensor_tensor(u[:, PAD:PAD + S], ga.ap, gb.ap, ALU.mult))
                ga.free(last)
                gb.free(last)
                dve.wait(last)
                out = y[:, i, :]
                last = dve.sig(dve.e.tensor_scalar(out, u[:, 0:S], self.v("dw_w_2", i * TAPS), self.v("dw_b_2", i),
                                                   ALU.mult, ALU.add))
                for j in range(1, TAPS):
                    dve.wait(last)
                    last = dve.sig(dve.e.scalar_tensor_tensor(out, u[:, j:j + S], self.v("dw_w_2", i * TAPS + j), out,
                                                              ALU.mult, ALU.add))
            with self.w_turns("conv_z", CONV_TILES // 2, 2) as i:
                for j in range(2):
                    acc, done = self.project()
                    act.wait(done)
                    acc.free(act.sig(act.e.activation(y[:, i * 2 + 4 + j, :], acc.ap, ACT.Silu,
                                                      bias=self.v("b_in_2", i * 2 + 8 + j))))
        with ExitStack() as ctx:
            c_hi = ctx.enter_context(self.nc.sbuf_tensor("pw_hi", [P, 4, S], F32R))
            c_lo = ctx.enter_context(self.nc.sbuf_tensor("pw_lo", [P, 4, S], F32R))
            ready = self.layer_norm([y[:, k, :] for k in range(4)], self.c("mean512"), "cln_g_2", "cln_b_2", EPS,
                                    "cln", lambda k: (c_hi[:, k, :], c_lo[:, k, :]), ACT.Silu)
            with self.scope("pw") as sb:
                t = [self.slot(f"pw_t{i}", sb(f"t{i}", [P, S])[:]) for i in range(2)]
                rstd = sb("rstd", [P, S])[:]
                for n in range(4):
                    if n % 2 == 0:
                        tile = self.next_tile()
                    acc = self.next_acc()
                    done = self.gemm(acc, tile, 4, 2 * P, (n % 2) * P,
                                     lambda k, part: (c_lo if part else c_hi)[:, k, :])
                    if n % 2:
                        tile.free(done)
                    act.wait(done)
                    out = y[:, n, :]
                    p = act.sig(act.e.activation(out, acc.ap, ACT.Identity, bias=self.v("pw_b_2", n)))
                    sq = act.sig(act.e.activation(t[0].claim(act), acc.ap, ACT.Square, bias=self.v("pw_b_2", n)))
                    acc.free(sq)
                    w, m = self.column_mean(self.c("mean64"), t[0].ap, sq)
                    t[0].free(m)
                    if n:
                        act.wait(g)
                    r = self.rsqrt_of(w, m, rstd, EPS)
                    dve.wait(r, p)
                    g = dve.sig(dve.e.scalar_tensor_tensor(out, out, self.v("gn_conv_g_2", n), rstd, ALU.mult, ALU.mult))
                    dve.wait(g)
                    g = dve.sig(dve.e.tensor_tensor(out, out, y[:, n + 4, :], ALU.mult))
                    dve.wait(g)

    def neighbourhood(self, y):
        act, dve, pe, sp = self.act, self.dve, self.pe, self.sp
        with self.scope("na") as sb:
            seen = sb("seen", [P, GRID_W])
            got_seen = self.fetch("seen", seen[:], self.t["seen"])
            self.copies_done("rel_copies")
            q2 = sb("q2", [P, ROWS, P])[:]
            k, t, gate = (sb(n, [P, S])[:] for n in ("k", "t", "gate"))
            vtok = sb("vtok", [P, 15, P])[:]
            bias = sb("bias", [P, REL_H, GRID_W])
            bias_slot = self.slot("na_bias", bias[:])
            self.line_for("na_bias")
            prob = [self.slot(f"na_prob{i}", sb(f"prob{i}", [P, HALF])[:]) for i in range(2)]
            prob_t = [self.slot(f"na_pt{i}", sb(f"pt{i}", [P, HALF])[:]) for i in range(2)]
            stat = [sb(f"stat{i}", [P, 4]) for i in range(2)]
            bq = sb("bq", [P, 4])
            at = VEC["b_in_2"] + 12
            dve.e.tensor_scalar(bq[:], self.vec[:, at:at + 4], SCALE, None, ALU.mult)
            z = dve.sig(dve.e.memset(q2, 0.0))
            act.wait(z)
            dve.wait(got_seen)
            score_bank = [self.bank[4], self.bank[5]]
            turn_bank, out_bank = self.bank[6], self.bank[7]
            with self.w_turns("na", NA_HEADS // 2, 4) as pair:
                bias_slot.claim(sp)
                for a in range(2):
                    one = self.t["rel_copies"][bass.ds(pair * 2 + a, 1), :]
                    src = bass.AP(tensor=one.tensor, offset=one.offset + GRID_W - 1,
                                  ap=[[REL_H * REL_PAD - 1, GRID_W], [REL_PAD, REL_H], [1, GRID_W]])
                    got_bias = self.fetch("na_bias", bias[64 * a:64 * a + 64, :, :], src)
                dve.wait(got_bias)
                b_in = lambda n: self.v("b_in_2", pair + n)
                before = [pe.turn_before(), dve.turn_before()]
                acc, done = self.project()
                act.wait(done, *before)
                for a in range(2):
                    c = slice(64 * a, 64 * a + 64)
                    tq = act.sig(act.e.activation(q2[c, :, c], acc.ap[c, :].rearrange("p (r w) -> p r w", w=GRID_W),
                                                  ACT.Identity, bias=bq[c, bass.ds(pair, 1)], scale=SCALE))
                acc.free(tq)
                acc, done = self.project()
                act.wait(done)
                tk = act.sig(act.e.activation(k, acc.ap, ACT.Identity, bias=b_in(16)))
                acc.free(tk)
                acc, done = self.project()
                act.wait(done)
                tv = act.sig(act.e.activation(t, acc.ap, ACT.Identity, bias=b_in(20)))
                acc.free(tv)
                acc, done = self.project()
                act.wait(done)
                tg = act.sig(act.e.activation(gate, acc.ap, ACT.Silu, bias=b_in(24)))
                acc.free(tg)
                masked = dve.sig(dve.e.tensor_tensor(
                    bias[:], bias[:], seen[:].unsqueeze(1).broadcast_to([P, REL_H, GRID_W]), ALU.add))
                dve.wait(masked)
                for part, n in ((0, 8), (1, 7)):
                    w = self.next_acc()
                    tr = self.transposes(w, t, tv, n=n, step=64, first=8 * part)
                    act.wait(tr)
                    v_tok = act.sig(act.e.activation(vtok[:, 8 * part:8 * part + n, :].rearrange("p a b -> p (a b)"),
                                                     w.ap[:, 0:n * P], ACT.Copy))
                    w.free(v_tok)
                out_y = y[:, pair + 4, :]
                key_row = lambda r: min(max(r - KH // 2, 0), ROWS - KH)
                normed, turned = {}, {}
                for step in range(ROWS + 2):
                    r = step
                    if r < ROWS:
                        ks = key_row(r)
                        b = score_bank[r % 2]
                        out = b.claim(pe)
                        pe.wait(tq, tk)
                        s_done = pe.sig(pe.e.matmul(out, q2[:, r, :], k[:, ks * GRID_W:(ks + KH) * GRID_W],
                                                    start=True, stop=True))
                        pr, st = prob[r % 2], stat[r % 2]
                        dve.wait(s_done)
                        p = pr.claim(dve)
                        rel = ks - r + KH - 1
                        dve.e.memset(st[:, 2:3], 0.0)
                        mx = dve.sig(dve.e.tensor_tensor_reduce(
                            p, out, bias[:, rel:rel + KH, :].rearrange("p a b -> p (a b)"), 1.0, 3 * MASKED,
                            ALU.add, ALU.max, st[:, 0:1]))
                        b.free(mx)
                        if r == ROWS - 1:
                            bias_slot.free(mx)
                        dve.wait(mx)
                        nm = dve.sig(dve.e.tensor_scalar(st[:, 1:2], st[:, 0:1], -1.0, None, ALU.mult))
                        act.wait(nm)
                        ex = act.sig(act.e.activation(p, p, ACT.Exp, bias=st[:, 1:2], accum_out=st[:, 2:3]))
                        dve.wait(ex)
                        rc = dve.sig(dve.e.reciprocal(st[:, 3:4], st[:, 2:3]))
                        dve.wait(rc)
                        normed[r] = dve.sig(dve.e.tensor_scalar(p, p, st[:, 3:4], None, ALU.mult))
                    r = step - 1
                    if 0 <= r < ROWS:
                        out = turn_bank.claim(pe)
                        pe.wait(normed[r])
                        for b in range(4):
                            ins = pe.e.transpose(out[:, b * P:(b + 1) * P], prob[r % 2].ap[:, b * P:(b + 1) * P],
                                                 self.c("ident"))
                        tr = pe.sig(ins)
                        prob[r % 2].free(tr)
                        act.wait(tr)
                        turned[r] = act.sig(act.e.activation(prob_t[r % 2].claim(act), out, ACT.Copy))
                        turn_bank.free(turned[r])
                    r = step - 2
                    if 0 <= r < ROWS:
                        ks = key_row(r)
                        if r % 4 == 0:
                            o = out_bank.claim(pe)
                        pe.wait(turned[r], v_tok)
                        for b in range(4):
                            ins = pe.e.matmul(o[:, (r % 4) * P:(r % 4 + 1) * P], vtok[:, ks + 2 * b, :],
                                              prob_t[r % 2].ap[:, b * P:(b + 1) * P], start=(b == 0), stop=(b == 3))
                        pv = pe.sig(ins)
                        prob_t[r % 2].free(pv)
                        if r % 4 == 3:
                            act.wait(pv)
                            for a in range(2):
                                c = slice(64 * a, 64 * a + 64)
                                dst = t[c, (r - 3) * 64:(r + 1) * 64].rearrange("p (r w) -> p r w", w=64)
                                src = o[c, :].rearrange("p (r q) -> p r q", q=P)[:, :, c]
                                last = act.sig(act.e.activation(dst, src, ACT.Copy))
                            out_bank.free(last)
                act.wait(last)
                sq = act.sig(act.e.activation(k, t, ACT.Square))
                acc, m = self.column_mean(self.c("mean64"), k, sq, self.next_acc())
                r_ = self.rsqrt_of(acc, m, k, EPS)
                self.next_acc()
                dve.wait(r_, last)
                n1 = dve.sig(dve.e.scalar_tensor_tensor(t, t, self.v("gn_att_g_2", pair), k, ALU.mult, ALU.mult))
                dve.wait(n1, tg)
                dve.sig(dve.e.tensor_tensor(out_y, t, gate, ALU.mult))

    def third(self):
        x = [self.x[:, k, :] for k in range(KD)]
        mean = self.c("mean1024")
        self.h_ready = self.layer_norm(x, mean, "ln_in_g_3", "ln_in_b_3", LN_EPS, "ln1", self.h)
        y = self.ctx_y("y3")
        self.attention_pairs(y)
        ready = self.rms([y[:, k, :] for k in range(4)], self.c("mean512"), "sb_norm_g_3", EPS, self.h, "norm6")
        ready += self.rms([y[:, k + 4, :] for k in range(4)], self.c("mean512"), "swa_norm_g_3", EPS,
                          lambda k: self.h(k + 4), "norm7")
        self.close_y()
        self.mix_out("mix3", ALPHA, ready)
        self.meet()
        self.h_ready = self.layer_norm(x, mean, "ln1_g_3", "ln1_b_3", LN_EPS, "ln2", self.h)
        scaled = [self.dve.sig(self.dve.e.tensor_scalar(a, a, ALPHA, None, ALU.mult)) for a in x]
        self.dve.wait(scaled[-1])
        self.mlp("mlp3", False)
        self.layer_norm(x, mean, "ln2_g_3", "ln2_b_3", LN_EPS, "ln3")

    def attention_pairs(self, y):
        act, dve, pe, sp = self.act, self.dve, self.pe, self.sp
        with ExitStack() as ctx:
            k2 = ctx.enter_context(self.nc.sbuf_tensor("swa_k2", [P, 2, S], F32))
            v2 = ctx.enter_context(self.nc.sbuf_tensor("swa_v2", [P, NCH, 2, 64], F32))
            with self.scope("kv") as sb:
                t = sb("t", [P, S])[:]
                acc, done = self.project(self.h_ready)
                act.wait(done)
                for g in range(2):
                    for a in range(2):
                        last = act.sig(act.e.activation(k2[64 * a:64 * a + 64, g, :], acc.ap[64 * g:64 * g + 64, :], ACT.Copy))
                acc.free(last)
                acc, done = self.project()
                act.wait(done)
                tv = act.sig(act.e.activation(t, acc.ap, ACT.Copy))
                acc.free(tv)
                w = self.next_wide()
                tr = self.transposes(w, t, tv)
                self.next_wide()
                act.wait(tr)
                last = act.sig(act.e.activation(v2[:].rearrange("p n g d -> p (n g d)"), w.ap, ACT.Copy))
                w.free(last)
            self.stick_breaking(y)
            self.sliding_window(y, k2, v2)

    def stick_breaking(self, y):
        act, dve, pe, sp = self.act, self.dve, self.pe, self.sp
        SOFT, SUM, OUT = 2, 3, 5
        with self.scope("sb") as sb:
            q, k, vtok = (sb(n, [P, S])[:] for n in ("q", "k", "vtok"))
            ring = lambda name, n: (lambda a: [self.slot(f"sb_{name}{i}", a[:, i, :]) for i in range(n)])(
                sb(name, [P, n, HALF]))
            mag_all = sb("mag", [P, 4, HALF])
            mag = [self.slot(f"sb_mag{i}", mag_all[:, i, :]) for i in range(4)]
            v_raw = mag_all[:, 0:2, :].rearrange("p a n -> p (a n)")
            soft, prob, carry = ring("soft", 3), ring("prob", 3), ring("carry", 2)
            tiles = []
            for qh in range(2):
                for kb in range(4 * qh + 3, -1, -1):
                    for hh in range(2):
                        q0 = max(kb * CH, qh * HALF)
                        tiles.append((hh, qh, kb, q0 - qh * HALF))
            act.e.preload_act_table_set("natural_log_exp_and_others")
            with self.w_turns("sb", 4, 4) as pair:
                before = [pe.turn_before()]
                acc, done = self.project()
                act.wait(done, *before)
                tq = act.sig(act.e.activation(q, acc.ap, ACT.Copy, scale=SCALE))
                acc.free(tq)
                acc, done = self.project()
                act.wait(done)
                tk = act.sig(act.e.activation(k, acc.ap, ACT.Copy))
                acc.free(tk)
                acc, done = self.project()
                act.wait(done)
                mag[0].claim(act)
                mag[1].claim(act)
                tv = act.sig(act.e.activation(v_raw, acc.ap, ACT.Copy))
                acc.free(tv)
                acc, done = self.project()
                act.wait(done)
                acc.free(act.sig(act.e.activation(y[:, pair + 4, :], acc.ap, ACT.Copy)))
                w = self.next_acc()
                tr = self.transposes(w, v_raw, tv)
                mag[0].free(tr)
                mag[1].free(tr)
                act.wait(tr)
                v_tok = act.sig(act.e.activation(vtok, w.ap, ACT.Copy))
                w.free(v_tok)
                oslot = self.next_acc()
                o = oslot.claim(pe)
                pe.wait(tq, tk, v_tok)
                banks = [self.bank[b] for b in (4, 5, 6, 7, 0, 1)]
                score, softened, logit, weight, carried = {}, {}, {}, {}, {}
                for step in range(len(tiles) + OUT):
                    i = step
                    if i < len(tiles):
                        hh, qh, kb, c0 = tiles[i]
                        hp = slice(64 * hh, 64 * hh + 64)
                        c = slice(c0, HALF)
                        z = banks[i % 6].claim(pe)
                        z_done = pe.sig(pe.e.matmul(z[:, c], k[hp, kb * CH:(kb + 1) * CH],
                                                    q[hp, qh * HALF + c0:(qh + 1) * HALF],
                                                    start=True, stop=False, skip_group_check=True))
                        dve.wait(z_done)
                        m = mag[i % 4].claim(dve)
                        low = dve.sig(dve.e.tensor_scalar(m[:, c], z[:, c], LN_TOP, None, ALU.min))
                        act.wait(low)
                        ex = act.sig(act.e.activation(m[:, c], m[:, c], ACT.Exp))
                        act.wait(ex)
                        score[i] = act.sig(act.e.activation(m[:, c], m[:, c], ACT.Ln, bias=1.0))
                    i = step - SOFT
                    if 0 <= i < len(tiles):
                        hh, qh, kb, c0 = tiles[i]
                        c, d = slice(c0, HALF), slice(c0, c0 + CH)
                        diag = kb >= 4 * qh
                        z, mg, sf = banks[i % 6].ap, mag[i % 4], soft[i % 3]
                        dve.wait(score[i])
                        s = sf.claim(dve)
                        t = dve.sig(dve.e.tensor_tensor(s[:, c], mg.ap[:, c], z[:, c], ALU.max))
                        mg.free(t)
                        if diag:
                            dve.wait(t)
                            t = dve.sig(dve.e.tensor_tensor(s[:, d], s[:, d], self.c("after"), ALU.mult))
                        softened[i] = t
                    i = step - SUM
                    if 0 <= i < len(tiles):
                        hh, qh, kb, c0 = tiles[i]
                        c, d = slice(c0, HALF), slice(c0, c0 + CH)
                        diag = kb >= 4 * qh
                        z, sf, cr = banks[i % 6].ap, soft[i % 3], carry[hh]
                        s = sf.ap
                        later = slice(c0 + CH if diag else 0, HALF)
                        first = kb == 4 * qh + 3
                        pe.wait(softened[i])
                        ins = pe.e.matmul(z[:, c], self.c("neg_tri"), s[:, c], start=False, stop=False,
                                          skip_group_check=True)
                        if diag:
                            ins = pe.e.matmul(z[:, d], self.c("ident"), self.c("bar_after"), start=False,
                                              stop=first, skip_group_check=True)
                        if not first:
                            pe.wait(*carried[hh])
                            ins = pe.e.matmul(z[:, later], self.c("neg_ones"), cr.ap[:, later], start=False,
                                              stop=True, skip_group_check=True)
                        logit[i] = pe.sig(ins)
                        cr.free(logit[i])
                        if kb > 0:
                            cr.claim(dve)
                            dve.wait(softened[i])
                            new = []
                            if diag:
                                new.append(dve.sig(dve.e.tensor_copy(cr.ap[:, d], s[:, d])))
                            if not first:
                                dve.wait(*carried[hh])
                                new.append(dve.sig(dve.e.tensor_tensor(cr.ap[:, later], cr.ap[:, later],
                                                                       s[:, later], ALU.add)))
                            carried[hh] = new
                            sf.free(logit[i], new[-1])
                        else:
                            sf.free(logit[i])
                        act.wait(logit[i])
                        weight[i] = act.sig(act.e.activation(prob[i % 3].claim(act)[:, c], z[:, c], ACT.Exp))
                        banks[i % 6].free(weight[i])
                    i = step - OUT
                    if 0 <= i < len(tiles):
                        hh, qh, kb, c0 = tiles[i]
                        hp = slice(64 * hh, 64 * hh + 64)
                        pe.wait(weight[i])
                        ins = pe.e.matmul(o[hp, qh * HALF + c0:(qh + 1) * HALF],
                                          vtok[:, kb * CH + 64 * hh:kb * CH + 64 * hh + 64], prob[i % 3].ap[:, c0:HALF],
                                          start=(kb == 4 * qh + 3), stop=(kb == 0), skip_group_check=True)
                        o_done = pe.sig(ins)
                        prob[i % 3].free(o_done)
                w.free(weight[len(tiles) - 1])
                act.wait(o_done)
                oslot.free(act.sig(act.e.activation(y[:, pair, :], o, ACT.Copy)))

    def sliding_window(self, y, k2, v2):
        act, dve, pe, sp = self.act, self.dve, self.pe, self.sp
        with self.scope("swa") as sb:
            sinks = sb("sinks", [P, SWA_HEADS])
            dve.wait(self.fetch("sinks", sinks[:], self.t["sinks"].broadcast_to([P, SWA_HEADS])))
            self.copies_done("band_copies")
            q2 = sb("q2", [P, 2, S])[:]
            kg = sb("kg", [P, S])[:]
            vg = sb("vg", [P, NCH, P])[:]
            sink = sb("sink", [P, 2])
            bias = sb("bias", [P, 2, BAND])
            bias_slot = self.slot("swa_bias", bias[:])
            self.line_for("swa_bias")
            prob = [self.slot(f"swa_p{i}", sb(f"p{i}", [P, 2, BAND])[:]) for i in range(2)]
            prob_t = [self.slot(f"swa_pt{i}", sb(f"pt{i}", [P, 2, 2, CH])[:]) for i in range(2)]
            stat = [sb(f"stat{i}", [P, 6, 2]) for i in range(2)]
            z = dve.sig(dve.e.memset(q2, 0.0))
            dve.wait(z)
            with self.repeat("swa", SWA_HEADS // 2) as pair:
                bias_slot.claim(sp)
                one = self.t["band_copies"][bass.ds(pair * 2, 1), :]
                src = bass.AP(tensor=one.tensor, offset=one.offset + CH - 1,
                              ap=[[REL_BAND - 1, CH], [CH * REL_BAND, 2], [1, BAND]])
                got_bias = self.fetch("swa_bias", bias[:], src)
                dve.wait(pe.turn_before(), act.turn_before())
                act.wait(pe.turn_before())
                for a in range(2):
                    c = slice(64 * a, 64 * a + 64)
                    dve.e.tensor_scalar(q2[c, a, :], y[c, pair + 4, :], SCALE, None, ALU.mult)
                dve.e.tensor_copy(sink[:], sinks[:, bass.ds(pair * 2, 2)])
                act_staged = act.sig(act.e.activation(kg, k2[:, pair // 2, :], ACT.Copy))
                for a in range(2):
                    staged = dve.sig(dve.e.tensor_copy(vg[:, :, 64 * a:64 * a + 64], v2[:, :, pair // 2, :]))
                dve.wait(staged)
                normed, turned = {}, {}
                for step in range(NCH + 2):
                    n = step
                    if n < NCH:
                        lo = 0 if n else CH
                        sbk = self.bank[4 + n % 2]
                        out = sbk.claim(pe).rearrange("p (a c) -> p a c", a=2)
                        pe.wait(staged, act_staged)
                        for a in range(2):
                            ins = pe.e.matmul(out[:, a, lo:], q2[:, a, n * CH:(n + 1) * CH],
                                              kg[:, (n - 1) * CH + lo:(n + 1) * CH], start=True, stop=True)
                        s_done = pe.sig(ins)
                        pr, st = prob[n % 2], stat[n % 2]
                        dve.wait(s_done, got_bias)
                        p = pr.claim(dve)
                        dve.e.memset(st[:, 3, :], 0.0)
                        for a in range(2):
                            m = dve.sig(dve.e.tensor_tensor_reduce(
                                p[:, a, lo:], out[:, a, lo:], bias[:, a, lo:], 1.0, sink[:, a:a + 1],
                                ALU.add, ALU.max, st[:, 0, a:a + 1]))
                        sbk.free(m)
                        if n == NCH - 1:
                            bias_slot.free(m)
                        dve.wait(m)
                        dve.sig(dve.e.tensor_scalar(st[:, 1, :], st[:, 0, :], -1.0, None, ALU.mult))
                        d = dve.sig(dve.e.tensor_tensor(st[:, 2, :], sink[:], st[:, 0, :], ALU.subtract))
                        act.wait(d)
                        for a in range(2):
                            act.sig(act.e.activation(p[:, a, lo:], p[:, a, lo:], ACT.Exp, bias=st[:, 1, a:a + 1],
                                                     accum_out=st[:, 3, a:a + 1]))
                        ex = act.sig(act.e.activation(st[:, 4, :], st[:, 2, :], ACT.Exp))
                        dve.wait(ex)
                        dn = dve.sig(dve.e.tensor_tensor(st[:, 5, :], st[:, 3, :], st[:, 4, :], ALU.add))
                        dve.wait(dn)
                        dn = dve.sig(dve.e.reciprocal(st[:, 5, :], st[:, 5, :]))
                        dve.wait(dn)
                        for a in range(2):
                            normed[n] = dve.sig(dve.e.tensor_scalar(p[:, a, lo:], p[:, a, lo:], st[:, 5, a:a + 1], None,
                                                                    ALU.mult))
                    n = step - 1
                    if 0 <= n < NCH:
                        tb = self.bank[6]
                        out = tb.claim(pe).rearrange("p (k a q) -> p k a q", k=2, a=2)
                        pe.wait(normed[n])
                        ks = range(2) if n else range(1, 2)
                        for kb in ks:
                            for a in range(2):
                                ins = pe.e.transpose(out[:, kb, a, :], prob[n % 2].ap[:, a, kb * CH:(kb + 1) * CH],
                                                     self.c("ident"))
                        tr = pe.sig(ins)
                        prob[n % 2].free(tr)
                        act.wait(tr)
                        dst = prob_t[n % 2].claim(act)
                        turned[n] = act.sig(act.e.activation(dst[:, ks[0]:, :, :], out[:, ks[0]:, :, :], ACT.Copy))
                        tb.free(turned[n])
                    n = step - 2
                    if 0 <= n < NCH:
                        ob = self.bank[7]
                        out = ob.claim(pe)
                        pe.wait(turned[n])
                        ks = range(2) if n else range(1, 2)
                        for kb in ks:
                            ins = pe.e.matmul(out[:, 0:2 * CH], vg[:, n - 1 + kb, :],
                                              prob_t[n % 2].ap[:, kb, :, :].rearrange("p a q -> p (a q)"),
                                              start=(kb == ks[0]), stop=(kb == 1))
                        pv = pe.sig(ins)
                        prob_t[n % 2].free(pv)
                        act.wait(pv)
                        for a in range(2):
                            c = slice(64 * a, 64 * a + 64)
                            last = act.sig(act.e.activation(y[c, pair + 4, n * CH:(n + 1) * CH],
                                                            out[c, a * CH:(a + 1) * CH], ACT.Copy))
                        ob.free(last)

    def finish(self):
        sp = self.sp
        self.meet()
        out = self.out_line.sig(sp.e.dma_start(self.t["out"].rearrange("(c p) s -> p c s", p=P), self.x[:]))
        sp.wait(out)
        for loaded in self.w_loaded:
            loaded.follow(sp)


BLOCKS = (1, 2, 3)


def program(nc, tensors, blocks, counts, last_turn):
    with ExitStack() as ctx:
        b = Blocks(nc, ctx, counts, last_turn)
        b.setup(tensors, blocks)
        for n in blocks:
            (b.first, b.second, b.third)[n - 1]()
        b.finish()
        return b


def k_tiles(w):
    k, n = w.shape
    return w.reshape(k // P, P, n // P, P).transpose(2, 1, 0, 3).reshape(n // P, P, KD * P)


def down_tiles(w):
    return w.reshape(NGROUP, 2, P, 2, 4 * P).transpose(0, 3, 2, 1, 4).reshape(2 * NGROUP, P, KD * P)


def mlp_order(up, down):
    a, b = up[:DFF // P], up[DFF // P:]
    out = [a[0], b[0], a[1], b[1]]
    for g in range(1, NGROUP):
        out += [a[2 * g], down[2 * g - 2], down[2 * g - 1], b[2 * g], a[2 * g + 1], b[2 * g + 1]]
    return out + [down[-2], down[-1]]


def weight_stream(i, blocks):
    tiles = []
    if 1 in blocks:
        w = k_tiles(i["w_in"][0])
        for h in range(4):
            tiles += [w[h], w[4 + h], w[8 + h], w[12 + h]]
        for g in range(4):
            tiles += [w[16 + g], w[20 + g]]
        tiles += list(k_tiles(i["w_out"][0]))
        tiles += mlp_order(k_tiles(i["w_up"][0]), down_tiles(i["w_down"][0]))
    if 2 in blocks:
        w = k_tiles(i["w_in_2"][0])
        for c in range(4):
            tiles += [w[c], w[4 + c]]
        tiles += list(w[8:12])
        tiles += list(i["pw_w_2"][0].reshape(4, P, 2, 2 * P).transpose(2, 1, 0, 3).reshape(2, P, KD * P))
        for p in range(4):
            tiles += [w[12 + p], w[16 + p], w[20 + p], w[24 + p]]
        tiles += list(k_tiles(i["w_out_2"][0]))
    if 3 in blocks:
        w = k_tiles(i["w_in_3"][0])
        tiles += [w[16], w[17]]
        for p in range(4):
            tiles += [w[p], w[4 + p], w[8 + p], w[12 + p]]
        tiles += list(k_tiles(i["w_out_3"][0]))
        tiles += mlp_order(k_tiles(i["w_gate_up_3"][0]), down_tiles(i["w_down_3"][0]))
    tiles += [np.zeros((P, KD * P), np.float32)] * 2
    return np.stack(tiles)


def columns(a):
    return np.asarray(a).reshape(-1, P).T


def kernel(**inputs):
    import concourse.bacc as bacc
    from concourse.bass_utils import run_bass_kernel_spmd as run

    i = {k: np.asarray(v) for k, v in inputs.items()}
    vec = {"conv_w0": columns(i["conv_w"][0, 0]), "conv_w1": columns(i["conv_w"][0, 1]),
           "conv_w2": columns(i["conv_w"][0, 2]),
           "dw_w_2": i["dw_w_2"][0].reshape(TAPS, 4, P).transpose(2, 1, 0).reshape(P, 4 * TAPS)}
    arrays = {
        "x_t": i["x"][0].T,
        "vectors": np.concatenate([vec[n] if n in vec else columns(i[n]) for n in VEC], axis=1),
        "common": COMMON,
        "rotary": TABLES["rotary"],
        "retention": TABLES["retention"],
        "seen": TABLES["seen"],
        "onehot": TABLES["onehot"],
        "outside": TABLES["outside"],
        "sgu_w_t": i["sgu_w_s"][0].transpose(0, 2, 1),
        "sgu_b_s": i["sgu_b_s"][0],
        "rpb": i["rpb_2"][0].reshape(NA_HEADS * REL_H, REL_W),
        "sinks": i["sinks_3"],
        "rel_bias": i["rel_bias_3"],
        "weights": weight_stream(i, BLOCKS),
    }
    arrays = {f"in_{k}": np.ascontiguousarray(v) for k, v in arrays.items()}

    def build(counts, last_turn):
        nc = bacc.Bacc("TRN2", target_bir_lowering=False, num_devices=1)
        t = {k[3:]: nc.dram_tensor(k, v.shape, F32, kind="ExternalInput").ap() for k, v in arrays.items()}
        t["out"] = nc.dram_tensor("out_t", (D, S), F32, kind="ExternalOutput").ap()
        for name, shape in (("rel_rows", (NA_HEADS * REL_H, REL_PAD)), ("band_rows", (SWA_HEADS, REL_BAND)),
                            ("rel_copies", (NA_HEADS, GRID_W * REL_H * REL_PAD)),
                            ("band_copies", (SWA_HEADS, CH * REL_BAND))):
            t[name] = nc.dram_tensor(name, shape, F32, kind="Internal").ap()
        return nc, program(nc, t, BLOCKS, counts, last_turn)

    _, dry = build({}, {})
    nc, _ = build(dry.found_counts, dry.found_last)
    r = run(nc, [arrays], core_ids=[0])
    return np.ascontiguousarray(r.results[0]["out_t"].T)[None]
```

```python
from contextlib import ExitStack, contextmanager

import concourse.bass as bass
from concourse import mybir
import numpy as np

ALU = mybir.AluOpType
ACT = mybir.ActivationFunctionType
F32 = mybir.dt.float32
F32R = mybir.dt.float32r
AX_X = mybir.AxisListType.X

P = 128
S = 1024
D = 1024
KD = D // P
HALF = 512
CH = 128
NCH = S // CH
DFF = 2816
NGROUP = DFF // (2 * P)
MASKED = -1e30
SCALE = 64 ** -0.5
EPS = 1e-6
LN_EPS = 1e-5
ALPHA = 2.0 ** 0.25

RET_HEADS = 4
SGU_GROUPS = 4
CONV_TILES = 4
TAPS = 31
PAD = TAPS // 2
GRID_W = 64
ROWS = S // GRID_W
KH = 8
KW = 16
NA_HEADS = 8
REL_H = 2 * KH - 1
REL_W = 2 * KW - 1
REL_PAD = 2 * GRID_W
SWA_HEADS = 8
BUCKETS = 32
LN_TOP = 40.0
BAND = 2 * CH
REL_BAND = 384

VEC = {}


def _lay_vectors():
    at = 0
    for name, n in (("mix_norm_g", 8), ("ret_norm_g", 4), ("sgu_ln_g", 4), ("sgu_ln_b", 4),
                    ("ffn_norm_g", 8), ("conv_w0", 44), ("conv_w1", 44), ("conv_w2", 44), ("conv_b", 44),
                    ("final_norm_g", 8), ("ln_g_2", 8), ("b_in_2", 28), ("dw_w_2", 4 * TAPS), ("dw_b_2", 4),
                    ("cln_g_2", 4), ("cln_b_2", 4), ("pw_b_2", 4), ("gn_conv_g_2", 4), ("gn_att_g_2", 4),
                    ("final_g_2", 8), ("ln_in_g_3", 8), ("ln_in_b_3", 8), ("sb_norm_g_3", 4),
                    ("swa_norm_g_3", 4), ("ln1_g_3", 8), ("ln1_b_3", 8), ("ln2_g_3", 8), ("ln2_b_3", 8)):
        VEC[name] = at
        at += n
    return at


NVEC = _lay_vectors()

CONST_COLS = {}


def shape_constants():
    f = np.float32
    i = np.arange(P)
    parts = [
        ("ident", np.eye(P)),
        ("mean1024", np.full((P, P), 1 / 1024)),
        ("mean512", np.full((P, P), 1 / 512)),
        ("mean128", np.full((P, P), 1 / 128)),
        ("mean64", (i[:, None] // 64 == i[None, :] // 64) / 64),
        ("neg_tri", -(i[:, None] >= i[None, :]).astype(f)),
        ("neg_ones", np.full((P, P), -1.0)),
        ("after", (i[:, None] < i[None, :])),
        ("bar_after", np.where(i[:, None] < i[None, :], 0, MASKED)),
        ("tril_t", (i[:, None] <= i[None, :])),
        (f"eps{EPS}", np.full((P, 1), EPS)),
        (f"eps{LN_EPS}", np.full((P, 1), LN_EPS)),
    ]
    at = 0
    for name, a in parts:
        CONST_COLS[name] = at
        at += a.shape[1]
    common = np.concatenate([np.asarray(a, f) for _, a in parts], axis=1)

    half = P // 2
    inv = np.power(f(10000.0), -np.arange(half, dtype=f) / f(half)).astype(f)
    ang = (np.arange(S, dtype=f)[None, :] * inv[:, None]).astype(f)
    rotary = np.stack([np.concatenate([np.cos(ang)] * 2), np.concatenate([np.sin(ang), -np.sin(ang)])], 1)

    pos = np.arange(CH, dtype=np.float64)
    ret = []
    for h in range(RET_HEADS):
        lg = np.log(1.0 - 2.0 ** (-5.0 - h))
        diff = pos[None, :] - pos[:, None]
        scale = P ** -0.5
        mask = np.where(diff >= 0, np.exp(lg * np.maximum(diff, 0)), 0) * scale
        qd = np.broadcast_to(np.exp(lg * (pos + 1))[None, :], (P, CH))
        kd = (np.exp(lg * (CH - 1 - pos)) * scale)[:, None]
        ret.append(np.concatenate([mask, qd, kd, np.full((P, 1), np.exp(lg * CH))], 1))

    w = np.arange(GRID_W)
    start = np.clip(w - KW // 2, 0, GRID_W - KW)
    seen = (w[None, :] >= start[:, None]) & (w[None, :] < start[:, None] + KW)
    cols = np.tile(np.where(seen, 0, MASKED), (2, 1))

    j = np.arange(REL_BAND)
    dist = 255 - j
    exact = BUCKETS // 2
    d = np.maximum(dist, 0)
    large = exact + (np.log(np.maximum(d, 1).astype(f) / exact) / f(np.log(128 / exact)) * exact).astype(np.int32)
    bucket = np.where(d < exact, d, np.minimum(large, BUCKETS - 1))
    inside = (dist >= 0) & (dist < CH)
    onehot = ((np.arange(BUCKETS)[:, None] == bucket[None, :]) & inside[None, :])
    outside = np.broadcast_to(np.where(inside, 0, MASKED)[None, :], (SWA_HEADS, REL_BAND))
    tables = {"rotary": rotary, "retention": np.stack(ret), "seen": cols, "onehot": onehot, "outside": outside}
    return common, {k: np.ascontiguousarray(v, dtype=f) for k, v in tables.items()}


COMMON, TABLES = shape_constants()


class Token:
    def __init__(self, line, count, loop, shift=0):
        self.line, self.count, self.loop, self.shift = line, count, loop, shift


class Line:

    def __init__(self, prog, sem, step=1):
        self.prog, self.sem, self.step, self.count = prog, sem, step, 0
        prog.lines.append(self)
        prog.line_of[sem.name] = self

    def sig(self, ins):
        ins.then_inc(self.sem, self.step)
        self.count += self.step
        return Token(self, self.count, self.prog.loop)


class Loop:
    def __init__(self, name, n, index, starts, per):
        self.name, self.n, self.index, self.starts, self.per, self.open = name, n, index, starts, per, True


class Held:

    def __init__(self, prog, name):
        self.prog, self.name, self.tokens, self.loop = prog, name, [], None
        prog.held.append(self)

    def set(self, *tokens):
        self.tokens, self.loop = list(tokens), self.prog.loop

    def follow(self, *engines):
        loop = self.prog.loop
        for eng in engines:
            eng.wait(*self.tokens)
            if loop is not None and self.loop is not loop:
                for sem, back in self.prog.last_turn.get((loop.name, self.name), []):
                    line = self.prog.line_of[sem]
                    eng.wait(Token(line, loop.starts[line] + back, loop, shift=-1))


class Slot(Held):

    def __init__(self, prog, name, ap):
        super().__init__(prog, name)
        self.ap = ap

    def claim(self, eng):
        self.follow(eng)
        self.set()
        return self.ap

    def free(self, *tokens):
        self.set(*self.tokens, *tokens)


class Engine:

    def __init__(self, prog, eng, sem):
        self.prog, self.e, self.line, self.seen = prog, eng, Line(prog, sem), {}

    def sig(self, ins):
        return self.line.sig(ins)

    def wait(self, *tokens):
        for t in tokens:
            loop = t.loop
            if loop is not None and loop.open:
                per = loop.per.get(t.line.sem.name, 0)
                base = t.count + t.shift * per
                key = (t.line, loop, t.shift)
                if self.seen.get(key, -1) >= t.count:
                    continue
                self.seen[key] = t.count
                if per == 0:
                    self.e.wait_ge(t.line.sem, max(base, 1))
                else:
                    assert base >= 1, (loop.name, t.line.sem.name, base)
                    self.e.wait_ge(t.line.sem, loop.index * per + base)
            else:
                value = t.count
                if loop is not None:
                    value += (loop.n - 1) * loop.per.get(t.line.sem.name, 0)
                if self.seen.get(t.line, 0) >= value:
                    continue
                self.seen[t.line] = value
                self.e.wait_ge(t.line.sem, value)

    def turn_before(self):
        loop = self.prog.loop
        return Token(self.line, loop.starts[self.line], loop)


class Program:
    BUMP = 1024

    def __init__(self, nc, ctx, counts, last_turn):
        self.nc, self.ctx, self.counts, self.last_turn = nc, ctx, counts, last_turn
        self.lines, self.line_of, self.held, self.loop = [], {}, [], None
        self.found_counts, self.found_last = {}, {}
        self.pe, self.act, self.dve, self.pool, self.sp = (
            Engine(self, e, self.sem(n)) for e, n in (
                (nc.tensor, "pe_done"), (nc.scalar, "act_done"), (nc.vector, "dve_done"),
                (nc.gpsimd, "pool_done"), (nc.sync, "sp_done")))
        for eng in (self.pe, self.act, self.dve, self.pool):
            eng.e.sem_inc(eng.line.sem, self.BUMP)
            eng.line.count = self.BUMP

    def sem(self, name):
        return self.ctx.enter_context(self.nc.semaphore(name))

    def dma_line(self, name):
        line = Line(self, self.sem(name), 16)
        self.nc.sync.sem_inc(line.sem, self.BUMP)
        line.count = self.BUMP
        return line

    def slot(self, name, ap):
        return Slot(self, name, ap)

    @contextmanager
    def repeat(self, name, n):
        starts = {x: x.count for x in self.lines}
        with self.nc.Fori(0, n) as index:
            self.loop = Loop(name, n, index, starts, self.counts.get(name, {}))
            loop = self.loop
            yield index
            self.loop = None
        per = {x.sem.name: x.count - starts[x] for x in self.lines}
        assert not self.counts or per == self.counts[name], name
        self.found_counts[name] = per
        loop.per, loop.open = per, False
        for s in self.held:
            mine = [t for t in s.tokens if t.loop is loop]
            if mine:
                self.found_last[(name, s.name)] = [(t.line.sem.name, t.count - starts[t.line]) for t in mine]
        for x in self.lines:
            x.count = starts[x] + n * per[x.sem.name]
        for eng in (self.pe, self.act, self.dve, self.pool, self.sp):
            eng.seen = {}

    def meet(self):
        self.nc.all_engine_barrier()


class Norm:

    def __init__(self, prog, ctx, name, ones, eps, n, centred):
        self.b, self.name, self.ones, self.eps, self.n, self.centred = prog, name, prog.c(ones), eps, n, centred
        sb = lambda x: ctx.enter_context(prog.nc.sbuf_tensor(f"{name}_{x}", [P, S], F32))
        self.acc = sb("acc")[:]
        self.rstd = sb("rstd")[:]
        self.buf = [prog.slot(f"{name}_buf{i}", sb(f"buf{i}")[:]) for i in range(2)]
        self.k, self.mean, self.last = 0, None, Held(prog, f"{name}_last")

    def gather(self, tile, token, on_pe=False):
        if self.centred:
            if on_pe:
                self.sum_on_pe(tile, token)
            else:
                self.sum_on_dve(tile, token, self.k == 0)
        else:
            self.square(tile, token, on_pe)
        self.k += 1

    def square(self, tile, token, on_pe):
        act = self.b.act
        act.wait(token)
        if on_pe:
            buf = self.buf[self.k % 2]
            q = act.sig(act.e.activation(buf.claim(act), tile, ACT.Square))
            buf.free(self.sum_on_pe(buf.ap, q))
        elif self.k == 0:
            self.last.set(act.sig(act.e.activation(self.acc, tile, ACT.Square)))
        else:
            buf = self.buf[self.k % 2]
            q = act.sig(act.e.activation(buf.claim(act), tile, ACT.Square))
            buf.free(self.sum_on_dve(buf.ap, q, False))

    def sum_on_dve(self, src, token, first):
        dve = self.b.dve
        dve.wait(token)
        self.last.follow(dve)
        if first:
            t = dve.sig(dve.e.tensor_copy(self.acc, src))
        else:
            t = dve.sig(dve.e.tensor_tensor(self.acc, self.acc, src, ALU.add))
        self.last.set(t)
        return t

    def sum_on_pe(self, src, token):
        pe = self.b.pe
        if self.k == 0:
            self.mean = self.b.next_wide()
            self.mean.claim(pe)
        pe.wait(token)
        for half in range(2):
            s = slice(half * HALF, (half + 1) * HALF)
            ins = pe.e.matmul(self.mean.ap[:, s], self.ones, src[:, s], start=(self.k == 0), stop=(self.k == self.n - 1))
        self.mean_done = pe.sig(ins)
        return self.mean_done

    def means(self):
        if self.mean is None:
            self.last.follow(self.b.pe)
            self.mean, self.mean_done = self.b.column_mean(self.ones, self.acc)
        mean, self.mean = self.mean, None
        return mean, self.mean_done

    def start(self, tiles):
        act, dve = self.b.act, self.b.dve
        mean, done = self.means()
        if self.centred:
            dve.wait(done)
            self.k = 0
            for tile in tiles:
                last = dve.sig(dve.e.tensor_tensor(tile, tile, mean.ap, ALU.subtract))
                self.square(tile, last, True)
                self.k += 1
            mean.free(last)
            mean, done = self.means()
        dve.wait(self.b.rsqrt_of(mean, done, self.rstd, self.eps))

    def scale(self, tile, dst, gain, k):
        dve = self.b.dve
        return dve.sig(dve.e.scalar_tensor_tensor(dst, tile, self.b.v(gain, k), self.rstd, ALU.mult, ALU.mult))

    def in_place(self, tiles, gain, bias=None, func=ACT.Identity):
        act = self.b.act
        self.start(tiles)
        for k, tile in enumerate(tiles):
            t = self.scale(tile, tile, gain, k)
            if bias is not None:
                act.wait(t)
                t = act.sig(act.e.activation(tile, tile, func, bias=self.b.v(bias, k)))
            yield k, tile, t

    def split_to(self, tiles, gain, out):
        act, dve = self.b.act, self.b.dve
        self.start(tiles)
        pairs, before = [], None

        def low(buf, hi, lo, h):
            dve.wait(h)
            t = dve.sig(dve.e.tensor_tensor(lo, buf.ap, hi.bitcast(F32), ALU.subtract))
            buf.free(t)
            pairs.append((h, t))

        for k, tile in enumerate(tiles):
            buf = self.buf[k % 2]
            n = self.scale(tile, buf.claim(dve), gain, k)
            hi, lo = out(k)
            act.wait(n)
            h = act.sig(act.e.activation(hi, buf.ap, ACT.Copy))
            if before:
                low(*before)
            before = (buf, hi, lo, h)
        low(*before)
        return pairs

    def split_and_keep(self, tiles, gain, bias, out, keep_scale=1.0, keep_bias=None):
        act, dve, b = self.b.act, self.b.dve, self.b
        self.start(tiles)
        pairs, before = [], None

        def low(k, hi, lo, h):
            dve.wait(h)
            t = dve.sig(dve.e.scalar_tensor_tensor(lo, tiles[k], b.v(bias, k), hi.bitcast(F32), ALU.add, ALU.subtract))
            pairs.append((h, t))
            act.wait(t)
            act.sig(act.e.activation(tiles[k], tiles[k], ACT.Identity, scale=keep_scale,
                                     bias=b.v(bias, k) if keep_bias is None else keep_bias[:, k:k + 1]))

        for k, tile in enumerate(tiles):
            n = self.scale(tile, tile, gain, k)
            hi, lo = out(k)
            act.wait(n)
            h = act.sig(act.e.activation(hi, tile, ACT.Identity, bias=b.v(bias, k)))
            if before:
                low(*before)
            before = (k, hi, lo, h)
        low(*before)
        b.kept = Token(act.line, act.line.count, None)
        return pairs


class Blocks(Program):
    def setup(self, t, blocks):
        nc, ctx = self.nc, self.ctx
        self.t = t
        self.blocks = blocks

        def sb(name, shape, dt=F32):
            return ctx.enter_context(nc.sbuf_tensor(name, shape, dt))

        self.x = sb("residual", [P, KD, S])
        self.h_hi = sb("h_hi", [P, KD, S], F32R)
        self.h_lo = sb("h_lo", [P, KD, S], F32R)
        self.vec = sb("vectors", [P, NVEC])
        self.common = sb("common", [P, COMMON.shape[1]])
        raw = sb("w_raw", [P, 2, KD * P])
        whi = sb("w_hi", [P, 2, KD * P], F32R)
        wlo = sb("w_lo", [P, 2, KD * P], F32R)
        self.w_raw = [self.slot(f"w_raw{i}", raw[:, i, :]) for i in range(2)]
        self.w_split = [self.slot(f"w_split{i}", (whi[:, i, :], wlo[:, i, :])) for i in range(2)]
        self.w_line = [self.dma_line(f"w_loaded{i}") for i in range(2)]
        self.aux = {}
        psum = ctx.enter_context(nc.psum_tensor("psum", [P, 8, HALF], F32))
        self.psum = psum
        two = lambda b: psum[:, b:b + 2, :].rearrange("p b n -> p (b n)")
        self.acc = [self.slot(f"acc{i}", two(2 * i)) for i in range(2)]
        self.wide = [self.slot(f"wide{i}", two(4 + 2 * i)) for i in range(2)]
        self.bank = [self.slot(f"bank{i}", psum[:, i, :]) for i in range(8)]
        self.n_acc = self.n_wide = 0
        self.w_loaded = [Held(self, f"w_loaded{i}") for i in range(2)]
        self.w_ready = [Held(self, f"w_ready{i}") for i in range(2)]
        self.tile_no, self.tile_base = 0, 0
        sp = self.sp
        self.fetch("start", self.common[:], t["common"])
        started = self.fetch("start", self.vec[:], t["vectors"])
        x = t["x_t"].rearrange("(c p) s -> p c s", p=P)
        self.x_loaded = [self.fetch(f"x{k}", self.x[:, k, :], x[:, k, :]) for k in range(KD)]
        for eng in (self.pe, self.act, self.dve, self.pool):
            eng.wait(started)
        self.end_norm = None
        self.w_load(0)
        self.w_load(1)
        self.w_split_tile(0)
        if blocks != (1,):
            self.bias_copies()

    def fetch(self, name, dst, src):
        return self.line_for(name).sig(self.sp.e.dma_start(dst, src))

    def line_for(self, name):
        if name not in self.aux:
            self.aux[name] = self.dma_line(f"{name}_loaded")
        return self.aux[name]

    def c(self, name, n=P):
        at = CONST_COLS[name]
        return self.common[:, at:at + n]

    def v(self, name, i=0):
        at = VEC[name] + i
        return self.vec[:, bass.ds(at, 1)]

    def bias_copies(self):
        sp, pe, dve, t = self.sp, self.pe, self.dve, self.t
        with self.scope("bias") as sb:
            padded = sb("padded", [NA_HEADS * REL_H, REL_PAD])
            sp.wait(dve.sig(dve.e.memset(padded[:], 0.0)))
            off = GRID_W - KW
            sp.wait(self.fetch("rpb", padded[:, off:off + REL_W], t["rpb"]))
            put_rel = self.fetch("rel_rows", t["rel_rows"], padded[:])
            rel = sb("rel", [BUCKETS, SWA_HEADS])
            onehot = sb("onehot", [BUCKETS, REL_BAND])
            band = sb("band", [SWA_HEADS, REL_BAND])
            self.fetch("swa", rel[:], t["rel_bias"])
            self.fetch("swa", onehot[:], t["onehot"])
            got = self.fetch("swa", band[:], t["outside"])
            pe.wait(got)
            b = self.bank[7]
            done = pe.sig(pe.e.matmul(b.claim(pe)[0:SWA_HEADS, 0:REL_BAND], rel[:], onehot[:], start=True, stop=True))
            dve.wait(done, got)
            line = dve.sig(dve.e.tensor_tensor(band[:], band[:], b.ap[0:SWA_HEADS, 0:REL_BAND], ALU.add))
            b.free(line)
            sp.wait(line)
            put_band = self.fetch("band_rows", t["band_rows"], band[:])
            sp.wait(put_rel, put_band)
            for h in range(NA_HEADS):
                rows = t["rel_rows"][h * REL_H:(h + 1) * REL_H, :].rearrange("(o r) w -> o (r w)", o=1)
                self.fetch("rel_copies", t["rel_copies"][h, :].rearrange("(q n) -> q n", q=GRID_W),
                           rows.broadcast_to([GRID_W, REL_H * REL_PAD]))
                self.fetch("band_copies", t["band_copies"][h, :].rearrange("(q n) -> q n", q=CH),
                           t["band_rows"][h:h + 1, :].broadcast_to([CH, REL_BAND]))

    def copies_done(self, name):
        line = self.aux[name]
        self.sp.wait(Token(line, line.count, None))

    def w_load(self, ahead_no):
        slot = self.w_raw[ahead_no % 2]
        slot.claim(self.sp)
        no = ahead_no
        if self.loop is not None:
            no = ahead_no + self.loop.index * self.w_turn
        src = self.t["weights"][bass.ds(no, 1), :, :].rearrange("a p n -> (a p) n") if self.loop is not None \
            else self.t["weights"][no, :, :]
        self.w_loaded[ahead_no % 2].set(self.w_line[ahead_no % 2].sig(self.sp.e.dma_start(slot.ap, src)))

    def w_split_tile(self, no):
        raw, out = self.w_raw[no % 2], self.w_split[no % 2]
        hi, lo = out.claim(self.act)
        self.w_loaded[no % 2].follow(self.act)
        a = self.act.sig(self.act.e.activation(hi, raw.ap, ACT.Copy))
        self.dve.wait(a)
        b = self.dve.sig(self.dve.e.tensor_tensor(lo, raw.ap, hi.bitcast(F32), ALU.subtract))
        raw.free(b)
        self.w_ready[no % 2].set(a, b)

    @contextmanager
    def w_turns(self, name, n, tiles):
        assert tiles % 2 == 0
        self.w_turn = tiles
        before = self.tile_no
        with self.repeat(name, n) as i:
            yield i
            assert self.tile_no == before + tiles, (name, self.tile_no - before)
        self.tile_no = before + n * tiles

    def next_tile(self):
        t = self.tile_no
        self.w_split_tile(t + 1)
        slot = self.w_split[t % 2]
        self.w_ready[t % 2].follow(self.pe)
        self.w_load(t + 2)
        self.tile_no = t + 1
        return slot

    def gemm(self, slot_out, tile, n_k, cols, lo_col, src, ready=None):
        pe = self.pe
        out = slot_out.claim(pe)
        hi, lo = (a.rearrange("p (k n) -> p k n", n=cols) for a in tile.ap)
        for k in range(n_k):
            if ready is not None:
                pe.wait(*ready[k])
            for part, (w, x) in enumerate(((hi, src(k, 0)), (hi, src(k, 1)), (lo, src(k, 0)))):
                for half in range(2):
                    s = slice(half * HALF, (half + 1) * HALF)
                    ins = pe.e.matmul(out[:, s], w[:, k, lo_col:lo_col + P], x[:, s],
                                      start=(k == 0 and part == 0), stop=(k == n_k - 1 and part == 2))
        return pe.sig(ins)

    def next_acc(self):
        self.n_acc += 1
        return self.acc[(self.n_acc - 1) % 2]

    def next_wide(self):
        self.n_wide += 1
        return self.wide[(self.n_wide - 1) % 2]

    def project(self, ready=None):
        tile = self.next_tile()
        acc = self.next_acc()
        done = self.gemm(acc, tile, KD, P, 0, lambda k, part: (self.h_lo if part else self.h_hi)[:, k, :], ready)
        tile.free(done)
        return acc, done

    def prepare_pair(self):
        t = self.tile_no
        self.w_split_tile(t + 1)
        self.w_load(t + 2)
        self.w_load(t + 3)

    def project_pair(self, ready):
        pe, t = self.pe, self.tile_no
        tiles = [self.w_split[(t + j) % 2] for j in range(2)]
        accs = [self.next_acc() for j in range(2)]
        for j in range(2):
            self.w_ready[(t + j) % 2].follow(pe)
            accs[j].claim(pe)
        done = [None, None]
        for k in range(KD):
            pe.wait(*ready[k])
            for j in range(2):
                hi, lo = (a[:, k * P:(k + 1) * P] for a in tiles[j].ap)
                for part, (w, x) in enumerate(((hi, self.h_hi), (hi, self.h_lo), (lo, self.h_hi))):
                    for half in range(2):
                        s = slice(half * HALF, (half + 1) * HALF)
                        ins = pe.e.matmul(accs[j].ap[:, s], w, x[:, k, s],
                                          start=(k == 0 and part == 0), stop=(k == KD - 1 and part == 2))
                if k == KD - 1:
                    done[j] = pe.sig(ins)
                    tiles[j].free(done[j])
        self.w_split_tile(t + 2)
        self.tile_no = t + 2
        return [(accs[j], done[j]) for j in range(2)]

    def column_mean(self, ones, src, token=None, w=None):
        w = w or self.next_wide()
        out = w.claim(self.pe)
        if token is not None:
            self.pe.wait(token)
        for half in range(2):
            s = slice(half * HALF, (half + 1) * HALF)
            ins = self.pe.e.matmul(out[:, s], ones, src[:, s], start=True, stop=True)
        return w, self.pe.sig(ins)

    def rsqrt_of(self, w, token, out, eps):
        act = self.act
        act.wait(token)
        ln = act.sig(act.e.activation(out, w.ap, ACT.Ln, bias=self.c(f"eps{eps}", 1)))
        w.free(ln)
        act.wait(ln)
        return act.sig(act.e.activation(out, out, ACT.Exp, scale=-0.5))

    def split(self, src, hi, lo, token):
        self.act.wait(token)
        a = self.act.sig(self.act.e.activation(hi, src, ACT.Copy))
        self.dve.wait(a)
        b = self.dve.sig(self.dve.e.tensor_tensor(lo, src, hi.bitcast(F32), ALU.subtract))
        return (a, b)

    def norm(self, ctx, name, ones, eps, n, centred=False):
        return Norm(self, ctx, name, ones, eps, n, centred)

    def x_tiles(self):
        return [self.x[:, k, :] for k in range(KD)]

    @contextmanager
    def scope(self, name, meet=True):
        with ExitStack() as ctx:
            yield lambda n, shape, dt=F32: ctx.enter_context(self.nc.sbuf_tensor(f"{name}_{n}", shape, dt))
            if meet:
                self.meet()

    def h(self, k):
        return self.h_hi[:, k, :], self.h_lo[:, k, :]

    def mix_out(self, name, alpha, ready, norm):
        def add(x, acc, done):
            self.dve.wait(done)
            t = self.dve.sig(self.dve.e.scalar_tensor_tensor(x, x, alpha, acc.ap, ALU.mult, ALU.add))
            acc.free(t)
            norm.gather(x, t)

        for j, (acc, done) in enumerate(self.project_pair(ready)):
            add(self.x[:, j, :], acc, done)
        with self.w_turns(f"{name}_out", KD // 2 - 1, 2) as i:
            for j in range(2):
                acc, done = self.project()
                add(self.x[:, i * 2 + 2 + j, :], acc, done)

    def mlp(self, name, conv, norm):
        act, dve, pe = self.act, self.dve, self.pe
        with self.scope(name, meet=False) as sb:
            act_hi = sb("act_hi", [P, 2, S], F32R)
            act_lo = sb("act_lo", [P, 2, S], F32R)
            hid = [self.slot(f"{name}_hid{j}", (act_hi[:, j, :], act_lo[:, j, :])) for j in range(2)]
            ta = self.slot(f"{name}_ta", sb("ta", [P, S])[:])
            tb = self.slot(f"{name}_tb", sb("tb", [P, S])[:])
            tp = self.slot(f"{name}_tp", sb("tp", [P, S])[:])
            state = {}
            hid_ready = [Held(self, f"{name}_hid_ready{j}") for j in range(2)]

            def taps(dst, acc, done, channel):
                act.wait(done)
                y = dst.claim(act)
                t0 = act.sig(act.e.activation(y, acc.ap, ACT.Identity, bias=self.v("conv_b", channel),
                                              scale=self.v("conv_w2", channel)))
                dve.wait(t0)
                t1 = dve.sig(dve.e.scalar_tensor_tensor(y[:, 1:S], acc.ap[:, 0:S - 1], self.v("conv_w1", channel),
                                                        y[:, 1:S], ALU.mult, ALU.add))
                dve.wait(t1)
                t2 = dve.sig(dve.e.scalar_tensor_tensor(y[:, 2:S], acc.ap[:, 0:S - 2], self.v("conv_w0", channel),
                                                        y[:, 2:S], ALU.mult, ALU.add))
                acc.free(t2)
                return t2

            def gate(channel, given=None):
                acc, done = given or self.project()
                if conv:
                    t = taps(ta, acc, done, channel)
                    act.wait(t)
                    state["a"] = act.sig(act.e.activation(ta.ap, ta.ap, ACT.Silu))
                else:
                    act.wait(done)
                    state["a"] = act.sig(act.e.activation(ta.claim(act), acc.ap, ACT.Silu))
                    acc.free(state["a"])

            def up(channel, j, given=None):
                acc, done = given or self.project()
                if conv:
                    t = taps(tb, acc, done, channel + DFF // P)
                    src = tb.ap
                else:
                    t, src = done, acc.ap
                dve.wait(t, state["a"])
                out = tp.claim(dve)
                m = dve.sig(dve.e.tensor_tensor(out, ta.ap, src, ALU.mult))
                ta.free(m)
                (tb if conv else acc).free(m)
                hi, lo = hid[j].claim(act)
                pair = self.split(out, hi, lo, m)
                tp.free(*pair)
                hid_ready[j].set(*pair)

            def down(last=False):
                hid_ready[0].follow(pe)
                hid_ready[1].follow(pe)
                for half in range(2):
                    tile = self.next_tile()
                    for n in range(4):
                        w = self.next_wide()
                        done = self.gemm(w, tile, 2, 4 * P, n * P,
                                         lambda k, part: (act_lo if part else act_hi)[:, k, :])
                        x = self.x[:, half * 4 + n, :]
                        dve.wait(done)
                        t = dve.sig(dve.e.tensor_tensor(x, x, w.ap, ALU.add))
                        w.free(t)
                        if last:
                            norm.gather(x, t)
                    tile.free(done)
                hid[0].free(done)
                hid[1].free(done)

            first = self.project_pair(self.h_ready)
            gate(0, first[0])
            up(0, 0, first[1])
            gate(1)
            up(1, 1)
            with self.w_turns(name, NGROUP - 1, 6) as i:
                gate(i * 2 + 2)
                down()
                up(i * 2 + 2, 0)
                gate(i * 2 + 3)
                up(i * 2 + 3, 1)
            down(last=True)

    def first(self):
        x = self.x_tiles()
        with ExitStack() as ctx:
            n1 = self.norm(ctx, "norm1", "mean1024", EPS, KD)
            for k in range(KD):
                n1.gather(x[k], self.x_loaded[k], on_pe=True)
            self.h_ready = n1.split_to(x, "mix_norm_g", self.h)
        y = self.ctx_y("y1")
        self.retention(y)
        self.sgu(y)
        ready = self.split_y(y)
        with ExitStack() as ctx:
            n2 = self.norm(ctx, "norm2", "mean1024", EPS, KD)
            self.mix_out("mix1", 1.0, ready, n2)
            self.prepare_pair()
            self.h_ready = n2.split_to(x, "ffn_norm_g", self.h)
        self.end_norm = self.norm_with_its_memory("norm3", "mean1024", EPS, KD)
        self.mlp("mlp1", True, self.end_norm)

    def norm_with_its_memory(self, *args, **kw):
        ctx = ExitStack()
        n = self.norm(ctx, *args, **kw)
        n.close = ctx.close
        return n

    def split_y(self, y):
        self.prepare_pair()
        ready = [self.split(y[:, k, :], *self.h(k), self.dve_now()) for k in range(KD)]
        self.close_y()
        return ready

    def dve_now(self):
        return Token(self.dve.line, self.dve.line.count, None)

    def ctx_y(self, name):
        self.y_ctx = ExitStack()
        return self.y_ctx.enter_context(self.nc.sbuf_tensor(name, [P, KD, S], F32))

    def close_y(self):
        self.y_ctx.close()

    def transposes(self, w, src, token, n=NCH, step=CH, first=0):
        pe = self.pe
        out = w.claim(pe)
        pe.wait(token)
        for b in range(n):
            at = (first + b) * step
            ins = pe.e.transpose(out[:, b * P:(b + 1) * P], src[:, at:at + P], self.c("ident"))
        return pe.sig(ins)

    def retention(self, y):
        act, dve, pe, sp = self.act, self.dve, self.pe, self.sp
        with self.scope("ret") as sb:
            rot = sb("rotary", [P, 2, S])
            table = sb("table", [P, 2 * P + 2])
            buf = {n: sb(n, [P, S]) for n in ("q", "k", "t", "gate", "state", "vtok", "ktok", "sT")}
            q, k, t, gate, st, vtok, ktok, sT = (buf[n][:] for n in ("q", "k", "t", "gate", "state", "vtok", "ktok", "sT"))
            mask, qdec = table[:, 0:P], table[:, P:2 * P]
            kdec, cdec = table[:, 2 * P:2 * P + 1], table[:, 2 * P + 1:2 * P + 2]
            rot_loaded = self.fetch("rotary", rot[:], self.t["rotary"])
            dve.wait(rot_loaded)
            table_slot = self.slot("ret_table", table[:])
            self.line_for("ret_table")
            chunks = lambda a: a.rearrange("p (n c) -> p n c", c=CH)

            def rotary(dst, acc, done, prior):
                dve.wait(done, *prior)
                a = dve.sig(dve.e.tensor_tensor(t[0:64, :], acc.ap[64:P, :], rot[64:P, 1, :], ALU.mult))
                b = dve.sig(dve.e.tensor_tensor(t[64:P, :], acc.ap[0:64, :], rot[0:64, 1, :], ALU.mult))
                c = dve.sig(dve.e.tensor_tensor(dst, acc.ap, rot[:, 0, :], ALU.mult))
                acc.free(c)
                dve.wait(c)
                d = dve.sig(dve.e.tensor_tensor(dst, dst, t, ALU.add))
                dve.wait(d)
                return d

            first = [self.h_ready]
            with self.w_turns("ret", RET_HEADS, 4) as head:
                table_slot.claim(sp)
                got_table = self.fetch(
                    "ret_table", table[:], self.t["retention"][bass.ds(head, 1), :, :].rearrange("a p n -> (a p) n"))
                before = [pe.turn_before(), act.turn_before()]
                acc, done = self.project(first[0])
                q_rot = rotary(q, acc, done, before)
                acc, done = self.project()
                k_rot = rotary(k, acc, done, [])
                acc, done = self.project()
                act.wait(done, k_rot)
                v_raw = act.sig(act.e.activation(t, acc.ap, ACT.Copy))
                acc.free(v_raw)
                acc, done = self.project()
                act.wait(done, dve.turn_before())
                g_silu = act.sig(act.e.activation(gate, acc.ap, ACT.Silu))
                acc.free(g_silu)
                w = self.next_wide()
                tr = self.transposes(w, t, v_raw)
                act.wait(tr)
                v_tok = act.sig(act.e.activation(vtok, w.ap, ACT.Copy))
                w.free(v_tok)
                w = self.next_wide()
                tr = self.transposes(w, k, k_rot)
                act.wait(tr, got_table)
                k_tok = act.sig(act.e.activation(ktok, w.ap, ACT.Copy, scale=kdec))
                w.free(k_tok)
                w = self.next_wide()
                out = w.claim(pe)
                for n in range(NCH):
                    c = slice(n * CH, (n + 1) * CH)
                    ins = pe.e.matmul(out[:, c], k[:, c], q[:, c], start=True, stop=True)
                s_done = pe.sig(ins)
                dve.wait(s_done, got_table)
                s_mask = dve.sig(dve.e.tensor_tensor(
                    chunks(sT), chunks(w.ap), mask.unsqueeze(1).broadcast_to([P, NCH, CH]), ALU.mult))
                w.free(s_mask)
                q_dec = dve.sig(dve.e.tensor_tensor(
                    chunks(q), chunks(q), qdec.unsqueeze(1).broadcast_to([P, NCH, CH]), ALU.mult))
                w = self.next_wide()
                out = w.claim(pe)
                pe.wait(v_tok, k_tok)
                for n in range(NCH - 1):
                    c = slice(n * CH, (n + 1) * CH)
                    ins = pe.e.matmul(out[:, c], ktok[:, c], vtok[:, c], start=True, stop=True)
                kv = pe.sig(ins)
                dve.wait(kv)
                last = dve.sig(dve.e.tensor_copy(st[:, CH:2 * CH], w.ap[:, 0:CH]))
                for n in range(2, NCH):
                    dve.wait(last)
                    last = dve.sig(dve.e.scalar_tensor_tensor(
                        st[:, n * CH:(n + 1) * CH], st[:, (n - 1) * CH:n * CH], cdec,
                        w.ap[:, (n - 1) * CH:n * CH], ALU.mult, ALU.add))
                w.free(last)
                table_slot.free(last, k_tok)
                w = self.next_wide()
                out = w.claim(pe)
                pe.wait(s_mask, q_dec, last)
                for n in range(NCH):
                    c = slice(n * CH, (n + 1) * CH)
                    ins = pe.e.matmul(out[:, c], vtok[:, c], sT[:, c], start=True, stop=(n == 0))
                    if n:
                        ins = pe.e.matmul(out[:, c], st[:, c], q[:, c], start=False, stop=True)
                o_done = pe.sig(ins)
                act.wait(o_done)
                sq = act.sig(act.e.activation(sT, w.ap, ACT.Square))
                dve.wait(sq)
                o = dve.sig(dve.e.tensor_scalar(k, w.ap, self.v("ret_norm_g", head), None, ALU.mult))
                w.free(sq, o)
                w, m = self.column_mean(self.c("mean128"), sT, sq)
                r = self.rsqrt_of(w, m, st, EPS)
                dve.wait(r, o)
                n1 = dve.sig(dve.e.tensor_tensor(k, k, st, ALU.mult))
                dve.wait(n1, g_silu)
                dve.sig(dve.e.tensor_tensor(y[:, head, :], k, gate, ALU.mult))

    def sgu(self, y):
        act, dve, pe, sp = self.act, self.dve, self.pe, self.sp
        with self.scope("sgu") as sb:
            names = ("u", "v", "t", "rstd", "vtok")
            u, v, t, rstd, vtok = (sb(n, [P, S])[:] for n in names)
            w_t = sb("w_t", [P, CH])
            b_s = sb("b_s", [P, CH])
            load = self.slot("sgu_load", None)
            self.line_for("sgu")
            with self.w_turns("sgu", SGU_GROUPS, 2) as g:
                load.claim(sp)
                self.fetch("sgu", w_t[:], self.t["sgu_w_t"][bass.ds(g, 1), :, :].rearrange("a s t -> (a s) t"))
                loaded = self.fetch("sgu", b_s[:], self.t["sgu_b_s"][bass.ds(g, 1), :].broadcast_to([P, CH]))
                acc, done = self.project()
                act.wait(done, dve.turn_before())
                a = act.sig(act.e.activation(u, acc.ap, ACT.Gelu))
                acc.free(a)
                acc, done = self.project()
                act.wait(done)
                gv = act.sig(act.e.activation(v, acc.ap, ACT.Gelu))
                acc.free(gv)
                w, m = self.column_mean(self.c("mean128"), v, gv)
                dve.wait(m)
                cent = dve.sig(dve.e.tensor_tensor(v, v, w.ap, ALU.subtract))
                w.free(cent)
                act.wait(cent)
                sq = act.sig(act.e.activation(t, v, ACT.Square))
                w, m = self.column_mean(self.c("mean128"), t, sq)
                r = self.rsqrt_of(w, m, rstd, EPS)
                dve.wait(r)
                n1 = dve.sig(dve.e.scalar_tensor_tensor(v, v, self.v("sgu_ln_g", g), rstd, ALU.mult, ALU.mult))
                act.wait(n1)
                vn = act.sig(act.e.activation(v, v, ACT.Identity, bias=self.v("sgu_ln_b", g)))
                w = self.next_wide()
                tr = self.transposes(w, v, vn)
                act.wait(tr)
                vt = act.sig(act.e.activation(vtok, w.ap, ACT.Copy))
                w.free(vt)
                dve.wait(loaded)
                wm = dve.sig(dve.e.tensor_tensor(w_t[:], w_t[:], self.c("tril_t"), ALU.mult))
                w = self.next_wide()
                out = w.claim(pe)
                pe.wait(vt, wm)
                for n in range(NCH):
                    c = slice(n * CH, (n + 1) * CH)
                    ins = pe.e.matmul(out[:, c], vtok[:, c], w_t[:], start=True, stop=True)
                mixed = pe.sig(ins)
                dve.wait(mixed)
                b = dve.sig(dve.e.tensor_tensor(
                    t.rearrange("p (n c) -> p n c", c=CH), w.ap.rearrange("p (n c) -> p n c", c=CH),
                    b_s[:].unsqueeze(1).broadcast_to([P, NCH, CH]), ALU.add))
                w.free(b)
                load.free(b)
                dve.wait(b, a)
                dve.sig(dve.e.tensor_tensor(y[:, g + RET_HEADS, :], t, u, ALU.mult))

    def second(self):
        x = self.x_tiles()
        with ExitStack() as ctx:
            n4 = self.norm(ctx, "norm4", "mean1024", EPS, KD)
            for k, tile, t in self.block_input("final_norm_g"):
                n4.gather(tile, t, on_pe=True)
            self.prepare_pair()
            self.h_ready = n4.split_to(x, "ln_g_2", self.h)
        self.close_end_norm()
        y = self.ctx_y("y2")
        self.conformer(y)
        self.neighbourhood(y)
        ready = self.split_y(y)
        self.end_norm = self.norm_with_its_memory("norm5", "mean1024", EPS, KD)
        self.mix_out("mix2", 1.0, ready, self.end_norm)

    def block_input(self, gain, bias=None):
        if self.end_norm is not None:
            yield from self.end_norm.in_place(self.x_tiles(), gain, bias)
        else:
            yield from ((k, tile, self.x_loaded[k]) for k, tile in enumerate(self.x_tiles()))

    def close_end_norm(self):
        if self.end_norm is not None:
            self.end_norm.close()
            self.end_norm = None

    def conformer(self, y):
        act, dve, pe, sp = self.act, self.dve, self.pe, self.sp
        with self.scope("conv") as sb:
            u = sb("u", [P, S + 2 * PAD])
            ga = self.slot("conv_ga", sb("ga", [P, S])[:])
            gb = self.slot("conv_gb", sb("gb", [P, S])[:])
            z1 = dve.sig(dve.e.memset(u[:, 0:PAD], 0.0))
            z2 = dve.sig(dve.e.memset(u[:, PAD + S:], 0.0))
            dve.wait(z1, z2)

            def gated(i, first, second):
                for slot, (acc, done), func, at in ((ga, first, ACT.Identity, 0), (gb, second, ACT.Sigmoid, 4)):
                    act.wait(done)
                    t = act.sig(act.e.activation(slot.claim(act), acc.ap, func, bias=self.v("b_in_2", i + at)))
                    acc.free(t)
                    dve.wait(t)
                u_read.follow(dve)
                t = dve.sig(dve.e.tensor_tensor(u[:, PAD:PAD + S], ga.ap, gb.ap, ALU.mult))
                ga.free(t)
                gb.free(t)
                u_ready.set(t)

            def taps(i, lo, hi):
                out = y[:, i, :]
                for j in range(lo, hi):
                    w = self.v("dw_w_2", i * TAPS + j)
                    u_ready.follow(dve)
                    u_read.follow(dve)
                    if j == 0:
                        t = dve.sig(dve.e.tensor_scalar(out, u[:, 0:S], w, self.v("dw_b_2", i), ALU.mult, ALU.add))
                    else:
                        t = dve.sig(dve.e.scalar_tensor_tensor(out, u[:, j:j + S], w, out, ALU.mult, ALU.add))
                    u_read.set(t)

            u_ready, u_read = Held(self, "u_ready"), Held(self, "u_read")
            gated(0, *self.project_pair(self.h_ready))
            with self.w_turns("conv", CONV_TILES - 1, 2) as i:
                first = self.project()
                taps(i, 0, TAPS // 2)
                second = self.project()
                taps(i, TAPS // 2, TAPS)
                gated(i + 1, first, second)
            cuts = [0, 8, 17, 26, TAPS]
            for j in range(CONV_TILES):
                acc, done = self.project()
                taps(CONV_TILES - 1, cuts[j], cuts[j + 1])
                act.wait(done)
                acc.free(act.sig(act.e.activation(y[:, j + 4, :], acc.ap, ACT.Silu, bias=self.v("b_in_2", j + 8))))
        with ExitStack() as ctx:
            c_hi = ctx.enter_context(self.nc.sbuf_tensor("pw_hi", [P, 4, S], F32R))
            c_lo = ctx.enter_context(self.nc.sbuf_tensor("pw_lo", [P, 4, S], F32R))
            with ExitStack() as norm_ctx:
                n = self.norm(norm_ctx, "cln", "mean512", EPS, 4, centred=True)
                tiles = [y[:, k, :] for k in range(4)]
                for tile in tiles:
                    n.gather(tile, self.dve_now(), on_pe=True)
                placed = list(n.in_place(tiles, "cln_g_2", "cln_b_2", ACT.Silu))
                ready = [self.split(tile, c_hi[:, k, :], c_lo[:, k, :], t) for k, tile, t in placed]
            with self.scope("pw") as sb:
                t = [self.slot(f"pw_t{i}", sb(f"t{i}", [P, S])[:]) for i in range(2)]
                rstd = sb("rstd", [P, S])[:]
                for n in range(4):
                    if n % 2 == 0:
                        tile = self.next_tile()
                    acc = self.next_acc()
                    done = self.gemm(acc, tile, 4, 2 * P, (n % 2) * P,
                                     lambda k, part: (c_lo if part else c_hi)[:, k, :], ready)
                    if n % 2:
                        tile.free(done)
                    act.wait(done)
                    out = y[:, n, :]
                    p = act.sig(act.e.activation(out, acc.ap, ACT.Identity, bias=self.v("pw_b_2", n)))
                    sq = act.sig(act.e.activation(t[0].claim(act), acc.ap, ACT.Square, bias=self.v("pw_b_2", n)))
                    acc.free(sq)
                    w, m = self.column_mean(self.c("mean64"), t[0].ap, sq)
                    t[0].free(m)
                    if n:
                        act.wait(g)
                    r = self.rsqrt_of(w, m, rstd, EPS)
                    dve.wait(r, p)
                    g = dve.sig(dve.e.scalar_tensor_tensor(out, out, self.v("gn_conv_g_2", n), rstd, ALU.mult, ALU.mult))
                    dve.wait(g)
                    g = dve.sig(dve.e.tensor_tensor(out, out, y[:, n + 4, :], ALU.mult))
                    dve.wait(g)

    def neighbourhood(self, y):
        act, dve, pe, sp = self.act, self.dve, self.pe, self.sp
        with self.scope("na") as sb:
            seen = sb("seen", [P, GRID_W])
            got_seen = self.fetch("seen", seen[:], self.t["seen"])
            self.copies_done("rel_copies")
            q2 = sb("q2", [P, ROWS, P])[:]
            k, t, gate = (sb(n, [P, S])[:] for n in ("k", "t", "gate"))
            vtok = sb("vtok", [P, 15, P])[:]
            bias = sb("bias", [P, REL_H, GRID_W])
            bias_slot = self.slot("na_bias", bias[:])
            self.line_for("na_bias")
            prob = [self.slot(f"na_prob{i}", sb(f"prob{i}", [P, HALF])[:]) for i in range(2)]
            prob_t = [self.slot(f"na_pt{i}", sb(f"pt{i}", [P, HALF])[:]) for i in range(2)]
            stat = [sb(f"stat{i}", [P, 4]) for i in range(2)]
            bq = sb("bq", [P, 4])
            at = VEC["b_in_2"] + 12
            dve.e.tensor_scalar(bq[:], self.vec[:, at:at + 4], SCALE, None, ALU.mult)
            z = dve.sig(dve.e.memset(q2, 0.0))
            act.wait(z)
            dve.wait(got_seen)
            score_bank = [self.bank[4], self.bank[5]]
            turn_bank, out_bank = self.bank[6], self.bank[7]
            with self.w_turns("na", NA_HEADS // 2, 4) as pair:
                bias_slot.claim(sp)
                for a in range(2):
                    one = self.t["rel_copies"][bass.ds(pair * 2 + a, 1), :]
                    src = bass.AP(tensor=one.tensor, offset=one.offset + GRID_W - 1,
                                  ap=[[REL_H * REL_PAD - 1, GRID_W], [REL_PAD, REL_H], [1, GRID_W]])
                    got_bias = self.fetch("na_bias", bias[64 * a:64 * a + 64, :, :], src)
                dve.wait(got_bias)
                b_in = lambda n: self.v("b_in_2", pair + n)
                before = [pe.turn_before(), dve.turn_before()]
                acc, done = self.project()
                act.wait(done, *before)
                for a in range(2):
                    c = slice(64 * a, 64 * a + 64)
                    tq = act.sig(act.e.activation(q2[c, :, c], acc.ap[c, :].rearrange("p (r w) -> p r w", w=GRID_W),
                                                  ACT.Identity, bias=bq[c, bass.ds(pair, 1)], scale=SCALE))
                acc.free(tq)
                acc, done = self.project()
                act.wait(done)
                tk = act.sig(act.e.activation(k, acc.ap, ACT.Identity, bias=b_in(16)))
                acc.free(tk)
                acc, done = self.project()
                act.wait(done)
                tv = act.sig(act.e.activation(t, acc.ap, ACT.Identity, bias=b_in(20)))
                acc.free(tv)
                acc, done = self.project()
                act.wait(done)
                tg = act.sig(act.e.activation(gate, acc.ap, ACT.Silu, bias=b_in(24)))
                acc.free(tg)
                masked = dve.sig(dve.e.tensor_tensor(
                    bias[:], bias[:], seen[:].unsqueeze(1).broadcast_to([P, REL_H, GRID_W]), ALU.add))
                dve.wait(masked)
                for part, n in ((0, 8), (1, 7)):
                    w = self.next_acc()
                    tr = self.transposes(w, t, tv, n=n, step=64, first=8 * part)
                    act.wait(tr)
                    v_tok = act.sig(act.e.activation(vtok[:, 8 * part:8 * part + n, :].rearrange("p a b -> p (a b)"),
                                                     w.ap[:, 0:n * P], ACT.Copy))
                    w.free(v_tok)
                out_y = y[:, pair + 4, :]
                key_row = lambda r: min(max(r - KH // 2, 0), ROWS - KH)
                normed, turned = {}, {}
                for step in range(ROWS + 2):
                    r = step
                    if r < ROWS:
                        ks = key_row(r)
                        b = score_bank[r % 2]
                        out = b.claim(pe)
                        pe.wait(tq, tk)
                        s_done = pe.sig(pe.e.matmul(out, q2[:, r, :], k[:, ks * GRID_W:(ks + KH) * GRID_W],
                                                    start=True, stop=True))
                        pr, st = prob[r % 2], stat[r % 2]
                        dve.wait(s_done)
                        p = pr.claim(dve)
                        rel = ks - r + KH - 1
                        dve.e.memset(st[:, 2:3], 0.0)
                        mx = dve.sig(dve.e.tensor_tensor_reduce(
                            p, out, bias[:, rel:rel + KH, :].rearrange("p a b -> p (a b)"), 1.0, 3 * MASKED,
                            ALU.add, ALU.max, st[:, 0:1]))
                        b.free(mx)
                        if r == ROWS - 1:
                            bias_slot.free(mx)
                        dve.wait(mx)
                        nm = dve.sig(dve.e.tensor_scalar(st[:, 1:2], st[:, 0:1], -1.0, None, ALU.mult))
                        act.wait(nm)
                        ex = act.sig(act.e.activation(p, p, ACT.Exp, bias=st[:, 1:2], accum_out=st[:, 2:3]))
                        dve.wait(ex)
                        rc = dve.sig(dve.e.reciprocal(st[:, 3:4], st[:, 2:3]))
                        dve.wait(rc)
                        normed[r] = dve.sig(dve.e.tensor_scalar(p, p, st[:, 3:4], None, ALU.mult))
                    r = step - 1
                    if 0 <= r < ROWS:
                        out = turn_bank.claim(pe)
                        pe.wait(normed[r])
                        for b in range(4):
                            ins = pe.e.transpose(out[:, b * P:(b + 1) * P], prob[r % 2].ap[:, b * P:(b + 1) * P],
                                                 self.c("ident"))
                        tr = pe.sig(ins)
                        prob[r % 2].free(tr)
                        act.wait(tr)
                        turned[r] = act.sig(act.e.activation(prob_t[r % 2].claim(act), out, ACT.Copy))
                        turn_bank.free(turned[r])
                    r = step - 2
                    if 0 <= r < ROWS:
                        ks = key_row(r)
                        if r % 4 == 0:
                            o = out_bank.claim(pe)
                        pe.wait(turned[r], v_tok)
                        for b in range(4):
                            ins = pe.e.matmul(o[:, (r % 4) * P:(r % 4 + 1) * P], vtok[:, ks + 2 * b, :],
                                              prob_t[r % 2].ap[:, b * P:(b + 1) * P], start=(b == 0), stop=(b == 3))
                        pv = pe.sig(ins)
                        prob_t[r % 2].free(pv)
                        if r % 4 == 3:
                            act.wait(pv)
                            for a in range(2):
                                c = slice(64 * a, 64 * a + 64)
                                dst = t[c, (r - 3) * 64:(r + 1) * 64].rearrange("p (r w) -> p r w", w=64)
                                src = o[c, :].rearrange("p (r q) -> p r q", q=P)[:, :, c]
                                last = act.sig(act.e.activation(dst, src, ACT.Copy))
                            out_bank.free(last)
                act.wait(last)
                sq = act.sig(act.e.activation(k, t, ACT.Square))
                acc, m = self.column_mean(self.c("mean64"), k, sq, self.next_acc())
                r_ = self.rsqrt_of(acc, m, k, EPS)
                self.next_acc()
                dve.wait(r_, last)
                n1 = dve.sig(dve.e.scalar_tensor_tensor(t, t, self.v("gn_att_g_2", pair), k, ALU.mult, ALU.mult))
                dve.wait(n1, tg)
                dve.sig(dve.e.tensor_tensor(out_y, t, gate, ALU.mult))

    def third(self):
        x = self.x_tiles()
        with ExitStack() as ctx:
            l1 = self.norm(ctx, "ln1", "mean1024", LN_EPS, KD, centred=True)
            for k, tile, t in self.block_input("final_g_2"):
                l1.gather(tile, t, on_pe=True)
            self.prepare_pair()
            self.h_ready = l1.split_and_keep(x, "ln_in_g_3", "ln_in_b_3", self.h)
        self.close_end_norm()
        y = self.ctx_y("y3")
        self.attention_pairs(y)
        self.prepare_pair()
        ready = []
        with ExitStack() as ctx:
            for name, gain, first in (("norm6", "sb_norm_g_3", 0), ("norm7", "swa_norm_g_3", 4)):
                n = self.norm(ctx, name, "mean512", EPS, 4)
                tiles = [y[:, first + k, :] for k in range(4)]
                for tile in tiles:
                    n.gather(tile, self.act_now(), on_pe=True)
                ready += n.split_to(tiles, gain, lambda k: self.h(first + k))
        self.close_y()
        with ExitStack() as ctx:
            l2 = self.norm(ctx, "ln2", "mean1024", LN_EPS, KD, centred=True)
            bias = ctx.enter_context(self.nc.sbuf_tensor("ln2_bias", [P, KD], F32))
            at = VEC["ln1_b_3"]
            self.act.wait(*ready[-1])
            scaled = self.act.sig(self.act.e.activation(bias[:], self.vec[:, at:at + KD], ACT.Copy, scale=ALPHA))
            self.mix_out("mix3", ALPHA, ready, l2)
            self.prepare_pair()
            self.act.wait(scaled)
            self.h_ready = l2.split_and_keep(x, "ln1_g_3", "ln1_b_3", self.h, ALPHA, bias)
            self.dve.wait(self.kept)
        self.end_norm = self.norm_with_its_memory("ln3", "mean1024", LN_EPS, KD, centred=True)
        self.mlp("mlp3", False, self.end_norm)

    def act_now(self):
        return Token(self.act.line, self.act.line.count, None)

    def attention_pairs(self, y):
        act, dve, pe, sp = self.act, self.dve, self.pe, self.sp
        with ExitStack() as ctx:
            k2 = ctx.enter_context(self.nc.sbuf_tensor("swa_k2", [P, 2, S], F32))
            v2 = ctx.enter_context(self.nc.sbuf_tensor("swa_v2", [P, NCH, 2, 64], F32))
            with self.scope("kv") as sb:
                t = sb("t", [P, S])[:]
                (acc, done), second = self.project_pair(self.h_ready)
                act.wait(done)
                for g in range(2):
                    for a in range(2):
                        last = act.sig(act.e.activation(k2[64 * a:64 * a + 64, g, :], acc.ap[64 * g:64 * g + 64, :], ACT.Copy))
                acc.free(last)
                acc, done = second
                act.wait(done)
                tv = act.sig(act.e.activation(t, acc.ap, ACT.Copy))
                acc.free(tv)
                w = self.next_wide()
                tr = self.transposes(w, t, tv)
                self.next_wide()
                act.wait(tr)
                last = act.sig(act.e.activation(v2[:].rearrange("p n g d -> p (n g d)"), w.ap, ACT.Copy))
                w.free(last)
            self.stick_breaking(y)
            self.sliding_window(y, k2, v2)

    def stick_breaking(self, y):
        act, dve, pe, sp = self.act, self.dve, self.pe, self.sp
        SOFT, SUM, OUT = 2, 3, 5
        with self.scope("sb") as sb:
            q, k, vtok = (sb(n, [P, S])[:] for n in ("q", "k", "vtok"))
            ring = lambda name, n: (lambda a: [self.slot(f"sb_{name}{i}", a[:, i, :]) for i in range(n)])(
                sb(name, [P, n, HALF]))
            mag_all = sb("mag", [P, 4, HALF])
            mag = [self.slot(f"sb_mag{i}", mag_all[:, i, :]) for i in range(4)]
            v_raw = mag_all[:, 0:2, :].rearrange("p a n -> p (a n)")
            soft, prob, carry = ring("soft", 3), ring("prob", 3), ring("carry", 2)
            tiles = []
            for qh in range(2):
                for kb in range(4 * qh + 3, -1, -1):
                    for hh in range(2):
                        q0 = max(kb * CH, qh * HALF)
                        tiles.append((hh, qh, kb, q0 - qh * HALF))
            act.e.preload_act_table_set("natural_log_exp_and_others")
            with self.w_turns("sb", 4, 4) as pair:
                before = [pe.turn_before()]
                acc, done = self.project()
                act.wait(done, *before)
                tq = act.sig(act.e.activation(q, acc.ap, ACT.Copy, scale=SCALE))
                acc.free(tq)
                acc, done = self.project()
                act.wait(done)
                tk = act.sig(act.e.activation(k, acc.ap, ACT.Copy))
                acc.free(tk)
                acc, done = self.project()
                act.wait(done)
                mag[0].claim(act)
                mag[1].claim(act)
                tv = act.sig(act.e.activation(v_raw, acc.ap, ACT.Copy))
                acc.free(tv)
                acc, done = self.project()
                act.wait(done)
                acc.free(act.sig(act.e.activation(y[:, pair + 4, :], acc.ap, ACT.Copy)))
                w = self.next_acc()
                tr = self.transposes(w, v_raw, tv)
                mag[0].free(tr)
                mag[1].free(tr)
                act.wait(tr)
                v_tok = act.sig(act.e.activation(vtok, w.ap, ACT.Copy))
                w.free(v_tok)
                oslot = self.next_acc()
                o = oslot.claim(pe)
                pe.wait(tq, tk, v_tok)
                banks = [self.bank[b] for b in (4, 5, 6, 7, 0, 1)]
                score, softened, logit, weight, carried = {}, {}, {}, {}, {}
                for step in range(len(tiles) + OUT):
                    i = step
                    if i < len(tiles):
                        hh, qh, kb, c0 = tiles[i]
                        hp = slice(64 * hh, 64 * hh + 64)
                        c = slice(c0, HALF)
                        z = banks[i % 6].claim(pe)
                        z_done = pe.sig(pe.e.matmul(z[:, c], k[hp, kb * CH:(kb + 1) * CH],
                                                    q[hp, qh * HALF + c0:(qh + 1) * HALF],
                                                    start=True, stop=False, skip_group_check=True))
                        dve.wait(z_done)
                        m = mag[i % 4].claim(dve)
                        low = dve.sig(dve.e.tensor_scalar(m[:, c], z[:, c], LN_TOP, None, ALU.min))
                        act.wait(low)
                        ex = act.sig(act.e.activation(m[:, c], m[:, c], ACT.Exp))
                        act.wait(ex)
                        score[i] = act.sig(act.e.activation(m[:, c], m[:, c], ACT.Ln, bias=1.0))
                    i = step - SOFT
                    if 0 <= i < len(tiles):
                        hh, qh, kb, c0 = tiles[i]
                        c, d = slice(c0, HALF), slice(c0, c0 + CH)
                        diag = kb >= 4 * qh
                        z, mg, sf = banks[i % 6].ap, mag[i % 4], soft[i % 3]
                        dve.wait(score[i])
                        s = sf.claim(dve)
                        t = dve.sig(dve.e.tensor_tensor(s[:, c], mg.ap[:, c], z[:, c], ALU.max))
                        mg.free(t)
                        if diag:
                            dve.wait(t)
                            t = dve.sig(dve.e.tensor_tensor(s[:, d], s[:, d], self.c("after"), ALU.mult))
                        softened[i] = t
                    i = step - SUM
                    if 0 <= i < len(tiles):
                        hh, qh, kb, c0 = tiles[i]
                        c, d = slice(c0, HALF), slice(c0, c0 + CH)
                        diag = kb >= 4 * qh
                        z, sf, cr = banks[i % 6].ap, soft[i % 3], carry[hh]
                        s = sf.ap
                        later = slice(c0 + CH if diag else 0, HALF)
                        first = kb == 4 * qh + 3
                        pe.wait(softened[i])
                        ins = pe.e.matmul(z[:, c], self.c("neg_tri"), s[:, c], start=False, stop=False,
                                          skip_group_check=True)
                        if diag:
                            ins = pe.e.matmul(z[:, d], self.c("ident"), self.c("bar_after"), start=False,
                                              stop=first, skip_group_check=True)
                        if not first:
                            pe.wait(*carried[hh])
                            ins = pe.e.matmul(z[:, later], self.c("neg_ones"), cr.ap[:, later], start=False,
                                              stop=True, skip_group_check=True)
                        logit[i] = pe.sig(ins)
                        cr.free(logit[i])
                        if kb > 0:
                            cr.claim(dve)
                            dve.wait(softened[i])
                            new = []
                            if diag:
                                new.append(dve.sig(dve.e.tensor_copy(cr.ap[:, d], s[:, d])))
                            if not first:
                                dve.wait(*carried[hh])
                                new.append(dve.sig(dve.e.tensor_tensor(cr.ap[:, later], cr.ap[:, later],
                                                                       s[:, later], ALU.add)))
                            carried[hh] = new
                            sf.free(logit[i], new[-1])
                        else:
                            sf.free(logit[i])
                        act.wait(logit[i])
                        weight[i] = act.sig(act.e.activation(prob[i % 3].claim(act)[:, c], z[:, c], ACT.Exp))
                        banks[i % 6].free(weight[i])
                    i = step - OUT
                    if 0 <= i < len(tiles):
                        hh, qh, kb, c0 = tiles[i]
                        hp = slice(64 * hh, 64 * hh + 64)
                        pe.wait(weight[i])
                        ins = pe.e.matmul(o[hp, qh * HALF + c0:(qh + 1) * HALF],
                                          vtok[:, kb * CH + 64 * hh:kb * CH + 64 * hh + 64], prob[i % 3].ap[:, c0:HALF],
                                          start=(kb == 4 * qh + 3), stop=(kb == 0), skip_group_check=True)
                        o_done = pe.sig(ins)
                        prob[i % 3].free(o_done)
                w.free(weight[len(tiles) - 1])
                act.wait(o_done)
                oslot.free(act.sig(act.e.activation(y[:, pair, :], o, ACT.Copy)))

    def sliding_window(self, y, k2, v2):
        act, dve, pe, sp = self.act, self.dve, self.pe, self.sp
        with self.scope("swa") as sb:
            sinks = sb("sinks", [P, SWA_HEADS])
            dve.wait(self.fetch("sinks", sinks[:], self.t["sinks"].broadcast_to([P, SWA_HEADS])))
            self.copies_done("band_copies")
            q2 = sb("q2", [P, 2, S])[:]
            kg = sb("kg", [P, S])[:]
            vg = sb("vg", [P, NCH, P])[:]
            sink = sb("sink", [P, 2])
            bias = sb("bias", [P, 2, BAND])
            bias_slot = self.slot("swa_bias", bias[:])
            self.line_for("swa_bias")
            prob = [self.slot(f"swa_p{i}", sb(f"p{i}", [P, 2, BAND])[:]) for i in range(2)]
            prob_t = [self.slot(f"swa_pt{i}", sb(f"pt{i}", [P, 2, 2, CH])[:]) for i in range(2)]
            stat = [sb(f"stat{i}", [P, 6, 2]) for i in range(2)]
            z = dve.sig(dve.e.memset(q2, 0.0))
            dve.wait(z)
            with self.repeat("swa", SWA_HEADS // 2) as pair:
                bias_slot.claim(sp)
                one = self.t["band_copies"][bass.ds(pair * 2, 1), :]
                src = bass.AP(tensor=one.tensor, offset=one.offset + CH - 1,
                              ap=[[REL_BAND - 1, CH], [CH * REL_BAND, 2], [1, BAND]])
                got_bias = self.fetch("swa_bias", bias[:], src)
                dve.wait(pe.turn_before(), act.turn_before())
                act.wait(pe.turn_before())
                for a in range(2):
                    c = slice(64 * a, 64 * a + 64)
                    dve.e.tensor_scalar(q2[c, a, :], y[c, pair + 4, :], SCALE, None, ALU.mult)
                dve.e.tensor_copy(sink[:], sinks[:, bass.ds(pair * 2, 2)])
                act_staged = act.sig(act.e.activation(kg, k2[:, pair // 2, :], ACT.Copy))
                for a in range(2):
                    staged = dve.sig(dve.e.tensor_copy(vg[:, :, 64 * a:64 * a + 64], v2[:, :, pair // 2, :]))
                dve.wait(staged)
                normed, turned = {}, {}
                for step in range(NCH + 2):
                    n = step
                    if n < NCH:
                        lo = 0 if n else CH
                        sbk = self.bank[4 + n % 2]
                        out = sbk.claim(pe).rearrange("p (a c) -> p a c", a=2)
                        pe.wait(staged, act_staged)
                        for a in range(2):
                            ins = pe.e.matmul(out[:, a, lo:], q2[:, a, n * CH:(n + 1) * CH],
                                              kg[:, (n - 1) * CH + lo:(n + 1) * CH], start=True, stop=True)
                        s_done = pe.sig(ins)
                        pr, st = prob[n % 2], stat[n % 2]
                        dve.wait(s_done, got_bias)
                        p = pr.claim(dve)
                        dve.e.memset(st[:, 3, :], 0.0)
                        for a in range(2):
                            m = dve.sig(dve.e.tensor_tensor_reduce(
                                p[:, a, lo:], out[:, a, lo:], bias[:, a, lo:], 1.0, sink[:, a:a + 1],
                                ALU.add, ALU.max, st[:, 0, a:a + 1]))
                        sbk.free(m)
                        if n == NCH - 1:
                            bias_slot.free(m)
                        dve.wait(m)
                        dve.sig(dve.e.tensor_scalar(st[:, 1, :], st[:, 0, :], -1.0, None, ALU.mult))
                        d = dve.sig(dve.e.tensor_tensor(st[:, 2, :], sink[:], st[:, 0, :], ALU.subtract))
                        act.wait(d)
                        for a in range(2):
                            act.sig(act.e.activation(p[:, a, lo:], p[:, a, lo:], ACT.Exp, bias=st[:, 1, a:a + 1],
                                                     accum_out=st[:, 3, a:a + 1]))
                        ex = act.sig(act.e.activation(st[:, 4, :], st[:, 2, :], ACT.Exp))
                        dve.wait(ex)
                        dn = dve.sig(dve.e.tensor_tensor(st[:, 5, :], st[:, 3, :], st[:, 4, :], ALU.add))
                        dve.wait(dn)
                        dn = dve.sig(dve.e.reciprocal(st[:, 5, :], st[:, 5, :]))
                        dve.wait(dn)
                        for a in range(2):
                            normed[n] = dve.sig(dve.e.tensor_scalar(p[:, a, lo:], p[:, a, lo:], st[:, 5, a:a + 1], None,
                                                                    ALU.mult))
                    n = step - 1
                    if 0 <= n < NCH:
                        tb = self.bank[6]
                        out = tb.claim(pe).rearrange("p (k a q) -> p k a q", k=2, a=2)
                        pe.wait(normed[n])
                        ks = range(2) if n else range(1, 2)
                        for kb in ks:
                            for a in range(2):
                                ins = pe.e.transpose(out[:, kb, a, :], prob[n % 2].ap[:, a, kb * CH:(kb + 1) * CH],
                                                     self.c("ident"))
                        tr = pe.sig(ins)
                        prob[n % 2].free(tr)
                        act.wait(tr)
                        dst = prob_t[n % 2].claim(act)
                        turned[n] = act.sig(act.e.activation(dst[:, ks[0]:, :, :], out[:, ks[0]:, :, :], ACT.Copy))
                        tb.free(turned[n])
                    n = step - 2
                    if 0 <= n < NCH:
                        ob = self.bank[7]
                        out = ob.claim(pe)
                        pe.wait(turned[n])
                        ks = range(2) if n else range(1, 2)
                        for kb in ks:
                            ins = pe.e.matmul(out[:, 0:2 * CH], vg[:, n - 1 + kb, :],
                                              prob_t[n % 2].ap[:, kb, :, :].rearrange("p a q -> p (a q)"),
                                              start=(kb == ks[0]), stop=(kb == 1))
                        pv = pe.sig(ins)
                        prob_t[n % 2].free(pv)
                        act.wait(pv)
                        for a in range(2):
                            c = slice(64 * a, 64 * a + 64)
                            last = act.sig(act.e.activation(y[c, pair + 4, n * CH:(n + 1) * CH],
                                                            out[c, a * CH:(a + 1) * CH], ACT.Copy))
                        ob.free(last)

    def finish(self, gain, bias):
        sp = self.sp
        for k, tile, t in self.block_input(gain, bias):
            sp.wait(t)
            out = self.fetch("out", self.t["out"][k * P:(k + 1) * P, :], tile)
        sp.wait(out)
        for loaded in self.w_loaded:
            loaded.follow(sp)
        self.close_end_norm()


BLOCKS = (1, 2, 3)


def program(nc, tensors, blocks, counts, last_turn):
    with ExitStack() as ctx:
        b = Blocks(nc, ctx, counts, last_turn)
        b.setup(tensors, blocks)
        for n in blocks:
            (b.first, b.second, b.third)[n - 1]()
        b.finish(*{1: ("final_norm_g", None), 2: ("final_g_2", None), 3: ("ln2_g_3", "ln2_b_3")}[blocks[-1]])
        return b


def k_tiles(w):
    k, n = w.shape
    return w.reshape(k // P, P, n // P, P).transpose(2, 1, 0, 3).reshape(n // P, P, KD * P)


def down_tiles(w):
    return w.reshape(NGROUP, 2, P, 2, 4 * P).transpose(0, 3, 2, 1, 4).reshape(2 * NGROUP, P, KD * P)


def mlp_order(up, down):
    a, b = up[:DFF // P], up[DFF // P:]
    out = [a[0], b[0], a[1], b[1]]
    for g in range(1, NGROUP):
        out += [a[2 * g], down[2 * g - 2], down[2 * g - 1], b[2 * g], a[2 * g + 1], b[2 * g + 1]]
    return out + [down[-2], down[-1]]


def weight_stream(i, blocks):
    tiles = []
    if 1 in blocks:
        w = k_tiles(i["w_in"][0])
        for h in range(4):
            tiles += [w[h], w[4 + h], w[8 + h], w[12 + h]]
        for g in range(4):
            tiles += [w[16 + g], w[20 + g]]
        tiles += list(k_tiles(i["w_out"][0]))
        tiles += mlp_order(k_tiles(i["w_up"][0]), down_tiles(i["w_down"][0]))
    if 2 in blocks:
        w = k_tiles(i["w_in_2"][0])
        for c in range(4):
            tiles += [w[c], w[4 + c]]
        tiles += list(w[8:12])
        tiles += list(i["pw_w_2"][0].reshape(4, P, 2, 2 * P).transpose(2, 1, 0, 3).reshape(2, P, KD * P))
        for p in range(4):
            tiles += [w[12 + p], w[16 + p], w[20 + p], w[24 + p]]
        tiles += list(k_tiles(i["w_out_2"][0]))
    if 3 in blocks:
        w = k_tiles(i["w_in_3"][0])
        tiles += [w[16], w[17]]
        for p in range(4):
            tiles += [w[p], w[4 + p], w[8 + p], w[12 + p]]
        tiles += list(k_tiles(i["w_out_3"][0]))
        tiles += mlp_order(k_tiles(i["w_gate_up_3"][0]), down_tiles(i["w_down_3"][0]))
    tiles += [np.zeros((P, KD * P), np.float32)] * 2
    return np.stack(tiles)


def columns(a):
    return np.asarray(a).reshape(-1, P).T


def kernel(**inputs):
    import concourse.bacc as bacc
    from concourse.bass_utils import run_bass_kernel_spmd as run

    i = {k: np.asarray(v) for k, v in inputs.items()}
    vec = {"conv_w0": columns(i["conv_w"][0, 0]), "conv_w1": columns(i["conv_w"][0, 1]),
           "conv_w2": columns(i["conv_w"][0, 2]),
           "dw_w_2": i["dw_w_2"][0].reshape(TAPS, 4, P).transpose(2, 1, 0).reshape(P, 4 * TAPS)}
    arrays = {
        "x_t": i["x"][0].T,
        "vectors": np.concatenate([vec[n] if n in vec else columns(i[n]) for n in VEC], axis=1),
        "common": COMMON,
        "rotary": TABLES["rotary"],
        "retention": TABLES["retention"],
        "seen": TABLES["seen"],
        "onehot": TABLES["onehot"],
        "outside": TABLES["outside"],
        "sgu_w_t": i["sgu_w_s"][0].transpose(0, 2, 1),
        "sgu_b_s": i["sgu_b_s"][0],
        "rpb": i["rpb_2"][0].reshape(NA_HEADS * REL_H, REL_W),
        "sinks": i["sinks_3"],
        "rel_bias": i["rel_bias_3"],
        "weights": weight_stream(i, BLOCKS),
    }
    arrays = {f"in_{k}": np.ascontiguousarray(v) for k, v in arrays.items()}

    def build(counts, last_turn):
        nc = bacc.Bacc("TRN2", target_bir_lowering=False, num_devices=1)
        t = {k[3:]: nc.dram_tensor(k, v.shape, F32, kind="ExternalInput").ap() for k, v in arrays.items()}
        t["out"] = nc.dram_tensor("out_t", (D, S), F32, kind="ExternalOutput").ap()
        for name, shape in (("rel_rows", (NA_HEADS * REL_H, REL_PAD)), ("band_rows", (SWA_HEADS, REL_BAND)),
                            ("rel_copies", (NA_HEADS, GRID_W * REL_H * REL_PAD)),
                            ("band_copies", (SWA_HEADS, CH * REL_BAND))):
            t[name] = nc.dram_tensor(name, shape, F32, kind="Internal").ap()
        return nc, program(nc, t, BLOCKS, counts, last_turn)

    _, dry = build({}, {})
    nc, _ = build(dry.found_counts, dry.found_last)
    r = run(nc, [arrays], core_ids=[0])
    return np.ascontiguousarray(r.results[0]["out_t"].T)[None]
```

```python
from contextlib import ExitStack, contextmanager

import concourse.bass as bass
from concourse import mybir
import numpy as np

ALU = mybir.AluOpType
ACT = mybir.ActivationFunctionType
F32 = mybir.dt.float32
F32R = mybir.dt.float32r
AX_X = mybir.AxisListType.X

P = 128
S = 1024
D = 1024
KD = D // P
HALF = 512
CH = 128
NCH = S // CH
DFF = 2816
NGROUP = DFF // (2 * P)
MASKED = -1e30
SCALE = 64 ** -0.5
EPS = 1e-6
LN_EPS = 1e-5
ALPHA = 2.0 ** 0.25

RET_HEADS = 4
SGU_GROUPS = 4
CONV_TILES = 4
TAPS = 31
PAD = TAPS // 2
PE_TAPS = 7
LAST_PE_TAPS = 3
GRID_W = 64
ROWS = S // GRID_W
KH = 8
KW = 16
NA_HEADS = 8
REL_H = 2 * KH - 1
REL_W = 2 * KW - 1
REL_PAD = 2 * GRID_W
SWA_HEADS = 8
BUCKETS = 32
LN_TOP = 40.0
BAND = 2 * CH
REL_BAND = 384

VEC = {}


def _lay_vectors():
    at = 0
    for name, n in (("mix_norm_g", 8), ("ret_norm_g", 4), ("sgu_ln_g", 4), ("sgu_ln_b", 4),
                    ("ffn_norm_g", 8), ("conv_w0", 44), ("conv_w1", 44), ("conv_w2", 44), ("conv_b", 44),
                    ("final_norm_g", 8), ("ln_g_2", 8), ("b_in_2", 28), ("dw_w_2", 4 * TAPS), ("dw_b_2", 4),
                    ("cln_g_2", 4), ("cln_b_2", 4), ("pw_b_2", 4), ("gn_conv_g_2", 4), ("gn_att_g_2", 4),
                    ("final_g_2", 8), ("ln_in_g_3", 8), ("ln_in_b_3", 8), ("sb_norm_g_3", 4),
                    ("swa_norm_g_3", 4), ("ln1_g_3", 8), ("ln1_b_3", 8), ("ln2_g_3", 8), ("ln2_b_3", 8)):
        VEC[name] = at
        at += n
    return at


NVEC = _lay_vectors()

CONST_COLS = {}


def shape_constants():
    f = np.float32
    i = np.arange(P)
    parts = [
        ("ident", np.eye(P)),
        ("mean1024", np.full((P, P), 1 / 1024)),
        ("mean512", np.full((P, P), 1 / 512)),
        ("mean128", np.full((P, P), 1 / 128)),
        ("mean64", (i[:, None] // 64 == i[None, :] // 64) / 64),
        ("neg_tri", -(i[:, None] >= i[None, :]).astype(f)),
        ("neg_ones", np.full((P, P), -1.0)),
        ("after", (i[:, None] < i[None, :])),
        ("bar_after", np.where(i[:, None] < i[None, :], 0, MASKED)),
        ("tril_t", (i[:, None] <= i[None, :])),
        (f"eps{EPS}", np.full((P, 1), EPS)),
        (f"eps{LN_EPS}", np.full((P, 1), LN_EPS)),
    ]
    at = 0
    for name, a in parts:
        CONST_COLS[name] = at
        at += a.shape[1]
    common = np.concatenate([np.asarray(a, f) for _, a in parts], axis=1)

    half = P // 2
    inv = np.power(f(10000.0), -np.arange(half, dtype=f) / f(half)).astype(f)
    ang = (np.arange(S, dtype=f)[None, :] * inv[:, None]).astype(f)
    rotary = np.stack([np.concatenate([np.cos(ang)] * 2), np.concatenate([np.sin(ang), -np.sin(ang)])], 1)

    pos = np.arange(CH, dtype=np.float64)
    ret = []
    for h in range(RET_HEADS):
        lg = np.log(1.0 - 2.0 ** (-5.0 - h))
        diff = pos[None, :] - pos[:, None]
        scale = P ** -0.5
        mask = np.where(diff >= 0, np.exp(lg * np.maximum(diff, 0)), 0) * scale
        qd = np.broadcast_to(np.exp(lg * (pos + 1))[None, :], (P, CH))
        kd = (np.exp(lg * (CH - 1 - pos)) * scale)[:, None]
        ret.append(np.concatenate([mask, qd, kd, np.full((P, 1), np.exp(lg * CH))], 1))

    w = np.arange(GRID_W)
    start = np.clip(w - KW // 2, 0, GRID_W - KW)
    seen = (w[None, :] >= start[:, None]) & (w[None, :] < start[:, None] + KW)
    cols = np.tile(np.where(seen, 0, MASKED), (2, 1))

    j = np.arange(REL_BAND)
    dist = 255 - j
    exact = BUCKETS // 2
    d = np.maximum(dist, 0)
    large = exact + (np.log(np.maximum(d, 1).astype(f) / exact) / f(np.log(128 / exact)) * exact).astype(np.int32)
    bucket = np.where(d < exact, d, np.minimum(large, BUCKETS - 1))
    inside = (dist >= 0) & (dist < CH)
    onehot = ((np.arange(BUCKETS)[:, None] == bucket[None, :]) & inside[None, :])
    outside = np.broadcast_to(np.where(inside, 0, MASKED)[None, :], (SWA_HEADS, REL_BAND))
    tables = {"rotary": rotary, "retention": np.stack(ret), "seen": cols, "onehot": onehot, "outside": outside}
    return common, {k: np.ascontiguousarray(v, dtype=f) for k, v in tables.items()}


COMMON, TABLES = shape_constants()


class Token:
    def __init__(self, line, count, loop, shift=0):
        self.line, self.count, self.loop, self.shift = line, count, loop, shift


class Line:

    def __init__(self, prog, sem, step=1):
        self.prog, self.sem, self.step, self.count = prog, sem, step, 0
        prog.lines.append(self)
        prog.line_of[sem.name] = self

    def sig(self, ins):
        ins.then_inc(self.sem, self.step)
        self.count += self.step
        return Token(self, self.count, self.prog.loop)


class Loop:
    def __init__(self, name, n, index, starts, per):
        self.name, self.n, self.index, self.starts, self.per, self.open = name, n, index, starts, per, True


class Held:

    def __init__(self, prog, name):
        self.prog, self.name, self.tokens, self.loop = prog, name, [], None
        prog.held.append(self)

    def set(self, *tokens):
        self.tokens, self.loop = list(tokens), self.prog.loop

    def follow(self, *engines):
        loop = self.prog.loop
        for eng in engines:
            eng.wait(*self.tokens)
            if loop is not None and self.loop is not loop:
                for sem, back in self.prog.last_turn.get((loop.name, self.name), []):
                    line = self.prog.line_of[sem]
                    eng.wait(Token(line, loop.starts[line] + back, loop, shift=-1))


class Slot(Held):

    def __init__(self, prog, name, ap):
        super().__init__(prog, name)
        self.ap = ap

    def claim(self, eng):
        self.follow(eng)
        self.set()
        return self.ap

    def free(self, *tokens):
        self.set(*self.tokens, *tokens)


class Engine:

    def __init__(self, prog, eng, sem):
        self.prog, self.e, self.line, self.seen = prog, eng, Line(prog, sem), {}

    def sig(self, ins):
        return self.line.sig(ins)

    def wait(self, *tokens):
        for t in tokens:
            loop = t.loop
            if loop is not None and loop.open:
                per = loop.per.get(t.line.sem.name, 0)
                base = t.count + t.shift * per
                key = (t.line, loop, t.shift)
                if self.seen.get(key, -1) >= t.count:
                    continue
                self.seen[key] = t.count
                if per == 0:
                    self.e.wait_ge(t.line.sem, max(base, 1))
                else:
                    assert base >= 1, (loop.name, t.line.sem.name, base)
                    self.e.wait_ge(t.line.sem, loop.index * per + base)
            else:
                value = t.count
                if loop is not None:
                    value += (loop.n - 1) * loop.per.get(t.line.sem.name, 0)
                if self.seen.get(t.line, 0) >= value:
                    continue
                self.seen[t.line] = value
                self.e.wait_ge(t.line.sem, value)

    def turn_before(self):
        loop = self.prog.loop
        return Token(self.line, loop.starts[self.line], loop)


class Program:
    BUMP = 1024

    def __init__(self, nc, ctx, counts, last_turn):
        self.nc, self.ctx, self.counts, self.last_turn = nc, ctx, counts, last_turn
        self.lines, self.line_of, self.held, self.loop = [], {}, [], None
        self.found_counts, self.found_last = {}, {}
        self.pe, self.act, self.dve, self.pool, self.sp = (
            Engine(self, e, self.sem(n)) for e, n in (
                (nc.tensor, "pe_done"), (nc.scalar, "act_done"), (nc.vector, "dve_done"),
                (nc.gpsimd, "pool_done"), (nc.sync, "sp_done")))
        for eng in (self.pe, self.act, self.dve, self.pool):
            eng.e.sem_inc(eng.line.sem, self.BUMP)
            eng.line.count = self.BUMP

    def sem(self, name):
        return self.ctx.enter_context(self.nc.semaphore(name))

    def dma_line(self, name):
        line = Line(self, self.sem(name), 16)
        self.nc.sync.sem_inc(line.sem, self.BUMP)
        line.count = self.BUMP
        return line

    def slot(self, name, ap):
        return Slot(self, name, ap)

    @contextmanager
    def repeat(self, name, n):
        starts = {x: x.count for x in self.lines}
        with self.nc.Fori(0, n) as index:
            self.loop = Loop(name, n, index, starts, self.counts.get(name, {}))
            loop = self.loop
            yield index
            self.loop = None
        per = {x.sem.name: x.count - starts[x] for x in self.lines}
        assert not self.counts or per == self.counts[name], name
        self.found_counts[name] = per
        loop.per, loop.open = per, False
        for s in self.held:
            mine = [t for t in s.tokens if t.loop is loop]
            if mine:
                self.found_last[(name, s.name)] = [(t.line.sem.name, t.count - starts[t.line]) for t in mine]
        for x in self.lines:
            x.count = starts[x] + n * per[x.sem.name]
        for eng in (self.pe, self.act, self.dve, self.pool, self.sp):
            eng.seen = {}

    def meet(self):
        self.nc.all_engine_barrier()


class Norm:

    def __init__(self, prog, ctx, name, ones, eps, n, centred=False, memory=None):
        self.b, self.name, self.ones, self.eps, self.n, self.centred = prog, name, prog.c(ones), eps, n, centred
        if memory is None:
            memory = [ctx.enter_context(prog.nc.sbuf_tensor(f"{name}_{x}", [P, S], F32))[:]
                      for x in ("acc", "rstd", "buf0", "buf1")]
        self.acc, self.rstd = memory[:2]
        self.buf = [prog.slot(f"{name}_buf{i}", memory[2 + i]) for i in range(2)]
        self.k, self.mean, self.last = 0, None, Held(prog, f"{name}_last")

    def gather(self, tile, token, on_pe=False):
        if self.centred:
            if on_pe:
                self.sum_on_pe(tile, token)
            else:
                self.sum_on_dve(tile, token, self.k == 0)
        else:
            self.square(tile, token, on_pe)
        self.k += 1

    def square(self, tile, token, on_pe):
        act = self.b.act
        act.wait(token)
        if on_pe:
            buf = self.buf[self.k % 2]
            q = act.sig(act.e.activation(buf.claim(act), tile, ACT.Square))
            buf.free(self.sum_on_pe(buf.ap, q))
        elif self.k == 0:
            self.last.set(act.sig(act.e.activation(self.acc, tile, ACT.Square)))
        else:
            buf = self.buf[self.k % 2]
            q = act.sig(act.e.activation(buf.claim(act), tile, ACT.Square))
            buf.free(self.sum_on_dve(buf.ap, q, False))

    def sum_on_dve(self, src, token, first):
        dve = self.b.dve
        dve.wait(token)
        self.last.follow(dve)
        if first:
            t = dve.sig(dve.e.tensor_copy(self.acc, src))
        else:
            t = dve.sig(dve.e.tensor_tensor(self.acc, self.acc, src, ALU.add))
        self.last.set(t)
        return t

    def sum_on_pe(self, src, token):
        pe = self.b.pe
        if self.k == 0:
            self.mean_done = [None, None]
            self.mean = self.b.next_wide()
            self.mean.claim(pe)
        pe.wait(token)
        for half in range(2):
            s = slice(half * HALF, (half + 1) * HALF)
            self.mean_done[half] = pe.sig(pe.e.matmul(self.mean.ap[:, s], self.ones, src[:, s],
                                                      start=(self.k == 0), stop=(self.k == self.n - 1)))
        return self.mean_done[1]

    def means(self):
        if self.mean is None:
            self.last.follow(self.b.pe)
            self.mean, self.mean_done = self.b.column_mean(self.ones, self.acc)
        mean, self.mean = self.mean, None
        return mean, self.mean_done

    def start(self, tiles):
        act, dve = self.b.act, self.b.dve
        mean, done = self.means()
        if self.centred:
            dve.wait(*done)
            self.k = 0
            for tile in tiles:
                last = dve.sig(dve.e.tensor_tensor(tile, tile, mean.ap, ALU.subtract))
                self.square(tile, last, True)
                self.k += 1
            mean.free(last)
            mean, done = self.means()
        self.rstd_ready = self.b.rsqrt_of(mean, done, self.rstd, self.eps)

    def scale(self, tile, dst, gain, k):
        dve = self.b.dve
        cuts = [0, S] if self.rstd_ready is None else [0, HALF, S]
        for n in range(len(cuts) - 1):
            s = slice(cuts[n], cuts[n + 1])
            if self.rstd_ready is not None:
                dve.wait(self.rstd_ready[n])
            t = dve.sig(dve.e.scalar_tensor_tensor(dst[:, s], tile[:, s], self.b.v(gain, k), self.rstd[:, s],
                                                   ALU.mult, ALU.mult))
        self.rstd_ready = None
        return t

    def in_place(self, tiles, gain, bias=None, func=ACT.Identity):
        act = self.b.act
        self.start(tiles)
        for k, tile in enumerate(tiles):
            t = self.scale(tile, tile, gain, k)
            if bias is not None:
                act.wait(t)
                t = act.sig(act.e.activation(tile, tile, func, bias=self.b.v(bias, k)))
            yield k, tile, t

    def split_one(self, tile, gain, k, hi, lo):
        return self.b.split(tile, hi, lo, self.scale(tile, tile, gain, k))

    def split_to(self, tiles, gain, out):
        act, dve = self.b.act, self.b.dve
        self.start(tiles)
        pairs, before = [], None

        def low(buf, hi, lo, h):
            dve.wait(h)
            t = dve.sig(dve.e.tensor_tensor(lo, buf.ap, hi.bitcast(F32), ALU.subtract))
            buf.free(t)
            pairs.append((h, t))

        for k, tile in enumerate(tiles):
            buf = self.buf[k % 2]
            n = self.scale(tile, buf.claim(dve), gain, k)
            hi, lo = out(k)
            act.wait(n)
            h = act.sig(act.e.activation(hi, buf.ap, ACT.Copy))
            if before:
                low(*before)
            before = (buf, hi, lo, h)
        low(*before)
        return pairs

    def split_and_keep(self, tiles, gain, bias, out, keep_scale=1.0, keep_bias=None):
        act, dve, b = self.b.act, self.b.dve, self.b
        self.start(tiles)
        pairs, before = [], None

        def low(k, hi, lo, h):
            dve.wait(h)
            t = dve.sig(dve.e.scalar_tensor_tensor(lo, tiles[k], b.v(bias, k), hi.bitcast(F32), ALU.add, ALU.subtract))
            pairs.append((h, t))
            act.wait(t)
            act.sig(act.e.activation(tiles[k], tiles[k], ACT.Identity, scale=keep_scale,
                                     bias=b.v(bias, k) if keep_bias is None else keep_bias[:, k:k + 1]))

        for k, tile in enumerate(tiles):
            n = self.scale(tile, tile, gain, k)
            hi, lo = out(k)
            act.wait(n)
            h = act.sig(act.e.activation(hi, tile, ACT.Identity, bias=b.v(bias, k)))
            if before:
                low(*before)
            before = (k, hi, lo, h)
        low(*before)
        b.kept = Token(act.line, act.line.count, None)
        return pairs


class Blocks(Program):
    def setup(self, t, blocks):
        nc, ctx = self.nc, self.ctx
        self.t = t
        self.blocks = blocks

        def sb(name, shape, dt=F32):
            return ctx.enter_context(nc.sbuf_tensor(name, shape, dt))

        self.x = sb("residual", [P, KD, S])
        self.h_hi = sb("h_hi", [P, KD, S], F32R)
        self.h_lo = sb("h_lo", [P, KD, S], F32R)
        self.vec = sb("vectors", [P, NVEC])
        self.common = sb("common", [P, COMMON.shape[1]])
        raw = sb("w_raw", [P, 2, KD * P])
        whi = sb("w_hi", [P, 2, KD * P], F32R)
        wlo = sb("w_lo", [P, 2, KD * P], F32R)
        self.w_raw = [self.slot(f"w_raw{i}", raw[:, i, :]) for i in range(2)]
        self.w_split = [self.slot(f"w_split{i}", (whi[:, i, :], wlo[:, i, :])) for i in range(2)]
        self.w_line = [self.dma_line(f"w_loaded{i}") for i in range(2)]
        self.aux = {}
        psum = ctx.enter_context(nc.psum_tensor("psum", [P, 8, HALF], F32))
        self.psum = psum
        two = lambda b: psum[:, b:b + 2, :].rearrange("p b n -> p (b n)")
        self.acc = [self.slot(f"acc{i}", two(2 * i)) for i in range(2)]
        self.wide = [self.slot(f"wide{i}", two(4 + 2 * i)) for i in range(2)]
        self.bank = [self.slot(f"bank{i}", psum[:, i, :]) for i in range(8)]
        self.n_acc = self.n_wide = 0
        self.w_loaded = [Held(self, f"w_loaded{i}") for i in range(2)]
        self.w_ready = [Held(self, f"w_ready{i}") for i in range(2)]
        self.tile_no, self.tile_base = 0, 0
        sp = self.sp
        self.fetch("start", self.common[:], t["common"])
        started = self.fetch("start", self.vec[:], t["vectors"])
        x = t["x_t"].rearrange("(c p) s -> p c s", p=P)
        self.x_loaded = [self.fetch(f"x{k}", self.x[:, k, :], x[:, k, :]) for k in range(KD)]
        for eng in (self.pe, self.act, self.dve, self.pool):
            eng.wait(started)
        self.end_norm = None
        self.w_load(0)
        self.w_load(1)
        self.w_split_tile(0)
        self.rows_put = []

    def fetch(self, name, dst, src):
        return self.line_for(name).sig(self.sp.e.dma_start(dst, src))

    def line_for(self, name):
        if name not in self.aux:
            self.aux[name] = self.dma_line(f"{name}_loaded")
        return self.aux[name]

    def c(self, name, n=P):
        at = CONST_COLS[name]
        return self.common[:, at:at + n]

    def v(self, name, i=0):
        at = VEC[name] + i
        return self.vec[:, bass.ds(at, 1)]

    def load_biases(self, spare):
        sp, pool, t = self.sp, self.pool, self.t
        padded = spare[0:NA_HEADS * REL_H, 0:REL_PAD]
        sp.wait(pool.sig(pool.e.memset(padded, 0.0)))
        off = GRID_W - KW
        padded_loaded = self.fetch("rpb", padded[:, off:off + REL_W], t["rpb"])
        at = REL_PAD
        onehot = spare[0:BUCKETS, at:at + REL_BAND]
        band = spare[0:SWA_HEADS, at + REL_BAND:at + 2 * REL_BAND]
        rel = spare[0:BUCKETS, at + 2 * REL_BAND:at + 2 * REL_BAND + SWA_HEADS]
        self.fetch("swa", rel, t["rel_bias"])
        self.fetch("swa", onehot, t["onehot"])
        got = self.fetch("swa", band, t["outside"])
        sp.wait(padded_loaded)
        self.rows_put = [self.fetch("rel_rows", t["rel_rows"], padded)]
        self.bias_parts = onehot, band, rel, got

    def bias_rows(self):
        sp, pe, dve, t = self.sp, self.pe, self.dve, self.t
        onehot, band, rel, got = self.bias_parts
        pe.wait(got)
        b = self.next_wide()
        done = pe.sig(pe.e.matmul(b.claim(pe)[0:SWA_HEADS, 0:REL_BAND], rel, onehot, start=True, stop=True))
        dve.wait(done, got)
        line = dve.sig(dve.e.tensor_tensor(band, band, b.ap[0:SWA_HEADS, 0:REL_BAND], ALU.add))
        b.free(line)
        self.next_wide()
        sp.wait(line)
        self.rows_put.append(self.fetch("band_rows", t["band_rows"], band))
        sp.wait(*self.rows_put)
        self.line_for("rel_copies")
        self.line_for("band_copies")

    def bias_copies(self, pair):
        t = self.t
        rows = t["rel_rows"].rearrange("(h r) w -> h (r w)", r=REL_H)
        for a in range(2):
            h = pair * 2 + a
            self.fetch("rel_copies", t["rel_copies"][bass.ds(h, 1), :].rearrange("h (q n) -> (h q) n", q=GRID_W),
                       rows[bass.ds(h, 1), :].broadcast_to([GRID_W, REL_H * REL_PAD]))
            self.fetch("band_copies", t["band_copies"][bass.ds(h, 1), :].rearrange("h (q n) -> (h q) n", q=CH),
                       t["band_rows"][bass.ds(h, 1), :].broadcast_to([CH, REL_BAND]))

    def biases_alone(self, y):
        if 1 not in self.blocks and not self.rows_put:
            self.load_biases(y[:, KD - 1, :])
            self.bias_rows()
            for pair in range(NA_HEADS // 2):
                self.bias_copies(pair)
            self.pe.wait(self.dve_now())

    def copies_done(self, name):
        line = self.aux[name]
        self.sp.wait(Token(line, line.count, None))

    def w_load(self, ahead_no):
        slot = self.w_raw[ahead_no % 2]
        slot.claim(self.sp)
        no = ahead_no
        if self.loop is not None:
            no = ahead_no + self.loop.index * self.w_turn
        src = self.t["weights"][bass.ds(no, 1), :, :].rearrange("a p n -> (a p) n") if self.loop is not None \
            else self.t["weights"][no, :, :]
        self.w_loaded[ahead_no % 2].set(self.w_line[ahead_no % 2].sig(self.sp.e.dma_start(slot.ap, src)))

    def w_split_tile(self, no):
        raw, out = self.w_raw[no % 2], self.w_split[no % 2]
        hi, lo = out.claim(self.act)
        self.w_loaded[no % 2].follow(self.act)
        a = self.act.sig(self.act.e.activation(hi, raw.ap, ACT.Copy))
        self.dve.wait(a)
        b = self.dve.sig(self.dve.e.tensor_tensor(lo, raw.ap, hi.bitcast(F32), ALU.subtract))
        raw.free(b)
        self.w_ready[no % 2].set(a, b)

    @contextmanager
    def w_turns(self, name, n, tiles):
        assert tiles % 2 == 0
        self.w_turn = tiles
        before = self.tile_no
        with self.repeat(name, n) as i:
            yield i
            assert self.tile_no == before + tiles, (name, self.tile_no - before)
        self.tile_no = before + n * tiles

    def next_tile(self):
        t = self.tile_no
        self.w_split_tile(t + 1)
        slot = self.w_split[t % 2]
        self.w_ready[t % 2].follow(self.pe)
        self.w_load(t + 2)
        self.tile_no = t + 1
        return slot

    def gemm(self, slot_out, tile, n_k, cols, lo_col, src, ready=None):
        pe = self.pe
        out = slot_out.claim(pe)
        hi, lo = (a.rearrange("p (k n) -> p k n", n=cols) for a in tile.ap)
        for k in range(n_k):
            for part, (w, x) in enumerate(((hi, src(k, 0)), (lo, src(k, 0)), (hi, src(k, 1)))):
                if ready is not None and part != 1:
                    pe.wait(ready[k][part // 2])
                for half in range(2):
                    s = slice(half * HALF, (half + 1) * HALF)
                    ins = pe.e.matmul(out[:, s], w[:, k, lo_col:lo_col + P], x[:, s],
                                      start=(k == 0 and part == 0), stop=(k == n_k - 1 and part == 2))
        return pe.sig(ins)

    def next_acc(self):
        self.n_acc += 1
        return self.acc[(self.n_acc - 1) % 2]

    def next_wide(self):
        self.n_wide += 1
        return self.wide[(self.n_wide - 1) % 2]

    def project(self, ready=None):
        tile = self.next_tile()
        acc = self.next_acc()
        done = self.gemm(acc, tile, KD, P, 0, lambda k, part: (self.h_lo if part else self.h_hi)[:, k, :], ready)
        tile.free(done)
        return acc, done

    def prepare_pair(self):
        t = self.tile_no
        self.w_split_tile(t + 1)
        self.w_load(t + 2)
        self.w_load(t + 3)

    def project_pair(self, ready):
        pe, t = self.pe, self.tile_no
        tiles = [self.w_split[(t + j) % 2] for j in range(2)]
        accs = [self.next_acc() for j in range(2)]
        for j in range(2):
            self.w_ready[(t + j) % 2].follow(pe)
            accs[j].claim(pe)
        done = [None, None]
        together = KD - 3
        order = [(k, j) for k in range(together) for j in range(2)]
        order += [(k, j) for j in range(2) for k in range(together, KD)]
        for k, j in order:
            hi, lo = (a[:, k * P:(k + 1) * P] for a in tiles[j].ap)
            for part, (w, x) in enumerate(((hi, self.h_hi), (lo, self.h_hi), (hi, self.h_lo))):
                if part != 1:
                    pe.wait(ready[k][part // 2])
                for half in range(2):
                    s = slice(half * HALF, (half + 1) * HALF)
                    ins = pe.e.matmul(accs[j].ap[:, s], w, x[:, k, s],
                                      start=(k == 0 and part == 0), stop=(k == KD - 1 and part == 2))
            if k == KD - 1:
                done[j] = pe.sig(ins)
                tiles[j].free(done[j])
        self.w_split_tile(t + 2)
        self.tile_no = t + 2
        return [(accs[j], done[j]) for j in range(2)]

    def column_mean(self, ones, src, token=None, w=None):
        w = w or self.next_wide()
        out = w.claim(self.pe)
        if token is not None:
            self.pe.wait(token)
        done = []
        for half in range(2):
            s = slice(half * HALF, (half + 1) * HALF)
            done.append(self.pe.sig(self.pe.e.matmul(out[:, s], ones, src[:, s], start=True, stop=True)))
        return w, done

    def rsqrt_of(self, w, done, out, eps):
        act = self.act
        act.e.preload_act_table_set("natural_log_exp_and_others")
        if isinstance(out, Slot):
            out = out.claim(act)
        res = []
        for half in range(2):
            s = slice(half * HALF, (half + 1) * HALF)
            act.wait(done[half])
            ln = act.sig(act.e.activation(out[:, s], w.ap[:, s], ACT.Ln, bias=self.c(f"eps{eps}", 1)))
            act.wait(ln)
            res.append(act.sig(act.e.activation(out[:, s], out[:, s], ACT.Exp, scale=-0.5)))
        w.free(ln)
        return res

    def split(self, src, hi, lo, token):
        self.act.wait(token)
        a = self.act.sig(self.act.e.activation(hi, src, ACT.Copy))
        self.dve.wait(a)
        b = self.dve.sig(self.dve.e.tensor_tensor(lo, src, hi.bitcast(F32), ALU.subtract))
        return (a, b)

    def norm(self, ctx, name, ones, eps, n, centred=False):
        return Norm(self, ctx, name, ones, eps, n, centred)

    def x_tiles(self):
        return [self.x[:, k, :] for k in range(KD)]

    @contextmanager
    def scope(self, name, meet=True):
        with ExitStack() as ctx:
            yield lambda n, shape, dt=F32: ctx.enter_context(self.nc.sbuf_tensor(f"{name}_{n}", shape, dt))
            if meet:
                self.meet()

    def h(self, k):
        return self.h_hi[:, k, :], self.h_lo[:, k, :]

    def mix_out(self, name, alpha, ready, norm):
        def add(x, acc, done):
            self.dve.wait(done)
            t = self.dve.sig(self.dve.e.scalar_tensor_tensor(x, x, alpha, acc.ap, ALU.mult, ALU.add))
            acc.free(t)
            norm.gather(x, t)

        for j, (acc, done) in enumerate(self.project_pair(ready)):
            add(self.x[:, j, :], acc, done)
        with self.w_turns(f"{name}_out", KD // 2 - 1, 2) as i:
            for j in range(2):
                acc, done = self.project()
                add(self.x[:, i * 2 + 2 + j, :], acc, done)

    def mlp(self, name, conv, norm):
        act, dve, pe = self.act, self.dve, self.pe
        with self.scope(name, meet=False) as sb:
            act_hi = sb("act_hi", [P, 2, S], F32R)
            act_lo = sb("act_lo", [P, 2, S], F32R)
            hid = [self.slot(f"{name}_hid{j}", (act_hi[:, j, :], act_lo[:, j, :])) for j in range(2)]
            ta = self.slot(f"{name}_ta", sb("ta", [P, S])[:])
            tb = self.slot(f"{name}_tb", sb("tb", [P, S])[:])
            tp = self.slot(f"{name}_tp", sb("tp", [P, S])[:])
            state = {}
            hid_ready = [Held(self, f"{name}_hid_ready{j}") for j in range(2)]

            def taps(dst, acc, done, channel):
                act.wait(done)
                y = dst.claim(act)
                t = act.sig(act.e.activation(y, acc.ap, ACT.Identity, bias=self.v("conv_b", channel),
                                             scale=self.v("conv_w2", channel)))
                for back, w in ((1, "conv_w1"), (2, "conv_w0")):
                    yield
                    dve.wait(t)
                    t = dve.sig(dve.e.scalar_tensor_tensor(y[:, back:S], acc.ap[:, 0:S - back], self.v(w, channel),
                                                           y[:, back:S], ALU.mult, ALU.add))
                acc.free(t)
                state[dst] = t

            def gate_steps(channel, acc, done):
                if conv:
                    yield from taps(ta, acc, done, channel)
                    yield
                    act.wait(state[ta])
                    state["a"] = act.sig(act.e.activation(ta.ap, ta.ap, ACT.Silu))
                else:
                    act.wait(done)
                    state["a"] = act.sig(act.e.activation(ta.claim(act), acc.ap, ACT.Silu))
                    acc.free(state["a"])

            def gate(channel, given=None):
                for _ in gate_steps(channel, *(given or self.project())):
                    pass

            def up(channel, j, given=None):
                acc, done = given or self.project()
                if conv:
                    for _ in taps(tb, acc, done, channel + DFF // P):
                        pass
                    t, src = state[tb], tb.ap
                else:
                    t, src = done, acc.ap
                dve.wait(t, state["a"])
                out = tp.claim(dve)
                m = dve.sig(dve.e.tensor_tensor(out, ta.ap, src, ALU.mult))
                ta.free(m)
                (tb if conv else acc).free(m)
                hi, lo = hid[j].claim(act)
                pair = self.split(out, hi, lo, m)
                tp.free(*pair)
                hid_ready[j].set(*pair)

            def down(last=False, between=iter(())):
                hid_ready[0].follow(pe)
                hid_ready[1].follow(pe)
                for half in range(2):
                    tile = self.next_tile()
                    for n in range(4):
                        w = self.next_wide()
                        done = self.gemm(w, tile, 2, 4 * P, n * P,
                                         lambda k, part: (act_lo if part else act_hi)[:, k, :])
                        x = self.x[:, half * 4 + n, :]
                        dve.wait(done)
                        t = dve.sig(dve.e.tensor_tensor(x, x, w.ap, ALU.add))
                        w.free(t)
                        if last:
                            norm.gather(x, t)
                        next(between, None)
                    tile.free(done)
                hid[0].free(done)
                hid[1].free(done)

            first = self.project_pair(self.h_ready)
            gate(0, first[0])
            up(0, 0, first[1])
            gate(1)
            up(1, 1)
            with self.w_turns(name, NGROUP - 1, 6) as i:
                steps = gate_steps(i * 2 + 2, *self.project())
                next(steps, None)
                down(between=steps)
                up(i * 2 + 2, 0)
                gate(i * 2 + 3)
                up(i * 2 + 3, 1)
            down(last=True)

    def first(self):
        x = self.x_tiles()
        with ExitStack() as ctx:
            n1 = self.norm(ctx, "norm1", "mean1024", EPS, KD)
            for k in range(KD):
                n1.gather(x[k], self.x_loaded[k], on_pe=True)
            self.prepare_pair()
            self.h_ready = n1.split_to(x, "mix_norm_g", self.h)
        y = self.ctx_y("y1")
        self.retention_and_sgu(y)
        ready = self.split_y(y)
        with ExitStack() as ctx:
            n2 = self.norm(ctx, "norm2", "mean1024", EPS, KD)
            self.mix_out("mix1", 1.0, ready, n2)
            self.prepare_pair()
            self.h_ready = n2.split_to(x, "ffn_norm_g", self.h)
        self.end_norm = self.norm_with_its_memory("norm3", "mean1024", EPS, KD)
        self.mlp("mlp1", True, self.end_norm)

    def norm_with_its_memory(self, *args, **kw):
        ctx = ExitStack()
        n = self.norm(ctx, *args, **kw)
        n.close = ctx.close
        return n

    def split_y(self, y):
        self.prepare_pair()
        ready = [self.split(y[:, k, :], *self.h(k), self.dve_now()) for k in range(KD)]
        self.close_y()
        return ready

    def dve_now(self):
        return Token(self.dve.line, self.dve.line.count, None)

    def ctx_y(self, name):
        self.y_ctx = ExitStack()
        return self.y_ctx.enter_context(self.nc.sbuf_tensor(name, [P, KD, S], F32))

    def close_y(self):
        self.y_ctx.close()

    def transposes(self, w, src, token=None, n=NCH, step=CH, first=0):
        pe = self.pe
        out = w.claim(pe)
        if token is not None:
            pe.wait(token)
        for b in range(n):
            at = (first + b) * step
            ins = pe.e.transpose(out[:, b * P:(b + 1) * P], src[:, at:at + P], self.c("ident"))
        return pe.sig(ins)

    def retention_and_sgu(self, y):
        act, dve, pe, sp = self.act, self.dve, self.pe, self.sp
        with self.scope("ret") as sb:
            rot = sb("rotary", [P, 2, S])
            table = self.slot("ret_table", sb("table", [P, 2 * P + 2])[:])
            mask, qdec = table.ap[:, 0:P], table.ap[:, P:2 * P]
            kdec, cdec = table.ap[:, 2 * P:2 * P + 1], table.ap[:, 2 * P + 1:2 * P + 2]
            mixer = self.slot("sgu_mixer", sb("mixer", [P, 2, CH])[:])
            w_t, b_s = mixer.ap[:, 0, :], mixer.ap[:, 1, :]
            q, k, t, qd, gate, st, vtok, ktok, sT = (
                self.slot(f"ret_{n}", sb(n, [P, S])[:])
                for n in ("q", "k", "t", "qd", "gate", "state", "vtok", "ktok", "sT"))
            dve.wait(self.fetch("rotary", rot[:], self.t["rotary"]))
            self.line_for("ret_table")
            self.line_for("sgu_mixer")
            chunks = lambda a: a.rearrange("p (n c) -> p n c", c=CH)
            wide = lambda a: a.unsqueeze(1).broadcast_to([P, NCH, CH])
            q_ready, k_ready = Held(self, "ret_q_ready"), Held(self, "ret_k_ready")
            u_ready, v_ready = Held(self, "sgu_u_ready"), Held(self, "sgu_v_ready")

            def rotary(dst, ready, acc, done):
                dve.wait(done)
                turned = t.claim(dve)
                dve.sig(dve.e.tensor_tensor(turned[0:64, :], acc.ap[64:P, :], rot[64:P, 1, :], ALU.mult))
                dve.sig(dve.e.tensor_tensor(turned[64:P, :], acc.ap[0:64, :], rot[0:64, 1, :], ALU.mult))
                c = dve.sig(dve.e.tensor_tensor(dst.claim(dve), acc.ap, rot[:, 0, :], ALU.mult))
                acc.free(c)
                dve.wait(c)
                d = dve.sig(dve.e.tensor_tensor(dst.ap, dst.ap, turned, ALU.add))
                t.free(d)
                dst.free(d)
                ready.set(d)

            def gelu(dst, ready, acc, done):
                act.wait(done)
                d = act.sig(act.e.activation(dst.claim(act), acc.ap, ACT.Gelu))
                acc.free(d)
                dst.free(d)
                ready.set(d)

            def head_turn(head, next_first, next_second):
                table.claim(sp)
                got_table = self.fetch("ret_table", table.ap, self.t["retention"][bass.ds(head, 1), :, :]
                                       .rearrange("a p n -> (a p) n"))
                self.bias_copies(head)
                acc, done = self.project()
                act.wait(done)
                v_raw = act.sig(act.e.activation(t.claim(act), acc.ap, ACT.Copy))
                acc.free(v_raw)
                k_ready.follow(pe)
                w = self.next_wide()
                tr = self.transposes(w, k.ap)
                act.wait(tr, got_table)
                k_tok = act.sig(act.e.activation(ktok.claim(act), w.ap, ACT.Copy, scale=kdec))
                w.free(k_tok)
                q_ready.follow(pe, dve)
                w = self.next_wide()
                out = w.claim(pe)
                for n in range(NCH):
                    c = slice(n * CH, (n + 1) * CH)
                    ins = pe.e.matmul(out[:, c], k.ap[:, c], q.ap[:, c], start=True, stop=True)
                s_done = pe.sig(ins)
                k.free(s_done)
                dve.wait(s_done, got_table)
                s_mask = dve.sig(dve.e.tensor_tensor(chunks(sT.claim(dve)), chunks(w.ap), wide(mask), ALU.mult))
                w.free(s_mask)
                q_dec = dve.sig(dve.e.tensor_tensor(chunks(qd.claim(dve)), chunks(q.ap), wide(qdec), ALU.mult))
                q.free(s_done, q_dec)
                w = self.next_wide()
                tr = self.transposes(w, t.ap, v_raw)
                t.free(tr)
                act.wait(tr)
                v_tok = act.sig(act.e.activation(vtok.claim(act), w.ap, ACT.Copy))
                w.free(v_tok)
                acc, done = self.project()
                act.wait(done)
                g_silu = act.sig(act.e.activation(gate.claim(act), acc.ap, ACT.Silu))
                acc.free(g_silu)
                w = self.next_wide()
                out = w.claim(pe)
                pe.wait(v_tok, k_tok)
                for n in range(NCH - 1):
                    c = slice(n * CH, (n + 1) * CH)
                    ins = pe.e.matmul(out[:, c], ktok.ap[:, c], vtok.ap[:, c], start=True, stop=True)
                kv = pe.sig(ins)
                ktok.free(kv)
                dve.wait(kv)
                state = st.claim(dve)
                last = dve.sig(dve.e.tensor_copy(state[:, CH:2 * CH], w.ap[:, 0:CH]))
                for n in range(2, NCH):
                    dve.wait(last)
                    last = dve.sig(dve.e.scalar_tensor_tensor(
                        state[:, n * CH:(n + 1) * CH], state[:, (n - 1) * CH:n * CH], cdec,
                        w.ap[:, (n - 1) * CH:n * CH], ALU.mult, ALU.add))
                w.free(last)
                table.free(last, k_tok)
                next_first()
                w = self.next_wide()
                out = w.claim(pe)
                pe.wait(s_mask, q_dec, last)
                for n in range(NCH):
                    c = slice(n * CH, (n + 1) * CH)
                    ins = pe.e.matmul(out[:, c], vtok.ap[:, c], sT.ap[:, c], start=True, stop=(n == 0))
                    if n:
                        ins = pe.e.matmul(out[:, c], state[:, c], qd.ap[:, c], start=False, stop=True)
                o_done = pe.sig(ins)
                for b in (vtok, sT, qd, st):
                    b.free(o_done)
                act.wait(o_done)
                sq = act.sig(act.e.activation(sT.claim(act), w.ap, ACT.Square))
                dve.wait(sq)
                o = dve.sig(dve.e.tensor_scalar(y[:, head, :], w.ap, self.v("ret_norm_g", head), None, ALU.mult))
                w.free(sq, o)
                next_second()
                w, m = self.column_mean(self.c("mean128"), sT.ap, sq)
                sT.free(m[-1])
                r = self.rsqrt_of(w, m, st, EPS)
                dve.wait(*r, o)
                n1 = dve.sig(dve.e.tensor_tensor(y[:, head, :], y[:, head, :], st.ap, ALU.mult))
                st.free(n1)
                dve.wait(n1, g_silu)
                gate.free(dve.sig(dve.e.tensor_tensor(y[:, head, :], y[:, head, :], gate.ap, ALU.mult)))

            def group_turn(g, next_first=None, next_second=None):
                mixer.claim(sp)
                self.fetch("sgu_mixer", w_t, self.t["sgu_w_t"][bass.ds(g, 1), :, :].rearrange("a s t -> (a s) t"))
                loaded = self.fetch("sgu_mixer", b_s, self.t["sgu_b_s"][bass.ds(g, 1), :].broadcast_to([P, CH]))
                v_ready.follow(pe, dve)
                w, m = self.column_mean(self.c("mean128"), k.ap)
                dve.wait(*m)
                cent = dve.sig(dve.e.tensor_tensor(k.ap, k.ap, w.ap, ALU.subtract))
                w.free(cent)
                act.wait(cent)
                sq = act.sig(act.e.activation(sT.claim(act), k.ap, ACT.Square))
                if next_first:
                    first = self.project()
                w, m = self.column_mean(self.c("mean128"), sT.ap, sq)
                sT.free(m[-1])
                r = self.rsqrt_of(w, m, st, EPS)
                dve.wait(*r)
                n1 = dve.sig(dve.e.scalar_tensor_tensor(k.ap, k.ap, self.v("sgu_ln_g", g), st.ap, ALU.mult, ALU.mult))
                st.free(n1)
                act.wait(n1)
                vn = act.sig(act.e.activation(k.ap, k.ap, ACT.Identity, bias=self.v("sgu_ln_b", g)))
                dve.wait(loaded)
                wm = dve.sig(dve.e.tensor_tensor(w_t, w_t, self.c("tril_t"), ALU.mult))
                if next_second:
                    second = self.project()
                w = self.next_wide()
                tr = self.transposes(w, k.ap, vn)
                k.free(tr)
                act.wait(tr)
                vt = act.sig(act.e.activation(vtok.claim(act), w.ap, ACT.Copy))
                w.free(vt)
                if next_second:
                    next_second(*second)
                w = self.next_wide()
                out = w.claim(pe)
                pe.wait(vt, wm)
                for n in range(NCH):
                    c = slice(n * CH, (n + 1) * CH)
                    ins = pe.e.matmul(out[:, c], vtok.ap[:, c], w_t, start=True, stop=True)
                mixed = pe.sig(ins)
                vtok.free(mixed)
                dve.wait(mixed)
                b = dve.sig(dve.e.tensor_tensor(chunks(t.claim(dve)), chunks(w.ap), wide(b_s), ALU.add))
                w.free(b)
                mixer.free(b)
                u_ready.follow(dve)
                dve.wait(b)
                last = dve.sig(dve.e.tensor_tensor(y[:, g + RET_HEADS, :], t.ap, q.ap, ALU.mult))
                t.free(last)
                q.free(last)
                if next_first:
                    next_first(*first)

            self.load_biases(y[:, KD - 1, :])
            first, second = self.project_pair(self.h_ready)
            rotary(q, q_ready, *first)
            rotary(k, k_ready, *second)
            self.bias_rows()
            with self.w_turns("ret", RET_HEADS - 1, 4) as head:
                head_turn(head, lambda: rotary(q, q_ready, *self.project()), lambda: rotary(k, k_ready, *self.project()))
            head_turn(RET_HEADS - 1, lambda: gelu(q, u_ready, *self.project()), lambda: gelu(k, v_ready, *self.project()))
            with self.w_turns("sgu", SGU_GROUPS - 1, 2) as g:
                group_turn(g, lambda *p: gelu(q, u_ready, *p), lambda *p: gelu(k, v_ready, *p))
            group_turn(SGU_GROUPS - 1)

    def second(self):
        x = self.x_tiles()
        with ExitStack() as ctx:
            n4 = self.norm(ctx, "norm4", "mean1024", EPS, KD)
            for k, tile, t in self.block_input("final_norm_g"):
                n4.gather(tile, t, on_pe=True)
            self.prepare_pair()
            self.h_ready = n4.split_to(x, "ln_g_2", self.h)
        self.close_end_norm()
        y = self.ctx_y("y2")
        self.biases_alone(y)
        self.conformer(y)
        self.neighbourhood(y)
        ready = self.split_y(y)
        self.end_norm = self.norm_with_its_memory("norm5", "mean1024", EPS, KD)
        self.mix_out("mix2", 1.0, ready, self.end_norm)

    def block_input(self, gain, bias=None):
        if self.end_norm is not None:
            yield from self.end_norm.in_place(self.x_tiles(), gain, bias)
        else:
            yield from ((k, tile, self.x_loaded[k]) for k, tile in enumerate(self.x_tiles()))

    def close_end_norm(self):
        if self.end_norm is not None:
            self.end_norm.close()
            self.end_norm = None

    def conformer(self, y):
        act, dve, pe, sp = self.act, self.dve, self.pe, self.sp
        with self.scope("conv", meet=False) as sb:
            u = self.slot("conv_u", sb("u", [P, S + 2 * PAD])[:])
            part = sb("part", [P, S])[:]
            diags = self.slot("conv_diags", sb("diags", [P, PE_TAPS, P])[:])
            ga = self.slot("conv_ga", sb("ga", [P, S])[:])
            gb = self.slot("conv_gb", sb("gb", [P, S])[:])
            z1 = dve.sig(dve.e.memset(u.ap[:, 0:PAD], 0.0))
            z2 = dve.sig(dve.e.memset(u.ap[:, PAD + S:], 0.0))
            dve.wait(z1, z2)

            def gated(i, first, second):
                for slot, (acc, done), func, at in ((ga, first, ACT.Identity, 0), (gb, second, ACT.Sigmoid, 4)):
                    act.wait(done)
                    t = act.sig(act.e.activation(slot.claim(act), acc.ap, func, bias=self.v("b_in_2", i + at)))
                    acc.free(t)
                    dve.wait(t)
                t = dve.sig(dve.e.tensor_tensor(u.claim(dve)[:, PAD:PAD + S], ga.ap, gb.ap, ALU.mult))
                ga.free(t)
                gb.free(t)
                u_ready.set(t)

            def taps_on_pe(i, pe_taps):
                diag = diags.claim(act)
                for n in range(pe_taps):
                    built = act.sig(act.e.activation(diag[:, n, :], self.c("ident"), ACT.Copy,
                                                     scale=self.v("dw_w_2", i * TAPS + TAPS - pe_taps + n)))
                w = self.next_wide()
                out = w.claim(pe)
                u_ready.follow(pe)
                pe.wait(built)
                for half in range(2):
                    for n in range(pe_taps):
                        at = half * HALF + TAPS - pe_taps + n
                        ins = pe.e.matmul(out[:, half * HALF:(half + 1) * HALF], diag[:, n, :], u.ap[:, at:at + HALF],
                                          start=(n == 0), stop=(n == pe_taps - 1))
                done = pe.sig(ins)
                diags.free(done)
                u.free(done)
                return w, done

            def taps(i, pe_taps, on_pe):
                n = TAPS - pe_taps
                sums = [y[:, i, :], part]
                last = [None, None]
                for j in range(n):
                    w, src = self.v("dw_w_2", i * TAPS + j), u.ap[:, j:j + S]
                    a = j % 2
                    out = sums[a]
                    u_ready.follow(dve)
                    if last[a]:
                        dve.wait(last[a])
                    if j == 0:
                        t = dve.e.tensor_scalar(out, src, w, self.v("dw_b_2", i), ALU.mult, ALU.add)
                    elif j == 1:
                        t = dve.e.tensor_scalar(out, src, w, None, ALU.mult)
                    else:
                        t = dve.e.scalar_tensor_tensor(out, src, w, out, ALU.mult, ALU.add)
                    last[a] = dve.sig(t)
                    yield
                u.free(*last)
                dve.wait(*last)
                t = dve.sig(dve.e.tensor_tensor(sums[0], sums[0], part, ALU.add))
                dve.wait(t, on_pe[1])
                t = dve.sig(dve.e.tensor_tensor(sums[0], sums[0], on_pe[0].ap, ALU.add))
                on_pe[0].free(t)
                dve.wait(t)

            def some(steps, n):
                for _ in range(n):
                    next(steps, None)

            u_ready = Held(self, "u_ready")
            gated(0, *self.project_pair(self.h_ready))
            with self.w_turns("conv", CONV_TILES - 1, 2) as i:
                on_pe = []
                steps = taps(i, PE_TAPS, on_pe)
                first = self.project()
                some(steps, TAPS // 4)
                on_pe += taps_on_pe(i, PE_TAPS)
                second = self.project()
                some(steps, TAPS)
                gated(i + 1, first, second)
            on_pe = []
            steps = taps(CONV_TILES - 1, LAST_PE_TAPS, on_pe)
            for j in range(CONV_TILES):
                acc, done = self.project()
                some(steps, 9)
                act.wait(done)
                acc.free(act.sig(act.e.activation(y[:, j + 4, :], acc.ap, ACT.Silu, bias=self.v("b_in_2", j + 8))))
                if j == 0:
                    on_pe += taps_on_pe(CONV_TILES - 1, LAST_PE_TAPS)
        with ExitStack() as ctx:
            c_hi = ctx.enter_context(self.nc.sbuf_tensor("pw_hi", [P, 4, S], F32R))
            c_lo = ctx.enter_context(self.nc.sbuf_tensor("pw_lo", [P, 4, S], F32R))
            ready = []
            with ExitStack() as norm_ctx:
                n = self.norm(norm_ctx, "cln", "mean512", EPS, 4, centred=True)
                tiles = [y[:, k, :] for k in range(4)]
                for tile in tiles:
                    n.gather(tile, self.dve_now(), on_pe=True)

                def low(k, h):
                    dve.wait(h)
                    ready.append((h, dve.sig(dve.e.tensor_tensor(c_lo[:, k, :], tiles[k], c_hi[:, k, :].bitcast(F32),
                                                                 ALU.subtract))))

                before = None
                for k, tile, t in n.in_place(tiles, "cln_g_2", "cln_b_2", ACT.Silu):
                    act.wait(t)
                    h = act.sig(act.e.activation(c_hi[:, k, :], tile, ACT.Copy))
                    if before:
                        low(*before)
                    before = (k, h)
                low(*before)
            with self.scope("pw", meet=False) as sb:
                sq = [self.slot(f"pw_sq{i}", sb(f"sq{i}", [P, S])[:]) for i in range(2)]
                rstd = self.slot("pw_rstd", sb("rstd", [P, S])[:])
                before = None

                def normed(n, square, p, s):
                    w, m = self.column_mean(self.c("mean64"), square.ap, s)
                    square.free(m[-1])
                    r = self.rsqrt_of(w, m, rstd, EPS)
                    dve.wait(*r, p)
                    out = y[:, n, :]
                    g = dve.sig(dve.e.scalar_tensor_tensor(out, out, self.v("gn_conv_g_2", n), rstd.ap, ALU.mult, ALU.mult))
                    rstd.free(g)
                    dve.wait(g)
                    dve.sig(dve.e.tensor_tensor(out, out, y[:, n + 4, :], ALU.mult))

                for n in range(4):
                    if n % 2 == 0:
                        tile = self.next_tile()
                    acc = self.next_acc()
                    done = self.gemm(acc, tile, 4, 2 * P, (n % 2) * P,
                                     lambda k, part: (c_lo if part else c_hi)[:, k, :], ready)
                    if n % 2:
                        tile.free(done)
                    act.wait(done)
                    p = act.sig(act.e.activation(y[:, n, :], acc.ap, ACT.Identity, bias=self.v("pw_b_2", n)))
                    s = act.sig(act.e.activation(sq[n % 2].claim(act), acc.ap, ACT.Square, bias=self.v("pw_b_2", n)))
                    acc.free(s)
                    if before:
                        normed(*before)
                    before = (n, sq[n % 2], p, s)
                normed(*before)

    def neighbourhood(self, y):
        act, dve, pe, sp = self.act, self.dve, self.pe, self.sp
        with self.scope("na") as sb:
            seen = sb("seen", [P, GRID_W])
            conv_done = self.dve_now()
            sp.wait(conv_done)
            got_seen = self.fetch("seen", seen[:], self.t["seen"])
            self.copies_done("rel_copies")
            q2 = sb("q2", [P, ROWS, P])[:]
            k, t, gate = (sb(n, [P, S])[:] for n in ("k", "t", "gate"))
            vtok = sb("vtok", [P, 15, P])[:]
            bias = sb("bias", [P, REL_H, GRID_W])
            bias_slot = self.slot("na_bias", bias[:])
            self.line_for("na_bias")
            prob = [self.slot(f"na_prob{i}", sb(f"prob{i}", [P, HALF])[:]) for i in range(2)]
            prob_t = [self.slot(f"na_pt{i}", sb(f"pt{i}", [P, HALF])[:]) for i in range(2)]
            stat = [sb(f"stat{i}", [P, 4]) for i in range(2)]
            bq = sb("bq", [P, 4])
            at = VEC["b_in_2"] + 12
            dve.e.tensor_scalar(bq[:], self.vec[:, at:at + 4], SCALE, None, ALU.mult)
            z = dve.sig(dve.e.memset(q2, 0.0))
            act.wait(z)
            dve.wait(got_seen)
            score_bank = [self.bank[4], self.bank[5]]
            turn_bank, out_bank = self.bank[6], self.bank[7]
            with self.w_turns("na", NA_HEADS // 2, 4) as pair:
                bias_slot.claim(sp)
                for a in range(2):
                    one = self.t["rel_copies"][bass.ds(pair * 2 + a, 1), :]
                    src = bass.AP(tensor=one.tensor, offset=one.offset + GRID_W - 1,
                                  ap=[[REL_H * REL_PAD - 1, GRID_W], [REL_PAD, REL_H], [1, GRID_W]])
                    got_bias = self.fetch("na_bias", bias[64 * a:64 * a + 64, :, :], src)
                dve.wait(got_bias)
                b_in = lambda n: self.v("b_in_2", pair + n)
                before = [pe.turn_before(), dve.turn_before()]
                acc, done = self.project()
                act.wait(done, *before)
                for a in range(2):
                    c = slice(64 * a, 64 * a + 64)
                    tq = act.sig(act.e.activation(q2[c, :, c], acc.ap[c, :].rearrange("p (r w) -> p r w", w=GRID_W),
                                                  ACT.Identity, bias=bq[c, bass.ds(pair, 1)], scale=SCALE))
                acc.free(tq)
                acc, done = self.project()
                act.wait(done)
                tv = act.sig(act.e.activation(t, acc.ap, ACT.Identity, bias=b_in(20)))
                acc.free(tv)
                masked = dve.sig(dve.e.tensor_tensor(
                    bias[:], bias[:], seen[:].unsqueeze(1).broadcast_to([P, REL_H, GRID_W]), ALU.add))
                dve.wait(masked)

                def token_major(first, n):
                    w = self.next_acc()
                    tr = self.transposes(w, t, tv, n=n, step=64, first=first)
                    act.wait(tr)
                    v_tok = act.sig(act.e.activation(vtok[:, first:first + n, :].rearrange("p a b -> p (a b)"),
                                                     w.ap[:, 0:n * P], ACT.Copy))
                    w.free(v_tok)
                    return v_tok

                acc, done = self.project()
                act.wait(done)
                tk = act.sig(act.e.activation(k, acc.ap, ACT.Identity, bias=b_in(16)))
                acc.free(tk)
                token_major(0, 8)
                acc, done = self.project()
                act.wait(done)
                tg = act.sig(act.e.activation(gate, acc.ap, ACT.Silu, bias=b_in(24)))
                acc.free(tg)
                v_tok = token_major(8, 7)
                out_y = y[:, pair + 4, :]
                key_row = lambda r: min(max(r - KH // 2, 0), ROWS - KH)
                normed, turned = {}, {}
                for step in range(ROWS + 2):
                    r = step
                    if r < ROWS:
                        ks = key_row(r)
                        b = score_bank[r % 2]
                        out = b.claim(pe)
                        pe.wait(tq, tk)
                        s_done = pe.sig(pe.e.matmul(out, q2[:, r, :], k[:, ks * GRID_W:(ks + KH) * GRID_W],
                                                    start=True, stop=True))
                        pr, st = prob[r % 2], stat[r % 2]
                        dve.wait(s_done)
                        p = pr.claim(dve)
                        rel = ks - r + KH - 1
                        dve.e.memset(st[:, 2:3], 0.0)
                        mx = dve.sig(dve.e.tensor_tensor_reduce(
                            p, out, bias[:, rel:rel + KH, :].rearrange("p a b -> p (a b)"), 1.0, 3 * MASKED,
                            ALU.add, ALU.max, st[:, 0:1]))
                        b.free(mx)
                        if r == ROWS - 1:
                            bias_slot.free(mx)
                        dve.wait(mx)
                        nm = dve.sig(dve.e.tensor_scalar(st[:, 1:2], st[:, 0:1], -1.0, None, ALU.mult))
                        act.wait(nm)
                        ex = act.sig(act.e.activation(p, p, ACT.Exp, bias=st[:, 1:2], accum_out=st[:, 2:3]))
                        dve.wait(ex)
                        rc = dve.sig(dve.e.reciprocal(st[:, 3:4], st[:, 2:3]))
                        dve.wait(rc)
                        normed[r] = dve.sig(dve.e.tensor_scalar(p, p, st[:, 3:4], None, ALU.mult))
                    r = step - 1
                    if 0 <= r < ROWS:
                        out = turn_bank.claim(pe)
                        pe.wait(normed[r])
                        for b in range(4):
                            ins = pe.e.transpose(out[:, b * P:(b + 1) * P], prob[r % 2].ap[:, b * P:(b + 1) * P],
                                                 self.c("ident"))
                        tr = pe.sig(ins)
                        prob[r % 2].free(tr)
                        act.wait(tr)
                        turned[r] = act.sig(act.e.activation(prob_t[r % 2].claim(act), out, ACT.Copy))
                        turn_bank.free(turned[r])
                    r = step - 2
                    if 0 <= r < ROWS:
                        ks = key_row(r)
                        if r % 4 == 0:
                            o = out_bank.claim(pe)
                        pe.wait(turned[r], v_tok)
                        for b in range(4):
                            ins = pe.e.matmul(o[:, (r % 4) * P:(r % 4 + 1) * P], vtok[:, ks + 2 * b, :],
                                              prob_t[r % 2].ap[:, b * P:(b + 1) * P], start=(b == 0), stop=(b == 3))
                        pv = pe.sig(ins)
                        prob_t[r % 2].free(pv)
                        if r % 4 == 3:
                            act.wait(pv)
                            for a in range(2):
                                c = slice(64 * a, 64 * a + 64)
                                dst = t[c, (r - 3) * 64:(r + 1) * 64].rearrange("p (r w) -> p r w", w=64)
                                src = o[c, :].rearrange("p (r q) -> p r q", q=P)[:, :, c]
                                last = act.sig(act.e.activation(dst, src, ACT.Copy))
                            out_bank.free(last)
                act.wait(last)
                sq = act.sig(act.e.activation(k, t, ACT.Square))
                acc, m = self.column_mean(self.c("mean64"), k, sq, self.next_acc())
                r_ = self.rsqrt_of(acc, m, k, EPS)
                self.next_acc()
                dve.wait(*r_, last)
                n1 = dve.sig(dve.e.scalar_tensor_tensor(t, t, self.v("gn_att_g_2", pair), k, ALU.mult, ALU.mult))
                dve.wait(n1, tg)
                dve.sig(dve.e.tensor_tensor(out_y, t, gate, ALU.mult))

    def third(self):
        x = self.x_tiles()
        with ExitStack() as ctx:
            l1 = self.norm(ctx, "ln1", "mean1024", LN_EPS, KD, centred=True)
            for k, tile, t in self.block_input("final_g_2"):
                l1.gather(tile, t, on_pe=True)
            self.prepare_pair()
            self.h_ready = l1.split_and_keep(x, "ln_in_g_3", "ln_in_b_3", self.h)
        self.close_end_norm()
        y = self.ctx_y("y3")
        self.biases_alone(y)
        ready = self.attention_pairs(y)
        self.close_y()
        with ExitStack() as ctx:
            l2 = self.norm(ctx, "ln2", "mean1024", LN_EPS, KD, centred=True)
            bias = ctx.enter_context(self.nc.sbuf_tensor("ln2_bias", [P, KD], F32))
            at = VEC["ln1_b_3"]
            self.act.wait(*ready[-1])
            scaled = self.act.sig(self.act.e.activation(bias[:], self.vec[:, at:at + KD], ACT.Copy, scale=ALPHA))
            self.mix_out("mix3", ALPHA, ready, l2)
            self.prepare_pair()
            self.act.wait(scaled)
            self.h_ready = l2.split_and_keep(x, "ln1_g_3", "ln1_b_3", self.h, ALPHA, bias)
            self.dve.wait(self.kept)
        self.end_norm = self.norm_with_its_memory("ln3", "mean1024", LN_EPS, KD, centred=True)
        self.mlp("mlp3", False, self.end_norm)

    def act_now(self):
        return Token(self.act.line, self.act.line.count, None)

    def attention_pairs(self, y):
        act, dve, pe, sp = self.act, self.dve, self.pe, self.sp
        with ExitStack() as ctx:
            k2 = ctx.enter_context(self.nc.sbuf_tensor("swa_k2", [P, 2, S], F32))
            v2 = ctx.enter_context(self.nc.sbuf_tensor("swa_v2", [P, NCH, 2, 64], F32))
            with self.scope("kv") as sb:
                t = sb("t", [P, S])[:]
                (acc, done), second = self.project_pair(self.h_ready)
                act.wait(done)
                for g in range(2):
                    for a in range(2):
                        last = act.sig(act.e.activation(k2[64 * a:64 * a + 64, g, :], acc.ap[64 * g:64 * g + 64, :], ACT.Copy))
                acc.free(last)
                acc, done = second
                act.wait(done)
                tv = act.sig(act.e.activation(t, acc.ap, ACT.Copy))
                acc.free(tv)
                w = self.next_wide()
                tr = self.transposes(w, t, tv)
                self.next_wide()
                act.wait(tr)
                last = act.sig(act.e.activation(v2[:].rearrange("p n g d -> p (n g d)"), w.ap, ACT.Copy))
                w.free(last)
            self.stick_breaking(y)
            self.prepare_pair()
            total = ctx.enter_context(self.nc.sbuf_tensor("swa_total", [P, S], F32))[:]
            ready = self.sliding_window(y, k2, v2, total)
            n7 = Norm(self, None, "norm7", "mean512", EPS, 4, memory=[total, y[:, 0, :], y[:, 1, :], y[:, 2, :]])
            return ready + n7.split_to([y[:, k + 4, :] for k in range(4)], "swa_norm_g_3", lambda k: self.h(k + 4))

    def stick_breaking(self, y):
        act, dve, pe, sp = self.act, self.dve, self.pe, self.sp
        SOFT, SUM, OUT = 2, 3, 5
        with self.scope("sb") as sb:
            q, k, vtok = (sb(n, [P, S])[:] for n in ("q", "k", "vtok"))
            ring = lambda name, n: (lambda a: [self.slot(f"sb_{name}{i}", a[:, i, :]) for i in range(n)])(
                sb(name, [P, n, HALF]))
            mag_all = sb("mag", [P, 4, HALF])
            mag = [self.slot(f"sb_mag{i}", mag_all[:, i, :]) for i in range(4)]
            v_raw = mag_all[:, 0:2, :].rearrange("p a n -> p (a n)")
            soft, prob, carry = ring("soft", 3), ring("prob", 3), ring("carry", 2)
            tiles = []
            for qh in range(2):
                for kb in range(4 * qh + 3, -1, -1):
                    for hh in range(2):
                        q0 = max(kb * CH, qh * HALF)
                        tiles.append((hh, qh, kb, q0 - qh * HALF))
            act.e.preload_act_table_set("natural_log_exp_and_others")
            with self.w_turns("sb", 4, 4) as pair:
                before = [pe.turn_before()]
                acc, done = self.project()
                act.wait(done, *before)
                tq = act.sig(act.e.activation(q, acc.ap, ACT.Copy, scale=SCALE))
                acc.free(tq)
                acc, done = self.project()
                act.wait(done)
                tk = act.sig(act.e.activation(k, acc.ap, ACT.Copy))
                acc.free(tk)
                acc, done = self.project()
                act.wait(done)
                mag[0].claim(act)
                mag[1].claim(act)
                tv = act.sig(act.e.activation(v_raw, acc.ap, ACT.Copy))
                acc.free(tv)
                acc, done = self.project()
                act.wait(done)
                acc.free(act.sig(act.e.activation(y[:, pair + 4, :], acc.ap, ACT.Copy)))
                w = self.next_acc()
                tr = self.transposes(w, v_raw, tv)
                mag[0].free(tr)
                mag[1].free(tr)
                act.wait(tr)
                v_tok = act.sig(act.e.activation(vtok, w.ap, ACT.Copy))
                w.free(v_tok)
                oslot = self.next_acc()
                o = oslot.claim(pe)
                pe.wait(tq, tk, v_tok)
                banks = [self.bank[b] for b in (4, 5, 6, 7, 0, 1)]
                score, softened, logit, weight, carried = {}, {}, {}, {}, {}
                for step in range(len(tiles) + OUT):
                    i = step
                    if i < len(tiles):
                        hh, qh, kb, c0 = tiles[i]
                        hp = slice(64 * hh, 64 * hh + 64)
                        c = slice(c0, HALF)
                        z = banks[i % 6].claim(pe)
                        z_done = pe.sig(pe.e.matmul(z[:, c], k[hp, kb * CH:(kb + 1) * CH],
                                                    q[hp, qh * HALF + c0:(qh + 1) * HALF],
                                                    start=True, stop=False, skip_group_check=True))
                        dve.wait(z_done)
                        m = mag[i % 4].claim(dve)
                        low = dve.sig(dve.e.tensor_scalar(m[:, c], z[:, c], LN_TOP, None, ALU.min))
                        act.wait(low)
                        ex = act.sig(act.e.activation(m[:, c], m[:, c], ACT.Exp))
                        act.wait(ex)
                        score[i] = act.sig(act.e.activation(m[:, c], m[:, c], ACT.Ln, bias=1.0))
                    i = step - SOFT
                    if 0 <= i < len(tiles):
                        hh, qh, kb, c0 = tiles[i]
                        c, d = slice(c0, HALF), slice(c0, c0 + CH)
                        diag = kb >= 4 * qh
                        z, mg, sf = banks[i % 6].ap, mag[i % 4], soft[i % 3]
                        dve.wait(score[i])
                        s = sf.claim(dve)
                        t = dve.sig(dve.e.tensor_tensor(s[:, c], mg.ap[:, c], z[:, c], ALU.max))
                        mg.free(t)
                        if diag:
                            dve.wait(t)
                            t = dve.sig(dve.e.tensor_tensor(s[:, d], s[:, d], self.c("after"), ALU.mult))
                        softened[i] = t
                    i = step - SUM
                    if 0 <= i < len(tiles):
                        hh, qh, kb, c0 = tiles[i]
                        c, d = slice(c0, HALF), slice(c0, c0 + CH)
                        diag = kb >= 4 * qh
                        z, sf, cr = banks[i % 6].ap, soft[i % 3], carry[hh]
                        s = sf.ap
                        later = slice(c0 + CH if diag else 0, HALF)
                        first = kb == 4 * qh + 3
                        pe.wait(softened[i])
                        ins = pe.e.matmul(z[:, c], self.c("neg_tri"), s[:, c], start=False, stop=False,
                                          skip_group_check=True)
                        if diag:
                            ins = pe.e.matmul(z[:, d], self.c("ident"), self.c("bar_after"), start=False,
                                              stop=first, skip_group_check=True)
                        if not first:
                            pe.wait(*carried[hh])
                            ins = pe.e.matmul(z[:, later], self.c("neg_ones"), cr.ap[:, later], start=False,
                                              stop=True, skip_group_check=True)
                        logit[i] = pe.sig(ins)
                        cr.free(logit[i])
                        if kb > 0:
                            cr.claim(dve)
                            dve.wait(softened[i])
                            new = []
                            if diag:
                                new.append(dve.sig(dve.e.tensor_copy(cr.ap[:, d], s[:, d])))
                            if not first:
                                dve.wait(*carried[hh])
                                new.append(dve.sig(dve.e.tensor_tensor(cr.ap[:, later], cr.ap[:, later],
                                                                       s[:, later], ALU.add)))
                            carried[hh] = new
                            sf.free(logit[i], new[-1])
                        else:
                            sf.free(logit[i])
                        act.wait(logit[i])
                        weight[i] = act.sig(act.e.activation(prob[i % 3].claim(act)[:, c], z[:, c], ACT.Exp))
                        banks[i % 6].free(weight[i])
                    i = step - OUT
                    if 0 <= i < len(tiles):
                        hh, qh, kb, c0 = tiles[i]
                        hp = slice(64 * hh, 64 * hh + 64)
                        pe.wait(weight[i])
                        ins = pe.e.matmul(o[hp, qh * HALF + c0:(qh + 1) * HALF],
                                          vtok[:, kb * CH + 64 * hh:kb * CH + 64 * hh + 64], prob[i % 3].ap[:, c0:HALF],
                                          start=(kb == 4 * qh + 3), stop=(kb == 0), skip_group_check=True)
                        o_done = pe.sig(ins)
                        prob[i % 3].free(o_done)
                w.free(weight[len(tiles) - 1])
                act.wait(o_done)
                oslot.free(act.sig(act.e.activation(y[:, pair, :], o, ACT.Copy)))

    def sliding_window(self, y, k2, v2, total):
        act, dve, pe, sp = self.act, self.dve, self.pe, self.sp
        NORM, TURN, OUT = 1, 2, 3
        with self.scope("swa") as sb:
            sinks = sb("sinks", [P, SWA_HEADS])
            dve.wait(self.fetch("sinks", sinks[:], self.t["sinks"].broadcast_to([P, SWA_HEADS])))
            self.copies_done("band_copies")
            q2 = sb("q2", [P, 2, S])[:]
            kg = sb("kg", [P, S])[:]
            vg = sb("vg", [P, NCH, P])[:]
            sink = sb("sink", [P, 2])
            bias = sb("bias", [P, 2, BAND])
            bias_slot = self.slot("swa_bias", bias[:])
            self.line_for("swa_bias")
            prob = [self.slot(f"swa_p{i}", sb(f"p{i}", [P, 2, BAND])[:]) for i in range(3)]
            prob_t = [self.slot(f"swa_pt{i}", sb(f"pt{i}", [P, 2, 2, CH])[:]) for i in range(2)]
            stat = [sb(f"stat{i}", [P, 6, 2]) for i in range(3)]
            score_banks, turn_banks, out_banks = ([self.bank[b] for b in x] for x in ((4, 5), (6, 0), (7, 1)))
            sb_norm = Norm(self, None, "norm6", "mean512", EPS, 4,
                           memory=[None, sb("rstd", [P, S])[:], q2[:, 0, :], q2[:, 1, :]])
            for k in range(4):
                sb_norm.gather(y[:, k, :], self.act_now(), on_pe=True)
            sb_norm.start(())
            dve.wait(*sb_norm.rstd_ready)
            sb_norm.rstd_ready = None
            z = dve.sig(dve.e.memset(q2, 0.0))
            dve.wait(z)
            dve.wait(dve.sig(dve.e.memset(total, 0.0)))
            kg_slot = self.slot("swa_kg", kg)
            with self.repeat("swa", SWA_HEADS // 2) as pair:
                bias_slot.claim(sp)
                one = self.t["band_copies"][bass.ds(pair * 2, 1), :]
                src = bass.AP(tensor=one.tensor, offset=one.offset + CH - 1,
                              ap=[[REL_BAND - 1, CH], [CH * REL_BAND, 2], [1, BAND]])
                got_bias = self.fetch("swa_bias", bias[:], src)
                dve.wait(pe.turn_before(), act.turn_before())
                act.wait(pe.turn_before())
                for a in range(2):
                    c = slice(64 * a, 64 * a + 64)
                    dve.e.tensor_scalar(q2[c, a, :], y[c, pair + 4, :], SCALE, None, ALU.mult)
                dve.e.tensor_copy(sink[:], sinks[:, bass.ds(pair * 2, 2)])
                act_staged = act.sig(act.e.activation(kg_slot.claim(act), k2[:, pair // 2, :], ACT.Copy))
                for a in range(2):
                    staged = dve.sig(dve.e.tensor_copy(vg[:, :, 64 * a:64 * a + 64], v2[:, :, pair // 2, :]))
                dve.wait(staged)
                act.wait(staged)
                exped, normed, turned = {}, {}, {}
                for step in range(NCH + OUT):
                    n = step
                    if n < NCH:
                        lo = 0 if n else CH
                        sbk = score_banks[n % 2]
                        out = sbk.claim(pe).rearrange("p (a c) -> p a c", a=2)
                        pe.wait(staged, act_staged)
                        for a in range(2):
                            ins = pe.e.matmul(out[:, a, lo:], q2[:, a, n * CH:(n + 1) * CH],
                                              kg[:, (n - 1) * CH + lo:(n + 1) * CH], start=True, stop=True)
                        s_done = pe.sig(ins)
                        pr, st = prob[n % 3], stat[n % 3]
                        dve.wait(s_done, got_bias)
                        p = pr.claim(dve)
                        dve.e.memset(st[:, 3, :], 0.0)
                        for a in range(2):
                            m = dve.sig(dve.e.tensor_tensor_reduce(
                                p[:, a, lo:], out[:, a, lo:], bias[:, a, lo:], 1.0, sink[:, a:a + 1],
                                ALU.add, ALU.max, st[:, 0, a:a + 1]))
                        sbk.free(m)
                        if n == NCH - 1:
                            bias_slot.free(m)
                        dve.wait(m)
                        dve.sig(dve.e.tensor_scalar(st[:, 1, :], st[:, 0, :], -1.0, None, ALU.mult))
                        d = dve.sig(dve.e.tensor_tensor(st[:, 2, :], sink[:], st[:, 0, :], ALU.subtract))
                        act.wait(d)
                        for a in range(2):
                            act.sig(act.e.activation(p[:, a, lo:], p[:, a, lo:], ACT.Exp, bias=st[:, 1, a:a + 1],
                                                     accum_out=st[:, 3, a:a + 1]))
                        exped[n] = act.sig(act.e.activation(st[:, 4, :], st[:, 2, :], ACT.Exp))
                    n = step - NORM
                    if 0 <= n < NCH:
                        p, st, lo = prob[n % 3].ap, stat[n % 3], 0 if n else CH
                        dve.wait(exped[n])
                        dn = dve.sig(dve.e.tensor_tensor(st[:, 5, :], st[:, 3, :], st[:, 4, :], ALU.add))
                        dve.wait(dn)
                        dn = dve.sig(dve.e.reciprocal(st[:, 5, :], st[:, 5, :]))
                        dve.wait(dn)
                        for a in range(2):
                            normed[n] = dve.sig(dve.e.tensor_scalar(p[:, a, lo:], p[:, a, lo:], st[:, 5, a:a + 1], None,
                                                                    ALU.mult))
                    n = step - TURN
                    if 0 <= n < NCH:
                        tb = turn_banks[n % 2]
                        out = tb.claim(pe).rearrange("p (k a q) -> p k a q", k=2, a=2)
                        pe.wait(normed[n])
                        ks = range(2) if n else range(1, 2)
                        for kb in ks:
                            for a in range(2):
                                ins = pe.e.transpose(out[:, kb, a, :], prob[n % 3].ap[:, a, kb * CH:(kb + 1) * CH],
                                                     self.c("ident"))
                        tr = pe.sig(ins)
                        prob[n % 3].free(tr)
                        act.wait(tr)
                        dst = prob_t[n % 2].claim(act)
                        turned[n] = act.sig(act.e.activation(dst[:, ks[0]:, :, :], out[:, ks[0]:, :, :], ACT.Copy))
                        tb.free(turned[n])
                    n = step - OUT
                    if 0 <= n < NCH:
                        ob = out_banks[n % 2]
                        out = ob.claim(pe)
                        pe.wait(turned[n])
                        ks = range(2) if n else range(1, 2)
                        for kb in ks:
                            ins = pe.e.matmul(out[:, 0:2 * CH], vg[:, n - 1 + kb, :],
                                              prob_t[n % 2].ap[:, kb, :, :].rearrange("p a q -> p (a q)"),
                                              start=(kb == ks[0]), stop=(kb == 1))
                        pv = pe.sig(ins)
                        prob_t[n % 2].free(pv)
                        act.wait(pv)
                        for a in range(2):
                            c = slice(64 * a, 64 * a + 64)
                            last = act.sig(act.e.activation(y[c, pair + 4, n * CH:(n + 1) * CH],
                                                            out[c, a * CH:(a + 1) * CH], ACT.Copy))
                        ob.free(last)
                    if step == NCH // 2:
                        placed = sb_norm.split_one(y[:, pair, :], "sb_norm_g_3", pair, self.h_hi[:, pair, :],
                                                   self.h_lo[:, pair, :])
                dve.wait(last)
                dve.wait(dve.sig(dve.e.tensor_tensor(kg, y[:, pair + 4, :], y[:, pair + 4, :], ALU.mult)))
                kg_slot.free(dve.sig(dve.e.tensor_tensor(total, total, kg, ALU.add)))
            self.dve.wait(*placed)
        return [placed] * 4

    def finish(self, gain, bias):
        sp = self.sp
        for k, tile, t in self.block_input(gain, bias):
            sp.wait(t)
            out = self.fetch("out", self.t["out"][k * P:(k + 1) * P, :], tile)
        sp.wait(out)
        for loaded in self.w_loaded:
            loaded.follow(sp)
        self.close_end_norm()


BLOCKS = (1, 2, 3)


def program(nc, tensors, blocks, counts, last_turn):
    with ExitStack() as ctx:
        b = Blocks(nc, ctx, counts, last_turn)
        b.setup(tensors, blocks)
        for n in blocks:
            (b.first, b.second, b.third)[n - 1]()
        b.finish(*{1: ("final_norm_g", None), 2: ("final_g_2", None), 3: ("ln2_g_3", "ln2_b_3")}[blocks[-1]])
        return b


def k_tiles(w):
    k, n = w.shape
    return w.reshape(k // P, P, n // P, P).transpose(2, 1, 0, 3).reshape(n // P, P, KD * P)


def down_tiles(w):
    return w.reshape(NGROUP, 2, P, 2, 4 * P).transpose(0, 3, 2, 1, 4).reshape(2 * NGROUP, P, KD * P)


def mlp_order(up, down):
    a, b = up[:DFF // P], up[DFF // P:]
    out = [a[0], b[0], a[1], b[1]]
    for g in range(1, NGROUP):
        out += [a[2 * g], down[2 * g - 2], down[2 * g - 1], b[2 * g], a[2 * g + 1], b[2 * g + 1]]
    return out + [down[-2], down[-1]]


def weight_stream(i, blocks):
    tiles = []
    if 1 in blocks:
        w = k_tiles(i["w_in"][0])
        for h in range(4):
            tiles += [w[h], w[4 + h], w[8 + h], w[12 + h]]
        for g in range(4):
            tiles += [w[16 + g], w[20 + g]]
        tiles += list(k_tiles(i["w_out"][0]))
        tiles += mlp_order(k_tiles(i["w_up"][0]), down_tiles(i["w_down"][0]))
    if 2 in blocks:
        w = k_tiles(i["w_in_2"][0])
        for c in range(4):
            tiles += [w[c], w[4 + c]]
        tiles += list(w[8:12])
        tiles += list(i["pw_w_2"][0].reshape(4, P, 2, 2 * P).transpose(2, 1, 0, 3).reshape(2, P, KD * P))
        for p in range(4):
            tiles += [w[12 + p], w[20 + p], w[16 + p], w[24 + p]]
        tiles += list(k_tiles(i["w_out_2"][0]))
    if 3 in blocks:
        w = k_tiles(i["w_in_3"][0])
        tiles += [w[16], w[17]]
        for p in range(4):
            tiles += [w[p], w[4 + p], w[8 + p], w[12 + p]]
        tiles += list(k_tiles(i["w_out_3"][0]))
        tiles += mlp_order(k_tiles(i["w_gate_up_3"][0]), down_tiles(i["w_down_3"][0]))
    tiles += [np.zeros((P, KD * P), np.float32)] * 2
    return np.stack(tiles)


def columns(a):
    return np.asarray(a).reshape(-1, P).T


def kernel(**inputs):
    import concourse.bacc as bacc
    from concourse.bass_utils import run_bass_kernel_spmd as run

    i = {k: np.asarray(v) for k, v in inputs.items()}
    vec = {"conv_w0": columns(i["conv_w"][0, 0]), "conv_w1": columns(i["conv_w"][0, 1]),
           "conv_w2": columns(i["conv_w"][0, 2]),
           "dw_w_2": i["dw_w_2"][0].reshape(TAPS, 4, P).transpose(2, 1, 0).reshape(P, 4 * TAPS)}
    arrays = {
        "x_t": i["x"][0].T,
        "vectors": np.concatenate([vec[n] if n in vec else columns(i[n]) for n in VEC], axis=1),
        "common": COMMON,
        "rotary": TABLES["rotary"],
        "retention": TABLES["retention"],
        "seen": TABLES["seen"],
        "onehot": TABLES["onehot"],
        "outside": TABLES["outside"],
        "sgu_w_t": i["sgu_w_s"][0].transpose(0, 2, 1),
        "sgu_b_s": i["sgu_b_s"][0],
        "rpb": i["rpb_2"][0].reshape(NA_HEADS * REL_H, REL_W),
        "sinks": i["sinks_3"],
        "rel_bias": i["rel_bias_3"],
        "weights": weight_stream(i, BLOCKS),
    }
    arrays = {f"in_{k}": np.ascontiguousarray(v) for k, v in arrays.items()}

    def build(counts, last_turn):
        nc = bacc.Bacc("TRN2", target_bir_lowering=False, num_devices=1)
        t = {k[3:]: nc.dram_tensor(k, v.shape, F32, kind="ExternalInput").ap() for k, v in arrays.items()}
        t["out"] = nc.dram_tensor("out_t", (D, S), F32, kind="ExternalOutput").ap()
        for name, shape in (("rel_rows", (NA_HEADS * REL_H, REL_PAD)), ("band_rows", (SWA_HEADS, REL_BAND)),
                            ("rel_copies", (NA_HEADS, GRID_W * REL_H * REL_PAD)),
                            ("band_copies", (SWA_HEADS, CH * REL_BAND))):
            t[name] = nc.dram_tensor(name, shape, F32, kind="Internal").ap()
        return nc, program(nc, t, BLOCKS, counts, last_turn)

    _, dry = build({}, {})
    nc, _ = build(dry.found_counts, dry.found_last)
    r = run(nc, [arrays], core_ids=[0])
    return np.ascontiguousarray(r.results[0]["out_t"].T)[None]
```
